# Optimizing a Trainium2 kernel written in Bass

```python
import math
import jax, jax.numpy as jnp
from jax import lax
import numpy as np

D_MODEL = 1024
BATCH = 1
SEQ = 256
DEPTH = 2

CHUNK = 64
Q_BLOCK = 128
A_HEADS = 8
A_HEAD_DIM = 64
A_WIDTH = A_HEADS * A_HEAD_DIM
IDX_HEADS = 8
IDX_DIM = 64
TOPK_MAX = 256
B_WIDTH = 512
B_GROUPS = 8
SHORT_CONV = 3
C_WIDTH = 512
POOL_WINDOWS = (2, 4, 8, 16)
C_GROUPS = len(POOL_WINDOWS)
C_GROUP_DIM = C_WIDTH // C_GROUPS
D_HEADS = 8
D_NOPE = 64
D_ROPE = 32
D_V = 64
Q_LORA = 384
KV_LORA = 256
ROPE_BASE = 10000.0
D_FF = 2816
FFN_CONV = 3
LN_EPS = 1e-5
RMS_EPS = 1e-6
DN_ALPHA = (2 * DEPTH) ** 0.25
DN_BETA = (8 * DEPTH) ** -0.25
NEG = -1e30

EVEN_SIZES = (A_WIDTH, A_WIDTH, A_WIDTH, IDX_HEADS * IDX_DIM, IDX_DIM, IDX_HEADS,
              B_WIDTH, B_WIDTH, B_WIDTH)
EVEN_IN = sum(EVEN_SIZES)
EVEN_OUT = A_WIDTH + B_WIDTH
ODD_SIZES = (C_WIDTH, Q_LORA, KV_LORA, D_ROPE)
ODD_IN = sum(ODD_SIZES)
ODD_OUT = C_WIDTH + D_HEADS * D_V
N_EVEN = (DEPTH + 1) // 2
N_ODD = DEPTH // 2


def _split(z, sizes):
    offs = []
    acc = 0
    for s in sizes[:-1]:
        acc += s
        offs.append(acc)
    return jnp.split(z, offs, axis=-1)

def layer_norm(x, g, b):
    x32 = x.astype(jnp.float32)
    mu = jnp.mean(x32, axis=-1, keepdims=True)
    var = jnp.mean(jnp.square(x32 - mu), axis=-1, keepdims=True)
    y = (x32 - mu) * lax.rsqrt(var + LN_EPS)
    return (y * g.astype(jnp.float32) + b.astype(jnp.float32)).astype(x.dtype)

def rms_norm(x, g):
    x32 = x.astype(jnp.float32)
    y = x32 * lax.rsqrt(jnp.mean(jnp.square(x32), axis=-1, keepdims=True) + RMS_EPS)
    return (y * g.astype(jnp.float32)).astype(x.dtype)

def causal_dwconv(x, w):
    k_w = w.shape[0]
    seq = x.shape[1]
    xp = jnp.pad(x, ((0, 0), (k_w - 1, 0), (0, 0)))
    y = xp[:, 0:seq] * w[0]
    for k in range(1, k_w):
        y = y + xp[:, k:k + seq] * w[k]
    return y

def chunk_limit(pos):
    return (pos // CHUNK + 1) * CHUNK

def alibi_slopes(n):
    return jnp.asarray([2.0 ** (-8.0 * (i + 1) / n) for i in range(n)], dtype=jnp.float32)

def rope_tables(seq, dim):
    inv = ROPE_BASE ** (-jnp.arange(0, dim, 2, dtype=jnp.float32) / dim)
    ang = jnp.arange(seq, dtype=jnp.float32)[:, None] * inv[None, :]
    return jnp.cos(ang), jnp.sin(ang)

def apply_rope(x, cos, sin):
    half = x.shape[-1] // 2
    x1, x2 = x[..., :half], x[..., half:]
    c = cos[None, :, None, :].astype(x.dtype)
    s = sin[None, :, None, :].astype(x.dtype)
    return jnp.concatenate([x1 * c - x2 * s, x2 * c + x1 * s], axis=-1)

def dsa_attention(q, k, v, q_idx, k_idx, w_idx):
    bsz, seq = q.shape[0], q.shape[1]
    topk = min(TOPK_MAX, seq // 4)
    nblk = seq // Q_BLOCK
    key_pos = jnp.arange(seq)
    slopes = alibi_slopes(A_HEADS)
    w_scaled = w_idx * (IDX_HEADS ** -0.5 * IDX_DIM ** -0.5)
    scale = A_HEAD_DIM ** -0.5

    def block(i):
        start = i * Q_BLOCK
        qb = lax.dynamic_slice_in_dim(q, start, Q_BLOCK, axis=1)
        qib = lax.dynamic_slice_in_dim(q_idx, start, Q_BLOCK, axis=1)
        wb = lax.dynamic_slice_in_dim(w_scaled, start, Q_BLOCK, axis=1)
        qpos = start + jnp.arange(Q_BLOCK)
        limit = chunk_limit(qpos)
        rel = jax.nn.relu(jnp.einsum('bthd,bsd->bths', qib, k_idx))
        score = jnp.einsum('bths,bth->bts', rel, wb)
        admissible = key_pos[None, :] < limit[:, None]
        score = jnp.where(admissible[None], score, NEG)
        _, idx = lax.top_k(score, topk)
        valid = idx < limit[None, :, None]
        k_sel = jax.vmap(lambda kk, ii: kk[ii])(k, idx)
        v_sel = jax.vmap(lambda vv, ii: vv[ii])(v, idx)
        logits = jnp.einsum('bthd,btjhd->bthj', qb, k_sel).astype(jnp.float32) * scale
        dist = jnp.abs(qpos[None, :, None] - idx).astype(jnp.float32)
        logits = logits - slopes[None, None, :, None] * dist[:, :, None, :]
        logits = jnp.where(valid[:, :, None, :], logits, NEG)
        p = jax.nn.softmax(logits, axis=-1).astype(v.dtype)
        return jnp.einsum('bthj,btjhd->bthd', p, v_sel)

    out = lax.map(block, jnp.arange(nblk))
    return jnp.moveaxis(out, 0, 1).reshape(bsz, seq, A_WIDTH)

def multiscale_pool(u, pool_w, pool_scale):
    bsz, seq = u.shape[0], u.shape[1]
    ug = u.reshape(bsz, seq, C_GROUPS, C_GROUP_DIM)
    cs = jnp.cumsum(ug.astype(jnp.float32), axis=1)
    cs = jnp.pad(cs, ((0, 0), (1, 0), (0, 0), (0, 0)))
    pos = jnp.arange(seq)
    means = []
    for g, win in enumerate(POOL_WINDOWS):
        hi = cs[:, 1:, g]
        lo = cs[:, jnp.maximum(pos + 1 - win, 0), g]
        cnt = jnp.minimum(pos + 1, win).astype(jnp.float32)
        means.append((hi - lo) / cnt[None, :, None])
    pooled = jnp.stack(means, axis=2).astype(u.dtype) - ug
    mixed = jnp.einsum('bsgc,gcd->bsgd', pooled, pool_w)
    return mixed.reshape(bsz, seq, C_WIDTH) * pool_scale

def mla_attention(q_lat, kv_lat, k_rope_in, q_norm_g, w_uq, kv_norm_g, w_ukv):
    bsz, seq = q_lat.shape[0], q_lat.shape[1]
    q = (rms_norm(q_lat, q_norm_g) @ w_uq).reshape(bsz, seq, D_HEADS, D_NOPE + D_ROPE)
    q_nope, q_rope = q[..., :D_NOPE], q[..., D_NOPE:]
    kv = (rms_norm(kv_lat, kv_norm_g) @ w_ukv).reshape(bsz, seq, D_HEADS, D_NOPE + D_V)
    k_nope, v = kv[..., :D_NOPE], kv[..., D_NOPE:]
    cos, sin = rope_tables(seq, D_ROPE)
    q_rope = apply_rope(q_rope, cos, sin)
    k_rope = apply_rope(k_rope_in[:, :, None, :], cos, sin)
    qh = jnp.concatenate([q_nope, q_rope], axis=-1)
    kh = jnp.concatenate([k_nope, jnp.broadcast_to(k_rope, (bsz, seq, D_HEADS, D_ROPE))], axis=-1)
    scale = (D_NOPE + D_ROPE) ** -0.5
    key_pos = jnp.arange(seq)
    nblk = seq // Q_BLOCK

    def block(i):
        start = i * Q_BLOCK
        qb = lax.dynamic_slice_in_dim(qh, start, Q_BLOCK, axis=1)
        limit = chunk_limit(start + jnp.arange(Q_BLOCK))
        logits = jnp.einsum('bthd,bshd->bhts', qb, kh).astype(jnp.float32) * scale
        mask = key_pos[None, :] < limit[:, None]
        logits = jnp.where(mask[None, None], logits, NEG)
        p = jax.nn.softmax(logits, axis=-1).astype(v.dtype)
        return jnp.einsum('bhts,bshd->bthd', p, v)

    out = lax.map(block, jnp.arange(nblk))
    return jnp.moveaxis(out, 0, 1).reshape(bsz, seq, D_HEADS * D_V)

def even_mixer(h, w_in, conv_w, w_out):
    bsz, seq = h.shape[0], h.shape[1]
    z = h @ w_in
    q, k, v, qi, ki, wi, bg, cg, xb = _split(z, EVEN_SIZES)
    ya = dsa_attention(q.reshape(bsz, seq, A_HEADS, A_HEAD_DIM),
                       k.reshape(bsz, seq, A_HEADS, A_HEAD_DIM),
                       v.reshape(bsz, seq, A_HEADS, A_HEAD_DIM),
                       qi.reshape(bsz, seq, IDX_HEADS, IDX_DIM), ki, wi)
    yb = bg * causal_dwconv(cg * xb, conv_w)
    return jnp.concatenate([ya, yb], axis=-1) @ w_out

def odd_mixer(h, w_in, pool_w, pool_scale, q_norm_g, w_uq, kv_norm_g, w_ukv, w_out):
    z = h @ w_in
    u, q_lat, kv_lat, k_rope = _split(z, ODD_SIZES)
    yc = multiscale_pool(u, pool_w, pool_scale)
    yd = mla_attention(q_lat, kv_lat, k_rope, q_norm_g, w_uq, kv_norm_g, w_ukv)
    return jnp.concatenate([yc, yd], axis=-1) @ w_out

def conv_ffn(h, w_up, conv_w, w_down):
    u = causal_dwconv(h @ w_up, conv_w)
    val, gate = u[..., :D_FF], u[..., D_FF:]
    return (jax.nn.silu(gate) * val) @ w_down

def first_inputs(seed: int = 0) -> dict:
    key = jax.random.key(seed)
    ks = iter(jax.random.split(key, 40))
    f32 = jnp.float32

    def nrm(shape, scale):
        return jax.random.normal(next(ks), shape, f32) * scale

    d = D_MODEL
    x = nrm((BATCH, SEQ, d), 1.0)
    c = nrm((BATCH, d), 1.0)
    ada_w = nrm((DEPTH, d, 6 * d), 0.1 * d ** -0.5)
    ada_b = nrm((DEPTH, 6 * d), 0.01)
    ln_mix_g = 1.0 + nrm((DEPTH, d), 0.01)
    ln_mix_b = nrm((DEPTH, d), 0.01)
    ln_ffn_g = 1.0 + nrm((DEPTH, d), 0.01)
    ln_ffn_b = nrm((DEPTH, d), 0.01)

    even_col_scale = jnp.concatenate([
        jnp.ones((2 * A_WIDTH,), f32), jnp.full((A_WIDTH,), DN_BETA, f32),
        jnp.ones((EVEN_IN - 3 * A_WIDTH,), f32)])
    ev_w_in = nrm((N_EVEN, d, EVEN_IN), d ** -0.5) * even_col_scale
    ev_conv_w = nrm((N_EVEN, SHORT_CONV, B_WIDTH), SHORT_CONV ** -0.5)
    ev_w_out = nrm((N_EVEN, EVEN_OUT, d), DN_BETA * EVEN_OUT ** -0.5)

    od_w_in = nrm((N_ODD, d, ODD_IN), d ** -0.5)
    pool_w = nrm((N_ODD, C_GROUPS, C_GROUP_DIM, C_GROUP_DIM), C_GROUP_DIM ** -0.5)
    pool_scale = 1.0 + nrm((N_ODD, C_WIDTH), 0.1)
    q_norm_g = 1.0 + nrm((N_ODD, Q_LORA), 0.01)
    w_uq = nrm((N_ODD, Q_LORA, D_HEADS * (D_NOPE + D_ROPE)), Q_LORA ** -0.5)
    kv_norm_g = 1.0 + nrm((N_ODD, KV_LORA), 0.01)
    ukv_col_scale = jnp.tile(jnp.concatenate([jnp.ones((D_NOPE,), f32),
                                              jnp.full((D_V,), DN_BETA, f32)]), D_HEADS)
    w_ukv = nrm((N_ODD, KV_LORA, D_HEADS * (D_NOPE + D_V)), KV_LORA ** -0.5) * ukv_col_scale
    od_w_out = nrm((N_ODD, ODD_OUT, d), DN_BETA * ODD_OUT ** -0.5)

    ffn_w_up = nrm((DEPTH, d, 2 * D_FF), d ** -0.5)
    ffn_conv_w = nrm((DEPTH, FFN_CONV, 2 * D_FF), FFN_CONV ** -0.5)
    ffn_w_down = nrm((DEPTH, D_FF, d), DN_BETA * D_FF ** -0.5)

    return {"x": x, "c": c, "ada_w": ada_w, "ada_b": ada_b,
            "ln_mix_g": ln_mix_g, "ln_mix_b": ln_mix_b, "ln_ffn_g": ln_ffn_g, "ln_ffn_b": ln_ffn_b,
            "ev_w_in": ev_w_in, "ev_conv_w": ev_conv_w, "ev_w_out": ev_w_out,
            "od_w_in": od_w_in, "pool_w": pool_w, "pool_scale": pool_scale,
            "q_norm_g": q_norm_g, "w_uq": w_uq, "kv_norm_g": kv_norm_g, "w_ukv": w_ukv,
            "od_w_out": od_w_out,
            "ffn_w_up": ffn_w_up, "ffn_conv_w": ffn_conv_w, "ffn_w_down": ffn_w_down}

def first_block(x, c, ada_w, ada_b, ln_mix_g, ln_mix_b, ln_ffn_g, ln_ffn_b,
              ev_w_in, ev_conv_w, ev_w_out,
              od_w_in, pool_w, pool_scale, q_norm_g, w_uq, kv_norm_g, w_ukv, od_w_out,
              ffn_w_up, ffn_conv_w, ffn_w_down):
    cond = jax.nn.silu(c)
    for l in range(DEPTH):
        mod = (cond @ ada_w[l] + ada_b[l])[:, None, :]
        sh_m, sc_m, g_m, sh_f, sc_f, g_f = jnp.split(mod, 6, axis=-1)
        h = x * (1.0 + sc_m) + sh_m
        if l % 2 == 0:
            e = l // 2
            y = even_mixer(h, ev_w_in[e], ev_conv_w[e], ev_w_out[e])
        else:
            o = l // 2
            y = odd_mixer(h, od_w_in[o], pool_w[o], pool_scale[o], q_norm_g[o], w_uq[o],
                          kv_norm_g[o], w_ukv[o], od_w_out[o])
        x = layer_norm(DN_ALPHA * x + (1.0 + g_m) * y, ln_mix_g[l], ln_mix_b[l])
        h = x * (1.0 + sc_f) + sh_f
        y = conv_ffn(h, ffn_w_up[l], ffn_conv_w[l], ffn_w_down[l])
        x = layer_norm(DN_ALPHA * x + (1.0 + g_f) * y, ln_ffn_g[l], ln_ffn_b[l])
    return x


DEPTH_2 = 1

HEAD_DIM = 64
N_HEADS_SB = 8
N_HEADS_FOX = 8
N_HEADS_MOBA = 8
BRANCH_WIDTH = 8 * HEAD_DIM
N_BRANCH = 3
D_FF_2 = 4 * D_MODEL
MOBA_BLOCK = 256
MOBA_TOPK = 3
MOBA_Q_CHUNK = 32
NEG_INF = -1e30
FORGET_BIAS_INIT = 2.0
IN_COLS = 9 * BRANCH_WIDTH + N_HEADS_FOX + N_BRANCH * D_MODEL


def rmsnorm(x, g):
    xf = x.astype(jnp.float32)
    y = xf * lax.rsqrt(jnp.mean(xf * xf, axis=-1, keepdims=True) + RMS_EPS)
    return (y * g.astype(jnp.float32)).astype(x.dtype)

def split_in_proj(proj):
    sizes = [BRANCH_WIDTH] * 6 + [N_HEADS_FOX] + [BRANCH_WIDTH] * 3 + [N_BRANCH * D_MODEL]
    points = [int(p) for p in np.cumsum(sizes)[:-1]]
    return jnp.split(proj, points, axis=-1)

def to_heads(t, n_heads):
    B, S, _ = t.shape
    return t.reshape(B, S, n_heads, HEAD_DIM).transpose(0, 2, 1, 3)

def merge_heads(t):
    B, H, S, d = t.shape
    return t.transpose(0, 2, 1, 3).reshape(B, S, H * d)

def alibi_slopes_2(n):
    return 2.0 ** (-8.0 * jnp.arange(1, n + 1, dtype=jnp.float32) / n)

def stick_breaking_attention(q, k, v):
    B, H, S, d = q.shape
    scale = 1.0 / math.sqrt(d)
    kf = k.astype(jnp.float32)
    vf = v.astype(jnp.float32)
    key_pos = jnp.arange(S)

    def block(i):
        t0 = i * Q_BLOCK
        qb = lax.dynamic_slice_in_dim(q, t0, Q_BLOCK, axis=2).astype(jnp.float32)
        z = jnp.einsum('bhqd,bhkd->bhqk', qb, kf) * scale
        q_pos = t0 + jnp.arange(Q_BLOCK)
        past = key_pos[None, :] < q_pos[:, None]
        log_1m = jnp.where(past, -jax.nn.softplus(z), 0.0)
        tail = lax.cumsum(log_1m, axis=3, reverse=True) - log_1m
        w = jnp.where(past, jnp.exp(jax.nn.log_sigmoid(z) + tail), 0.0)
        return jnp.einsum('bhqk,bhkd->bhqd', w, vf)

    out = lax.map(block, jnp.arange(S // Q_BLOCK))
    out = out.transpose(1, 2, 0, 3, 4).reshape(B, H, S, d)
    return out.astype(q.dtype)

def forgetting_attention(q, k, v, f_logit):
    B, H, S, d = q.shape
    scale = 1.0 / math.sqrt(d)
    kf = k.astype(jnp.float32)
    vf = v.astype(jnp.float32)
    c = lax.cumsum(jax.nn.log_sigmoid(f_logit.astype(jnp.float32)), axis=2)
    key_pos = jnp.arange(S)

    def block(i):
        t0 = i * Q_BLOCK
        qb = lax.dynamic_slice_in_dim(q, t0, Q_BLOCK, axis=2).astype(jnp.float32)
        cq = lax.dynamic_slice_in_dim(c, t0, Q_BLOCK, axis=2)
        logits = jnp.einsum('bhqd,bhkd->bhqk', qb, kf) * scale + (cq[..., :, None] - c[..., None, :])
        q_pos = t0 + jnp.arange(Q_BLOCK)
        causal = key_pos[None, :] <= q_pos[:, None]
        p = jax.nn.softmax(jnp.where(causal, logits, NEG_INF), axis=-1)
        return jnp.einsum('bhqk,bhkd->bhqd', p, vf)

    out = lax.map(block, jnp.arange(S // Q_BLOCK))
    out = out.transpose(1, 2, 0, 3, 4).reshape(B, H, S, d)
    return out.astype(q.dtype)

def moba_attention(q, k, v, slopes):
    B, H, S, d = q.shape
    scale = 1.0 / math.sqrt(d)
    n_kb = -(-S // MOBA_BLOCK)
    n_top = min(MOBA_TOPK, n_kb)
    pad = n_kb * MOBA_BLOCK - S
    kf = jnp.pad(k.astype(jnp.float32), ((0, 0), (0, 0), (0, pad), (0, 0)))
    vf = jnp.pad(v.astype(jnp.float32), ((0, 0), (0, 0), (0, pad), (0, 0)))
    k_blocks = kf.reshape(B, H, n_kb, MOBA_BLOCK, d)
    v_blocks = vf.reshape(B, H, n_kb, MOBA_BLOCK, d)
    k_mean = jnp.mean(k_blocks, axis=3)
    b_idx = jnp.arange(B)[:, None, None, None]
    h_idx = jnp.arange(H)[None, :, None, None]
    blk_ids = jnp.arange(n_kb)
    offs = jnp.arange(MOBA_BLOCK)
    slope = slopes[None, :, None, None]
    n_sel = n_top * MOBA_BLOCK

    def chunk(c):
        t0 = c * MOBA_Q_CHUNK
        own = t0 // MOBA_BLOCK
        qc = lax.dynamic_slice_in_dim(q, t0, MOBA_Q_CHUNK, axis=2).astype(jnp.float32)
        q_pos = t0 + jnp.arange(MOBA_Q_CHUNK)
        route = jnp.einsum('bhqd,bhnd->bhqn', qc, k_mean)
        route = jnp.where(blk_ids < own, route, NEG_INF)
        _, sel = lax.top_k(route, n_top)
        sel_valid = sel < own
        k_sel = k_blocks[b_idx, h_idx, sel]
        v_sel = v_blocks[b_idx, h_idx, sel]
        s_sel = jnp.einsum('bhqd,bhqrnd->bhqrn', qc, k_sel) * scale
        pos_sel = sel[..., None] * MOBA_BLOCK + offs
        s_sel = s_sel - slope[..., None] * (q_pos[:, None, None] - pos_sel)
        s_sel = jnp.where(sel_valid[..., None], s_sel, NEG_INF).reshape(B, H, MOBA_Q_CHUNK, n_sel)
        k_own = lax.dynamic_slice_in_dim(kf, own * MOBA_BLOCK, MOBA_BLOCK, axis=2)
        v_own = lax.dynamic_slice_in_dim(vf, own * MOBA_BLOCK, MOBA_BLOCK, axis=2)
        rel = q_pos[:, None] - (own * MOBA_BLOCK + offs)[None, :]
        s_own = jnp.einsum('bhqd,bhnd->bhqn', qc, k_own) * scale - slope * rel
        s_own = jnp.where(rel >= 0, s_own, NEG_INF)
        p = jax.nn.softmax(jnp.concatenate([s_sel, s_own], axis=-1), axis=-1)
        p_sel = p[..., :n_sel].reshape(B, H, MOBA_Q_CHUNK, n_top, MOBA_BLOCK)
        p_own = p[..., n_sel:]
        return (jnp.einsum('bhqrn,bhqrnd->bhqd', p_sel, v_sel)
                + jnp.einsum('bhqn,bhnd->bhqd', p_own, v_own))

    out = lax.map(chunk, jnp.arange(S // MOBA_Q_CHUNK))
    out = out.transpose(1, 2, 0, 3, 4).reshape(B, H, S, d)
    return out.astype(q.dtype)

def second_inputs(seed: int = 0) -> dict:
    key = jax.random.key(seed)
    ks = jax.random.split(key, 11)
    f32 = jnp.float32
    x = jax.random.normal(ks[0], (BATCH, SEQ, D_MODEL), f32)
    norm_mix = 1.0 + 0.02 * jax.random.normal(ks[1], (DEPTH_2, D_MODEL), f32)
    w_in = jax.random.normal(ks[2], (DEPTH_2, D_MODEL, IN_COLS), f32) * D_MODEL ** -0.5
    b_forget = FORGET_BIAS_INIT + 0.5 * jax.random.normal(ks[3], (DEPTH_2, N_HEADS_FOX), f32)
    w_branch = jax.random.normal(ks[4], (DEPTH_2, N_BRANCH, BRANCH_WIDTH, D_MODEL), f32) * BRANCH_WIDTH ** -0.5
    w_out = jax.random.normal(ks[5], (DEPTH_2, D_MODEL, D_MODEL), f32) * D_MODEL ** -0.5
    norm_mlp = 1.0 + 0.02 * jax.random.normal(ks[6], (DEPTH_2, D_MODEL), f32)
    w_up = jax.random.normal(ks[7], (DEPTH_2, D_MODEL, D_FF_2), f32) * D_MODEL ** -0.5
    w_down = jax.random.normal(ks[8], (DEPTH_2, D_FF_2, D_MODEL), f32) * D_FF_2 ** -0.5
    norm_final = 1.0 + 0.02 * jax.random.normal(ks[9], (D_MODEL,), f32)
    return {"x": x, "norm_mix": norm_mix, "w_in": w_in, "b_forget": b_forget,
            "w_branch": w_branch, "w_out": w_out, "norm_mlp": norm_mlp,
            "w_up": w_up, "w_down": w_down, "norm_final": norm_final}

def second_block(x, norm_mix, w_in, b_forget, w_branch, w_out, norm_mlp, w_up, w_down, norm_final):
    B, S, _ = x.shape
    slopes = alibi_slopes_2(N_HEADS_MOBA)
    for l in range(DEPTH_2):
        h = rmsnorm(x, norm_mix[l])
        proj = jnp.einsum('bsd,de->bse', h, w_in[l])
        q_a, k_a, v_a, q_b, k_b, v_b, f_b, q_c, k_c, v_c, g = split_in_proj(proj)
        o_a = stick_breaking_attention(to_heads(q_a, N_HEADS_SB), to_heads(k_a, N_HEADS_SB),
                                       to_heads(v_a, N_HEADS_SB))
        f_logit = (f_b + b_forget[l]).transpose(0, 2, 1)
        o_b = forgetting_attention(to_heads(q_b, N_HEADS_FOX), to_heads(k_b, N_HEADS_FOX),
                                   to_heads(v_b, N_HEADS_FOX), f_logit)
        o_c = moba_attention(to_heads(q_c, N_HEADS_MOBA), to_heads(k_c, N_HEADS_MOBA),
                             to_heads(v_c, N_HEADS_MOBA), slopes)
        branches = jnp.stack([merge_heads(o_a), merge_heads(o_b), merge_heads(o_c)], axis=2)
        lifted = jnp.einsum('bsnw,nwd->bsnd', branches, w_branch[l])
        gates = jax.nn.sigmoid(g.reshape(B, S, N_BRANCH, D_MODEL))
        mixed = jnp.sum(gates * lifted, axis=2)
        x = x + jnp.einsum('bsd,de->bse', mixed, w_out[l])
        h = rmsnorm(x, norm_mlp[l])
        hid = jnp.square(jax.nn.relu(jnp.einsum('bsd,df->bsf', h, w_up[l])))
        x = x + jnp.einsum('bsf,fd->bsd', hid, w_down[l])
    return rmsnorm(x, norm_final)


def setup_inputs(seed=0):
    out = dict(first_inputs(seed))
    for name, value in second_inputs(seed + 1).items():
        if name != "x":
            out[name + "_2"] = value
    return out


def reference(
    x, c, ada_w, ada_b, ln_mix_g, ln_mix_b, ln_ffn_g, ln_ffn_b, ev_w_in, ev_conv_w, ev_w_out,
    od_w_in, pool_w, pool_scale, q_norm_g, w_uq, kv_norm_g, w_ukv, od_w_out, ffn_w_up,
    ffn_conv_w, ffn_w_down, norm_mix_2, w_in_2, b_forget_2, w_branch_2, w_out_2, norm_mlp_2,
    w_up_2, w_down_2, norm_final_2,
):
    x = first_block(
        x, c, ada_w, ada_b, ln_mix_g, ln_mix_b, ln_ffn_g, ln_ffn_b, ev_w_in, ev_conv_w,
        ev_w_out, od_w_in, pool_w, pool_scale, q_norm_g, w_uq, kv_norm_g, w_ukv, od_w_out,
        ffn_w_up, ffn_conv_w, ffn_w_down,
    )
    return second_block(
        x, norm_mix_2, w_in_2, b_forget_2, w_branch_2, w_out_2, norm_mlp_2, w_up_2, w_down_2,
        norm_final_2,
    )


_drawn_inputs = setup_inputs


def setup_inputs(seed=0):
    import zlib

    import numpy as np

    out = dict(_drawn_inputs(seed))
    spreads = {}
    factors = {'ada_b': 3.943,
     'ln_mix_g': 3.239,
     'ln_mix_b': 2.726,
     'ln_ffn_g': 3.396,
     'ln_ffn_b': 3.044,
     'q_norm_g': 8.0,
     'w_uq': 3.067,
     'kv_norm_g': 8.0,
     'norm_mix_2': 4.403,
     'norm_mlp_2': 9.459,
     'norm_final_2': 7.376}
    for name, (base, spread) in spreads.items():
        noise = np.random.default_rng([zlib.crc32(name.encode()), seed]).standard_normal(out[name].shape)
        drawn = base * np.exp(spread * noise) if base else spread * noise
        out[name] = __import__('jax').numpy.asarray(drawn.astype(out[name].dtype))
    for name, factor in factors.items():
        out[name] = (out[name] * factor).astype(out[name].dtype)
    return out
```

```python
from contextlib import ExitStack

import numpy as np
import concourse.bass as bass
from concourse import mybir

ALU = mybir.AluOpType
ACT = mybir.ActivationFunctionType
AX = mybir.AxisListType
F32 = mybir.dt.float32
F32R = mybir.dt.float32r

P = 128
S = 256
TT = S // P
D = 1024
KD = D // P
DH = 64
HEADS = 8
CHUNK = 64
TOPK = S // 4
D_FF = 2816
NB_FF = D_FF // P
D_FF2 = 4096
NB_FF2 = D_FF2 // P
Q_LORA = 384
KV_LORA = 256
D_ROPE = 32
ODD_IN = 512 + Q_LORA + KV_LORA + D_ROPE
WINDOWS = (2, 4, 8, 16)
PAD = 16
ALPHA = 4 ** 0.25
LN_EPS = 1e-5
RMS_EPS = 1e-6
SCALE = DH ** -0.5
SCALE_MLA = (64 + D_ROPE) ** -0.5
IDX_SCALE = HEADS ** -0.5 * DH ** -0.5
SLOPES = [2.0 ** (-8.0 * (h + 1) / HEADS) for h in range(HEADS)]
NEG = -1e30
BIG = 1e34
REMOVED = -3e38
UC = 256
CHUNKW = KD * UC

CONST_AT = {}


def shape_constants():
    t = np.arange(P)[:, None]
    s = np.arange(P)[None, :]
    zero = np.zeros((P, P), np.float32)
    causal = np.where(s <= t, 0.0, NEG)
    chunk = np.where(s // CHUNK <= t // CHUNK, 0.0, NEG)
    inv = 10000.0 ** (-np.arange(0, D_ROPE, 2, dtype=np.float32) / D_ROPE)
    ang = (np.arange(S, dtype=np.float32)[:, None] * inv[None, :].astype(np.float32)).astype(np.float32)
    cs = np.stack([np.cos(ang), np.sin(ang)], 1).reshape(TT, P, 2 * D_ROPE // 2).transpose(1, 0, 2).reshape(P, -1)
    count = np.stack([np.minimum(np.arange(PAD) + 1, w) for w in WINDOWS]).astype(np.float32)
    parts = {
        "ident": np.eye(P),
        "ones": np.ones((P, P)),
        "suffix": (t >= s).astype(np.float32),
        "past_T": np.concatenate([np.where(t < s, 0.0, NEG), zero, np.where(t < s, 0.0, NEG)], 1),
        "causal": np.concatenate([zero, causal], 1),
        "chunk": np.concatenate([zero, chunk], 1),
        "dist_chunk": np.concatenate([t - s + P, np.abs(t - s) - BIG * (chunk < 0) * -1.0], 1),
        "dist_causal": np.concatenate([t - s + P, np.where(s <= t, t - s, BIG)], 1),
        "rope": cs,
        "rcount": np.broadcast_to((1.0 / count).reshape(1, -1), (P, PAD * len(WINDOWS))),
    }
    at = 0
    cols = []
    for name, a in parts.items():
        CONST_AT[name] = (at, at + a.shape[1])
        at += a.shape[1]
        cols.append(a.astype(np.float32))
    return np.ascontiguousarray(np.concatenate(cols, 1))


N_CONST = shape_constants().shape[1]

DSA, MLA, FOX, MOBA = range(4)
ATT_SET = {DSA: 0, MLA: 0, FOX: 0, MOBA: 1}


def build(nc, W, consts, out):
    units = []

    def unit(name, src, c0, n, nkt):
        units.append(dict(name=name, width=nkt * n, n=n, nkt=nkt, src=src, c0=c0, kind="cols"))
        return len(units) - 1

    ev_in, od_in, w2in = W["ev_w_in"][0], W["od_w_in"][0], W["w_in_2"][0]
    G_QI = [unit("qi", ev_in, 1536 + UC * j, UC, KD) for j in range(2)]
    G_KI = unit("ki", ev_in, 1984, 192, KD)
    G_QKV = {DSA: [unit("qkv", ev_in, UC * j, UC, KD) for j in range(6)]}
    G_CX = []
    for b in range(4):
        G_CX.append(len(units))
        units.append(dict(name="cx", width=CHUNKW, src=ev_in, c0=(2632 + P * b, 3144 + P * b), kind="pair"))
    G_BG = [unit("bg", ev_in, 2120 + UC * j, UC, KD) for j in range(2)]
    G_EO = [unit("ev_out", W["ev_w_out"][0], UC * j, UC, KD) for j in range(4)]

    def ffn_units(f, w_up, nb, half):
        g0 = len(units)
        for b in range(nb):
            if half:
                units.append(dict(name="ffn", width=CHUNKW, src=w_up, c0=(P * b, half + P * b), kind="pair"))
            else:
                units.append(dict(name="ffn2", width=KD * P, n=P, nkt=KD, src=w_up, c0=P * b, kind="cols"))
        return g0

    FFN_G0 = [ffn_units(0, W["ffn_w_up"][0], NB_FF, D_FF)]
    G_Z = [unit("z", od_in, 512, 256, KD), unit("z", od_in, 768, 256, KD), unit("z", od_in, 1024, 160, KD)]
    G_U = [unit("u", od_in, UC * j, UC, KD) for j in range(2)]
    uq = W["w_uq"][0].rearrange("k (h c) -> k h c", h=HEADS)
    ukv = W["w_ukv"][0].rearrange("k (h c) -> k h c", h=HEADS)

    def head_unit(name, src, h0, nh, c0, nc_, nkt):
        units.append(dict(name=name, width=nkt * nh * nc_, n=nh * nc_, nh=nh, hc=nc_, h0=h0, c0=c0, nkt=nkt,
                          src=src, kind="heads"))
        return len(units) - 1

    G_QN = [head_unit("qn", uq, 4 * j, 4, 0, 64, 3) for j in range(2)]
    G_QR = head_unit("qr", uq, 0, 8, 64, 32, 3)
    G_KN = [head_unit("kn", ukv, 4 * j, 4, 0, 64, 2) for j in range(2)]
    G_VV = [head_unit("vv", ukv, 4 * j, 4, 64, 64, 2) for j in range(2)]
    G_OO = [unit("od_out", W["od_w_out"][0], UC * j, UC, KD) for j in range(4)]
    FFN_G0.append(ffn_units(1, W["ffn_w_up"][1], NB_FF, D_FF))
    G_QKV[FOX] = [unit("qkv", w2in, 1536 + UC * j, UC, KD) for j in range(6)]
    G_F = unit("f", w2in, 3072, P, KD)
    G_QKV[MOBA] = [unit("qkv", w2in, 3080 + UC * j, UC, KD) for j in range(6)]
    G_QKVS = [unit("qkv", w2in, UC * j, UC, KD) for j in range(6)]
    G_GATE = [unit("gate", w2in, 4616 + UC * j, UC, KD) for j in range(12)]
    G_LIFT = {}
    for c in range(4):
        for n in range(3):
            G_LIFT[c, n] = unit("lift", W["w_branch_2"][0, n], UC * c, UC, 4)
    G_WO = [unit("out2", W["w_out_2"][0], UC * j, UC, KD) for j in range(4)]
    FFN_G0.append(ffn_units(2, W["w_up_2"][0], NB_FF2, 0))
    NU = len(units)
    FFN_NB = [NB_FF, NB_FF, NB_FF2]
    FFN_D0 = [0, NB_FF, 2 * NB_FF]
    FFN_DOWN = [W["ffn_w_down"][0], W["ffn_w_down"][1], W["w_down_2"][0]]

    turns = {}
    used, filled = [0] * 8, [0] * 8

    def turn(name, bank):
        filled[bank] += name[0] not in ("pv", "acc")
        turns[name] = (bank, used[bank], filled[bank])
        used[bank] += 1

    def att_turns(a):
        for st in range(HEADS + 2):
            if st < HEADS:
                turn(("score", a, st), st % 2)
            if 1 <= st <= HEADS:
                turn(("tr", a, st - 1), 2 + (st - 1) % 2)
            if st >= 2 and st % 2 == 0:
                turn(("pv", a, st // 2 - 1), 6 + (st // 2 - 1) % 2)

    turn("stage", 6)
    turn(("modc", 0, 0), 7)

    def ht_turns(n):
        for q in range(4):
            turn(("ht", n, q), q)

    def ffn_turns(f):
        for i in range(4):
            turn(("acc", f, i), i)

    ht_turns(0)
    for h in range(HEADS):
        turn(("idx", h), h % 2)
    turn("wi", 6)
    att_turns(DSA)
    for half in range(2):
        turn(("modr", 0, 0, half), 2 + half)
    turn(("modc", 0, 1), 7)
    for half in range(2):
        turn(("modr", 0, 1, half), 2 + half)
    ht_turns(1)
    ffn_turns(0)
    turn(("modc", 1, 0), 6)
    turn(("modc", 1, 1), 7)
    ht_turns(2)
    for w in range(2):
        for half in range(2):
            turn(("modr", 1, w, half), 2 * w + half)
    turn("latT0", 0)
    turn("latT1", 1)
    turn("latT2", 6)
    turn("pool0", 2)
    turn("pool1", 3)
    turn("qrT", 7)
    turn("krT", 6)
    att_turns(MLA)
    ht_turns(3)
    ffn_turns(1)
    ht_turns(4)
    turn("ccol", 6)
    att_turns(FOX)
    att_turns(MOBA)
    for st in range(HEADS + 2):
        if st < HEADS:
            turn(("z", st), st % 2)
        if 1 <= st <= HEADS:
            turn(("sfx", st - 1), 2 + (st - 1) % 2)
        if st >= 2 and st % 2 == 0:
            turn(("pv", "stick", st // 2 - 1), 6 + (st // 2 - 1) % 2)
    ht_turns(5)
    ffn_turns(2)

    ctx = ExitStack()
    with ctx:
        def sb(name, shape, dt=F32):
            return ctx.enter_context(nc.sbuf_tensor(name, shape, dt))

        def sem(name):
            return ctx.enter_context(nc.semaphore(name))

        raw = [sb(f"raw{i}", [P, CHUNKW]) for i in range(2)]
        uh = [sb(f"unit_hi{i}", [P, CHUNKW], F32R) for i in range(2)]
        ul = [sb(f"unit_lo{i}", [P, CHUNKW], F32R) for i in range(2)]
        rawd = [sb(f"raw_down{i}", [P, D]) for i in range(2)]
        down = sb("down", [P, 2, 2, D], F32R)
        accg = sb("accg", [P, 6 * D])
        x = sb("x", [P, TT, D])
        hh = sb("h_hi", [P, KD, S], F32R)
        hl = sb("h_lo", [P, KD, S], F32R)
        hf = sb("h_full", [P, 4 * S])
        yh = sb("y_hi", [P, KD, S], F32R)
        yl = sb("y_lo", [P, KD, S], F32R)
        att = sb("att", [P, 2, 3072])
        ada1 = sb("ada1", [P, CHUNKW + UC])
        cst = sb("consts", [P, N_CONST])
        work = sb("work", [P, 3072])
        grow = sb("gate_rows", [P, 2, D])
        cols = sb("cols", [P, 512])
        small = sb("small", [P, 256])

        def C(name):
            return cst[:, CONST_AT[name][0]:CONST_AT[name][1]]

        ident, ones = C("ident"), C("ones")
        ada = [att[:, 1, 0:CHUNKW + UC], ada1[:, :]]
        kiT = att[:, 1, 2304:2560]
        qiT = hf[:, :].rearrange("p (b t) -> p b t", b=4)
        ybc = hf[:, :].rearrange("p (b t) -> p b t", b=4)

        def qT(a):
            return att[:, a, 0:1024].rearrange("p (b t) -> p b t", b=4)

        def kT(a):
            return att[:, a, 1024:2048].rearrange("p (b t) -> p b t", b=4)

        def vv(a):
            return att[:, a, 2048:3072].rearrange("p (t n) -> p t n", t=TT)

        lnrow = att[:, 0, 0:2 * D].rearrange("p (a n) -> p a n", a=2)
        xn = att[:, 1, 0:TT * D].rearrange("p (t n) -> p t n", t=TT)
        mixed = att[:, 1, 0:KD * S].rearrange("p (k t) -> p k t", k=KD)
        stage = [work[:, P * i:P * (i + 1)] for i in range(4)]
        c_col = cols[:, 0:8]
        ev_conv = cols[:, 8:20]
        pool_scale = cols[:, 20:24]
        q_gain = cols[:, 24:27]
        kv_gain = cols[:, 27:29]
        mix_gain = cols[:, 29:37]
        mlp_gain = cols[:, 37:45]
        conv_w = [cols[:, 64:64 + 132], cols[:, 200:200 + 132]]
        modT = cols[:, 340:340 + 96].rearrange("p (l j) -> p l j", l=2)
        cond = cols[:, 440:448]
        cgb = [work[:, 1536:1792], work[:, 1920:2176]]
        cgx = [work[:, 768:1024], work[:, 1152:1408]]
        L = [work[:, 384 * i:384 * (i + 1)] for i in range(2)]
        PT = [work[:, 768 + 384 * i:768 + 384 * (i + 1)] for i in range(2)]
        rel = [work[:, 1536 + 384 * i:1536 + 384 * (i + 1)] for i in range(2)]
        idx = work[:, 2304:2688]
        distm = work[:, 2688:3072]
        zm = [work[:, 384 * i:384 * (i + 1)] for i in range(2)]
        sig = [work[:, 768 + 384 * i:768 + 384 * (i + 1)] for i in range(2)]
        sp = [work[:, 1536 + 384 * i:1536 + 384 * (i + 1)] for i in range(2)]
        wT = [work[:, 2304 + 384 * i:2304 + 384 * (i + 1)] for i in range(2)]
        fv = [work[:, 512 * i:512 * i + 256] for i in range(2)]
        fg = [work[:, 512 * i + 256:512 * i + 512] for i in range(2)]
        tmp = work[:, 1024:1536]
        acth = [yh[:, i, :] for i in range(2)]
        actl = [yl[:, i, :] for i in range(2)]
        smax = small[:, 0:16].rearrange("p (h t) -> p h t", t=2)
        sbias = small[:, 16:32].rearrange("p (h t) -> p h t", t=2)
        ssum = small[:, 32:48].rearrange("p (h t) -> p h t", t=2)
        srec = small[:, 48:64].rearrange("p (h t) -> p h t", t=2)
        wi = small[:, 64:80]
        top8 = small[:, 80:88]
        bnst = small[:, 88:112].rearrange("p (t a) -> p t a", t=2)
        mv = small[:, 112:116].rearrange("p (t a) -> p t a", t=2)
        var = small[:, 116:120]
        rstd = small[:, 120:124]
        half_neg = small[:, 124:128]
        ccol = small[:, 128:144].rearrange("p (t h) -> p t h", t=2)
        bfor = small[0:8, 144:145]
        cexp = small[:, 152:160]
        sqs = small[:, 164:168]
        zrow = accg[:, 0:1344].rearrange("p (t n) -> p t n", t=TT)
        upad = accg[:, 1344:2432].rearrange("p (g n) -> p g n", g=4)
        pp = [accg[:, 2432:2704], accg[:, 2704:2976]]
        pooled = accg[:, 2976:4000].rearrange("p (g n) -> p g n", g=4)
        qrow = accg[:, 4000:4512].rearrange("p (t n) -> p t n", t=TT)
        rt = [accg[:, 4512:4640], accg[:, 4640:4768]]
        qrot = accg[:, 4768:5280].rearrange("p (t n) -> p t n", t=TT)
        krot = accg[:, 5280:5536].rearrange("p (t n) -> p t n", t=TT)
        pool_w = accg[:, 5536:6048].rearrange("p (g n) -> p g n", g=4)
        qrT = att[:, 1, 0:512].rearrange("p (b t) -> p b t", b=2)
        krT = att[:, 1, 512:768]
        sq_scr = att[:, 1, 768:768 + Q_LORA]
        latn = att[:, 1, 1152:1152 + 1280].rearrange("p (t n) -> p t n", t=TT)
        downf = down[:, :, :, :].rearrange("p a b n -> p (a b n)")
        lat_h = downf[:, 0:1280].rearrange("p (k t) -> p k t", k=5)
        lat_l = downf[:, 1280:2560].rearrange("p (k t) -> p k t", k=5)
        lat_f = hf[:, :]
        gates = accg[:, :].rearrange("p (k t) -> p k t", k=24)
        o_h = [yh[:, 0:4, :], yh[:, 4:8, :], downf[:, 0:1024].rearrange("p (k t) -> p k t", k=4)]
        o_l = [yl[:, 0:4, :], yl[:, 4:8, :], downf[:, 1024:2048].rearrange("p (k t) -> p k t", k=4)]
        f_t = [hf[0:8, 256 * i:256 * (i + 1)] for i in range(4)]

        bank = [ctx.enter_context(nc.psum_tensor(f"bank{i}", [P, 512], F32)) for i in range(8)]

        bank_full = [sem(f"bank_full{i}") for i in range(8)]
        bank_free = [sem(f"bank_free{i}") for i in range(8)]
        raw_in = [sem(f"raw_in{i}") for i in range(2)]
        rawd_in = [sem(f"rawd_in{i}") for i in range(2)]
        ada_in = [sem(f"ada_in{i}") for i in range(2)]
        hi_up, lo_up, hi_dn, lo_dn = sem("hi_up"), sem("lo_up"), sem("hi_dn"), sem("lo_dn")
        down_done = sem("down_done")
        stage_in, const_in, x_in, ln_in, pw_in, out_done = (sem(n) for n in (
            "stage_in", "const_in", "x_in", "ln_in", "pool_w_in", "out_done"))
        dve_chain, act_chain, pool_chain = sem("dve_chain"), sem("act_chain"), sem("pool_chain")
        cond_exp, ada_acc = sem("cond_exp"), sem("ada_acc")
        row_ready, h_hi, h_lo = sem("row_ready"), sem("h_hi"), sem("h_lo")
        var_ready, rstd_ready = sem("var_ready"), sem("rstd_ready")
        idx_acc = sem("idx_acc")
        max_ready, exp_done, p_ready, pv_done, o_hi = (sem(n) for n in (
            "max_ready", "exp_done", "p_ready", "pv_done", "o_hi"))
        cg_ready, yb_hi, yb_lo = sem("cg_ready"), sem("yb_hi"), sem("yb_lo")
        tap_done, silu_done, prod_done, act_hi, act_lo = (sem(n) for n in (
            "tap_done", "silu_done", "prod_done", "act_hi", "act_lo"))
        lat_sq, lat_norm, lat_hi, lat_lo = sem("lat_sq"), sem("lat_norm"), sem("lat_hi"), sem("lat_lo")
        pool_ready, pool_hi, pool_lo, rot_ready, pool_zero = (sem(n) for n in (
            "pool_ready", "pool_hi", "pool_lo", "rot_ready", "pool_zero"))
        f_log, c_ready = sem("f_log"), sem("c_ready")
        soft_log, sp_ready, w_ready = sem("soft_log"), sem("sp_ready"), sem("w_ready")
        gate_ready, mix_ready, mix_hi, mix_lo = (sem(n) for n in ("gate_ready", "mix_ready", "mix_hi", "mix_lo"))

        ATT_N = {DSA: 0, MLA: 1, FOX: 2, MOBA: 3, "stick": 4}

        ATT_OUT = {DSA: (yh[:, 0:4, :], yl[:, 0:4, :]), MLA: (yh[:, 4:8, :], yl[:, 4:8, :]),
                   FOX: (o_h[1], o_l[1]), MOBA: (o_h[2], o_l[2]), "stick": (o_h[0], o_l[0])}

        def att_count(a, h):
            return HEADS * ATT_N[a] + h + 1

        def full(eng, name):
            b, _, k = turns[name]
            eng.wait_ge(bank_full[b], k)
            return bank[b]

        def evacuated(eng, name):
            b, k, _ = turns[name]
            eng.wait_ge(bank_free[b], k + 1)

        def free(name):
            return bank_free[turns[name][0]]

        def unit_full(eng, g):
            eng.wait_ge(bank_full[4 + g % 2], g // 2 + 1)
            return bank[4 + g % 2]

        def unit_evacuated(eng, g):
            eng.wait_ge(bank_free[4 + g % 2], g // 2 + 1)

        def unit_free(g):
            return bank_free[4 + g % 2]

        class Chain:

            def __init__(self, eng, semaphore):
                self.eng, self.sem, self.base, self.k = eng, semaphore, 0, 0

            def __call__(self, ins):
                self.k += 1
                ins.then_inc(self.sem, 1)
                self.eng.wait_ge(self.sem, self.base + self.k)

            def enter(self, i, first, per):
                self.start = self.base + self.k
                self.base, self.k = i * per + (self.start - first * per), 0

            def leave(self, iterations, per):
                assert self.k == per, (self.k, per)
                self.base, self.k = self.start + iterations * per, 0

        FILL = {DSA: {2: [G_BG[0]], 5: [G_BG[1]]}, MLA: {},
                FOX: {1 + i: [G_QKV[MOBA][i]] for i in range(6)},
                MOBA: {1 + i: [G_QKVS[i]] for i in range(6)},
                "stick": {i: [G_GATE[i]] for i in range(10)}}
        ADA_IDX = {1: [8], 3: [9], 5: [10], 7: [11]}
        ADA_ATT = {i: [12 + i] for i in range(10)}
        ADA_LATE = [22, 23]

        block = ctx.enter_context(nc.Block())

        @block.sync
        def _(sp_):
            def load_unit(g):
                u, s = units[g], g % 2
                if g >= 2:
                    sp_.wait_ge(lo_up, g - 1)
                if u["kind"] == "pair":
                    dst = raw[s][:, :].rearrange("p (t a n) -> p t a n", t=KD, a=2)
                    for a in range(2):
                        src = u["src"][:, u["c0"][a]:u["c0"][a] + P].rearrange("(t p) n -> p t n", p=P)
                        sp_.dma_start(dst[:, :, a, :], src).then_inc(raw_in[s], 16)
                elif u["kind"] == "heads":
                    nkt, n = u["nkt"], u["n"]
                    for lo, hi in ((0, 1), (1, nkt)):
                        for t in range(lo, hi):
                            dst = raw[s][:, t * n:(t + 1) * n].rearrange("p (h c) -> p h c", h=u["nh"])
                            src = u["src"][t * P:(t + 1) * P, u["h0"]:u["h0"] + u["nh"], u["c0"]:u["c0"] + u["hc"]]
                            sp_.dma_start(dst, src).then_inc(raw_in[s], 16)
                else:
                    nkt, n = u["nkt"], u["n"]
                    dst = raw[s][:, 0:nkt * n].rearrange("p (t n) -> p t n", t=nkt)
                    src = u["src"][:, u["c0"]:u["c0"] + n].rearrange("(t p) n -> p t n", p=P)
                    m = nkt // 2
                    for a, b in ((0, m), (m, nkt)):
                        sp_.dma_start(dst[:, a:b, :], src[:, a:b, :]).then_inc(raw_in[s], 16)

            def load_ada(a):
                layer, j, s = a // 24, a % 24, a % 2
                if a >= 2:
                    sp_.wait_ge(ada_acc, a - 1)
                sp_.dma_start(ada[s][:, 0:CHUNKW].rearrange("p (t n) -> p t n", t=KD),
                              W["ada_w"][layer][:, UC * j:UC * (j + 1)].rearrange("(t p) n -> p t n", p=P)
                              ).then_inc(ada_in[s], 16)
                sp_.dma_start(ada[s][0:1, CHUNKW:CHUNKW + UC],
                              W["ada_b"][layer:layer + 1, UC * j:UC * (j + 1)]).then_inc(ada_in[s], 16)

            rows = lambda a: a.rearrange("a (b n) -> (a b) n", n=P)
            for dst, src in (
                    (stage[0][0:8, :], rows(W["c"])), (stage[0][8:20, :], rows(W["ev_conv_w"][0])),
                    (stage[0][20:24, :], rows(W["pool_scale"])), (stage[0][24:27, :], rows(W["q_norm_g"])),
                    (stage[0][27:29, :], rows(W["kv_norm_g"])), (stage[0][29:37, :], rows(W["norm_mix_2"])),
                    (stage[0][37:45, :], rows(W["norm_mlp_2"])),
                    (stage[1][:, :], rows(W["ffn_conv_w"][0])[0:P, :]), (stage[2][:, :], rows(W["ffn_conv_w"][1])[0:P, :]),
                    (stage[3][0:4, :], rows(W["ffn_conv_w"][0])[P:132, :]), (stage[3][4:8, :], rows(W["ffn_conv_w"][1])[P:132, :]),
                    (bfor, W["b_forget_2"].rearrange("a n -> n a"))):
                sp_.dma_start(dst, src).then_inc(stage_in, 16)
            sp_.dma_start(cst[:, :], consts).then_inc(const_in, 16)
            load_ada(0)
            load_ada(1)
            sp_.dma_start(x[:, :, :], W["x"][0].rearrange("(t p) n -> p t n", p=P)).then_inc(x_in, 16)
            for a in range(2, 8):
                load_ada(a)
            for g in range(G_QKV[DSA][2]):
                load_unit(g)
            for h in range(HEADS):
                for a in ADA_IDX.get(h, []):
                    load_ada(a)
                if h % 2 == 0:
                    load_unit(G_QKV[DSA][2 + h // 2])
            for g in G_CX + G_BG:
                load_unit(g)
            for st in range(HEADS + 2):
                for g in FILL[DSA].get(st, []):
                    load_unit(g + 2)
                for a in ADA_ATT[st]:
                    load_ada(a)
            for a in ADA_LATE:
                load_ada(a)
            for g in G_EO[2:]:
                load_unit(g)

            def load_ffn(f, i, k, fixed):
                g0, d0, nb = FFN_G0[f], FFN_D0[f], FFN_NB[f]
                b = 2 * i + k
                s = (g0 + k) % 2
                sp_.wait_ge(lo_up, b + (g0 - 1))
                u = units[g0]
                if u["kind"] == "pair":
                    dst = raw[s][:, :].rearrange("p (t a n) -> p t a n", t=KD, a=2)
                    for a in range(2):
                        src = u["src"][:, bass.ds(b * P + a * D_FF, P)].rearrange("(t p) n -> p t n", p=P)
                        sp_.dma_start(dst[:, :, a, :], src).then_inc(raw_in[s], 16)
                else:
                    dst = raw[s][:, 0:KD * P].rearrange("p (t n) -> p t n", t=KD)
                    for a in range(2):
                        src = u["src"][a * 512:(a + 1) * 512, bass.ds(b * P, P)].rearrange("(t p) n -> p t n", p=P)
                        sp_.dma_start(dst[:, 4 * a:4 * a + 4, :], src).then_inc(raw_in[s], 16)
                if not (fixed and d0 + b < 2):
                    sp_.wait_ge(lo_dn, b + (d0 - 1))
                sp_.dma_start(rawd[k][:, :], FFN_DOWN[f][bass.ds(b * P, P), :]).then_inc(rawd_in[k], 16)
                if f == 0:
                    sp_.wait_ge(ada_acc, b + 23)
                    sp_.dma_start(ada[k][:, 0:CHUNKW].rearrange("p (t n) -> p t n", t=KD),
                                  W["ada_w"][1][:, bass.ds(b * UC, UC)].rearrange("(t p) n -> p t n", p=P)
                                  ).then_inc(ada_in[k], 16)
                    sp_.dma_start(ada[k][0:1, CHUNKW:CHUNKW + UC],
                                  W["ada_b"][1:2, bass.ds(b * UC, UC)]).then_inc(ada_in[k], 16)

            def load_all_ffn(f):
                for k in range(2):
                    load_ffn(f, 0, k, True)
                with sp_.Fori(1, FFN_NB[f] // 2) as i:
                    for k in range(2):
                        load_ffn(f, i, k, False)

            load_all_ffn(0)
            for g in G_Z[:2]:
                load_unit(g)
            for a in (46, 47):
                load_ada(a)
            for g in G_Z[2:] + G_U:
                load_unit(g)
            evacuated(sp_, ("modr", 1, 1, 1))
            sp_.dma_start(pool_w, W["pool_w"][0].rearrange("g c d -> c g d")).then_inc(pw_in, 16)
            for g in G_QN + [G_QR] + G_KN + G_VV + G_OO:
                load_unit(g)
            load_all_ffn(1)
            for g in range(G_QKV[FOX][0], FFN_G0[2]):
                load_unit(g)
            load_all_ffn(2)
            sp_.wait_ge(row_ready, 14)
            sp_.dma_start(out[0].rearrange("(t p) n -> p t n", p=P), xn).then_inc(out_done, 16)
            sp_.wait_ge(out_done, 16)

        raw_loads = [0, 0]
        raw_need = []
        for g, u in enumerate(units):
            raw_loads[g % 2] += 16 * (u["nkt"] if u["kind"] == "heads" else 2)
            raw_need.append(raw_loads[g % 2])

        @block.gpsimd
        def _(pool):
            def lo_unit(g):
                if g >= NU:
                    return
                pool.wait_ge(hi_up, g + 1)
                w = units[g]["width"]
                nc.gpsimd.tensor_tensor(ul[g % 2][:, 0:w], raw[g % 2][:, 0:w], uh[g % 2][:, 0:w].bitcast(F32),
                                        ALU.subtract).then_inc(lo_up, 1)

            def lo_down(d):
                pool.wait_ge(hi_dn, d + 1)
                s = d % 2
                nc.gpsimd.tensor_tensor(down[:, s, 1, :], rawd[s][:, :], down[:, s, 0, :].bitcast(F32),
                                        ALU.subtract).then_inc(lo_dn, 1)

            def power(n, w):
                pool.wait_ge(var_ready, n + 1)
                nc.gpsimd.tensor_tensor(rstd[:, 0:w], var[:, 0:w], half_neg[:, 0:w], ALU.pow).then_inc(rstd_ready, 1)

            def h_low(n):
                for q in range(4):
                    pool.wait_ge(h_hi, 4 * n + q + 1)
                    nc.gpsimd.tensor_tensor(hl[:, 2 * q:2 * q + 2, :],
                                            hf[:, 512 * (q % 2):512 * (q % 2) + 512].rearrange("p (k t) -> p k t", k=2),
                                            hh[:, 2 * q:2 * q + 2, :].bitcast(F32), ALU.subtract).then_inc(h_lo, 1)

            def ffn(f):
                g0, d0, nb = FFN_G0[f], FFN_D0[f], FFN_NB[f]
                w = units[g0]["width"]
                lo_down(d0)

                def body(i, k):
                    b = 2 * i + k
                    s = (g0 + k) % 2
                    pool.wait_ge(hi_up, b + (g0 + 3))
                    nc.gpsimd.tensor_tensor(ul[s][:, 0:w], raw[s][:, 0:w], uh[s][:, 0:w].bitcast(F32),
                                            ALU.subtract).then_inc(lo_up, 1)
                    pool.wait_ge(hi_dn, b + (d0 + 2))
                    nc.gpsimd.tensor_tensor(down[:, 1 - k, 1, :], rawd[1 - k][:, :], down[:, 1 - k, 0, :].bitcast(F32),
                                            ALU.subtract).then_inc(lo_dn, 1)

                with pool.Fori(0, nb // 2 - 1) as i:
                    for k in range(2):
                        body(i, k)
                lo_unit(g0 + nb)
                lo_down(d0 + nb - 1)
                lo_unit(g0 + nb + 1)

            nc.gpsimd.memset(half_neg[:, :], -0.5).then_inc(pool_chain, 1)
            pool.wait_ge(pool_chain, 1)
            lo_unit(0)
            lo_unit(1)
            h_low(0)
            for g in range(2, G_EO[-1] + 3):
                lo_unit(g)
            power(0, 2)
            h_low(1)
            ffn(0)
            power(1, 2)
            h_low(2)
            evacuated(pool, ("modr", 1, 1, 1))
            for pad in (upad[:, :, 0:PAD], pp[0][:, 0:PAD], pp[1][:, 0:PAD]):
                nc.gpsimd.memset(pad, 0.0).then_inc(pool_zero, 1)
            for g in range(G_Z[0] + 2, G_Z[-1] + 3):
                lo_unit(g)
            power(2, 4)
            for g in range(G_Z[-1] + 3, G_OO[-1] + 3):
                lo_unit(g)
            power(3, 2)
            h_low(3)
            ffn(1)
            power(4, 2)
            power(5, 2)
            h_low(4)
            for g in range(G_QKV[FOX][0] + 2, G_WO[-1] + 3):
                lo_unit(g)
            power(6, 2)
            h_low(5)
            ffn(2)
            power(7, 2)

        @block.scalar
        def _(act):
            link = Chain(act, act_chain)

            def hi_unit(g):
                if g >= NU:
                    return
                s, w = g % 2, units[g]["width"]
                act.wait_ge(raw_in[s], raw_need[g])
                if g >= 2:
                    act.wait_ge(bank_full[4 + s], g // 2)
                nc.scalar.activation(uh[s][:, 0:w], raw[s][:, 0:w], ACT.Copy).then_inc(hi_up, 1)

            def hi_down(d):
                s = d % 2
                act.wait_ge(rawd_in[s], 16 * (d // 2 + 1))
                if d >= 2:
                    act.wait_ge(down_done, d - 1)
                nc.scalar.activation(down[:, s, 0, :], rawd[s][:, :], ACT.Copy).then_inc(hi_dn, 1)

            def h_high(n):
                for q in range(4):
                    evacuated(act, ("ht", n, q))
                    nc.scalar.activation(hh[:, 2 * q:2 * q + 2, :],
                                         hf[:, 512 * (q % 2):512 * (q % 2) + 512].rearrange("p (k t) -> p k t", k=2),
                                         ACT.Copy).then_inc(h_hi, 1)

            def evac(g, dst):
                b = unit_full(act, g)
                nc.scalar.activation(dst, b[:, :].rearrange("p (k t) -> p k t", k=2), ACT.Copy).then_inc(unit_free(g), 1)
                hi_unit(g + 2)

            def evac_qkv(g, a, j):
                evac(g, qT(a)[:, 2 * j:2 * j + 2, :] if j < 2 else kT(a)[:, 2 * j - 4:2 * j - 2, :] if j < 4
                     else vv(a)[:, :, UC * (j - 4):UC * (j - 3)])

            def other(g):
                unit_full(act, g)
                hi_unit(g + 2)

            def exps(a, h):
                scale = SCALE_MLA if a == MLA else SCALE
                act.wait_ge(max_ready, att_count(a, h))
                t = L[h % 2]
                nc.scalar.activation(t[:, 0:128], t[:, 0:128], ACT.Exp, bias=sbias[:, h, 0:1], scale=scale,
                                     accum_out=ssum[:, h, 0:1])
                nc.scalar.activation(t[:, 128:384], t[:, 128:384], ACT.Exp, bias=sbias[:, h, 1:2], scale=scale,
                                     accum_out=ssum[:, h, 1:2]).then_inc(exp_done, 1)

            def evac_pt(a, h):
                b = full(act, ("tr", a, h))
                if att_count(a, h) > 2:
                    act.wait_ge(pv_done, att_count(a, h) - 2)
                nc.scalar.activation(PT[h % 2], b[:, 0:384], ACT.Copy).then_inc(free(("tr", a, h)), 1)

            def out_high(a, p):
                act.wait_ge(pv_done, att_count(a, 2 * p + 1))
                b = bank[turns["pv", a, p][0]]
                nc.scalar.activation(ATT_OUT[a][0][:, p, :], b[:, 0:256], ACT.Copy).then_inc(o_hi, 1)

            def attention(a, filler):
                for st in range(HEADS + 2):
                    if st < HEADS:
                        exps(a, st)
                    for g in FILL[a].get(st, []):
                        filler(g)
                    if 1 <= st <= HEADS:
                        evac_pt(a, st - 1)
                    if st >= 2 and st % 2 == 1:
                        out_high(a, (st - 2) // 2)

            def load_rows(a, *srcs):
                for i, src in enumerate(srcs):
                    act.dma_start(lnrow[:, i, :], src.partition_broadcast(P)).then_inc(ln_in, 16)

            def ffn(f):
                g0, d0, nb = FFN_G0[f], FFN_D0[f], FFN_NB[f]
                w = units[g0]["width"]
                half = units[g0]["kind"] == "pair"
                act0 = sum(FFN_NB[:f])
                hi_down(d0)

                def body(i, k, fixed):
                    b, s = 2 * i + k, (g0 + k) % 2
                    act.wait_ge(bank_full[4 + s], i + ((g0 + k) // 2 + 1))
                    if not (fixed and act0 + b < 2):
                        act.wait_ge(act_lo, b + (act0 - 1))
                    if half:
                        cw = conv_w[f]
                        nc.scalar.activation(fv[k], bank[4 + s][:, 0:256], ACT.Copy,
                                             scale=cw[:, bass.ds(b + 2 * 44, 1)])
                        nc.scalar.activation(fg[k], bank[4 + s][:, 256:512], ACT.Copy,
                                             scale=cw[:, bass.ds(b + (2 * 44 + 22), 1)]).then_inc(tap_done, 1)
                    else:
                        nc.scalar.activation(fv[k], bank[4 + s][:, 0:256], ACT.Relu).then_inc(bank_free[4 + s], 1)
                    if fixed:
                        hi_unit(g0 + b + 2)
                    else:
                        act.wait_ge(raw_in[s], i * 32 + (raw_need[g0 + k] + 32))
                        nc.scalar.activation(uh[s][:, 0:w], raw[s][:, 0:w], ACT.Copy).then_inc(hi_up, 1)
                    if half:
                        act.wait_ge(bank_free[4 + s], i + ((g0 + k) // 2 + 1))
                        nc.scalar.activation(fg[k], fg[k], ACT.Silu).then_inc(silu_done, 1)
                    if fixed:
                        if b + 1 < nb:
                            hi_down(d0 + b + 1)
                    else:
                        act.wait_ge(rawd_in[1 - k], i * 16 + (16 * ((d0 + k + 1) // 2) + 16))
                        act.wait_ge(down_done, b + d0)
                        nc.scalar.activation(down[:, 1 - k, 0, :], rawd[1 - k][:, :], ACT.Copy).then_inc(hi_dn, 1)
                    act.wait_ge(prod_done, b + (act0 + 1))
                    nc.scalar.activation(acth[k], fv[k], ACT.Copy).then_inc(act_hi, 1)

                for k in range(2):
                    body(0, k, True)
                with act.Fori(1, nb // 2 - 1) as i:
                    for k in range(2):
                        body(i, k, False)
                for k in range(2):
                    body(nb // 2 - 1, k, True)

            evacuated(act, "stage")
            nc.scalar.activation(cexp, c_col, ACT.Exp, scale=-1.0).then_inc(cond_exp, 1)
            hi_unit(0)
            hi_unit(1)
            h_high(0)
            for j in range(2):
                evac(G_QI[j], qiT[:, 2 * j:2 * j + 2, :])
            full(act, "wi")
            nc.scalar.activation(wi, bank[turns["wi"][0]][:, 0:16], ACT.Copy, scale=IDX_SCALE).then_inc(free("wi"), 1)
            b = unit_full(act, G_KI)
            nc.scalar.activation(kiT[0:64, :], b[0:64, 0:256], ACT.Copy)
            nc.scalar.activation(kiT[64:128, :], b[64:128, 256:512], ACT.Copy).then_inc(unit_free(G_KI), 1)
            hi_unit(G_KI + 2)
            for h in range(HEADS):
                b = full(act, ("idx", h))
                if h >= 2:
                    act.wait_ge(idx_acc, h - 1)
                nc.scalar.activation(rel[h % 2], b[:, 0:384], ACT.Relu).then_inc(free(("idx", h)), 1)
                if h % 2 == 0:
                    evac_qkv(G_QKV[DSA][h // 2], 0, h // 2)
            for j in range(4, 6):
                evac_qkv(G_QKV[DSA][j], 0, j)

            def cg(i, g):
                b = unit_full(act, g)
                act.wait_ge(idx_acc, HEADS)
                nc.scalar.activation(cgb[i % 2], b[:, 0:256], ACT.Copy).then_inc(cg_ready, 1)
                hi_unit(g + 2)

            for i, g in enumerate(G_CX):
                cg(i, g)

            attention(DSA, other)
            for p in range(4):
                unit_evacuated(act, G_BG[p // 2])
                nc.scalar.activation(yh[:, 4 + p, :], ybc[:, p, :], ACT.Copy).then_inc(yb_hi, 1)
            load_rows(0, W["ln_mix_g"][0:1, :], W["ln_mix_b"][0:1, :])
            for g in G_EO:
                other(g)
            h_high(1)
            act.wait_ge(row_ready, 2)
            load_rows(0, W["ln_ffn_g"][0:1, :], W["ln_ffn_b"][0:1, :])
            ffn(0)
            h_high(2)
            evacuated(act, ("modr", 1, 1, 1))
            at = 0
            for g in G_Z:
                n = units[g]["n"]
                b = unit_full(act, g)
                nc.scalar.activation(zrow[:, :, at:at + n], b[:, 0:2 * n].rearrange("p (t n) -> p t n", t=TT),
                                     ACT.Copy).then_inc(unit_free(g), 1)
                hi_unit(g + 2)
                at += n
            for g in G_Z[1:]:
                unit_evacuated(act, g)
            for tt in range(TT):
                nc.scalar.activation(sq_scr, zrow[:, tt, 0:Q_LORA], ACT.Square, accum_out=sqs[:, tt:tt + 1]
                                     ).then_inc(lat_sq, 1)
                act.wait_ge(lat_sq, 2 * tt + 1)
                nc.scalar.activation(sq_scr[:, 0:KV_LORA], zrow[:, tt, Q_LORA:Q_LORA + KV_LORA], ACT.Square,
                                     accum_out=sqs[:, 2 + tt:3 + tt]).then_inc(lat_sq, 1)
                act.wait_ge(lat_sq, 2 * tt + 2)
            act.wait_ge(pool_zero, 3)
            for j, g in enumerate(G_U):
                evac(g, upad[:, 2 * j:2 * j + 2, PAD:PAD + S])
            for i, (k0, k1) in enumerate(((0, 2), (2, 4), (4, 5))):
                evacuated(act, f"latT{i}")
                n = k1 - k0
                nc.scalar.activation(lat_h[:, k0:k1, :], lat_f[:, 512 * (i % 2):512 * (i % 2) + 256 * n]
                                     .rearrange("p (k t) -> p k t", k=n), ACT.Copy).then_inc(lat_hi, 1)
            for j, g in enumerate(G_QN):
                evac(g, qT(0)[:, 2 * j:2 * j + 2, :])
            evac(G_QR, qrow)
            for j, g in enumerate(G_KN):
                evac(g, kT(0)[:, 2 * j:2 * j + 2, :])
            for j, g in enumerate(G_VV):
                evac(g, vv(0)[:, :, UC * j:UC * (j + 1)])
            b = full(act, "krT")
            nc.scalar.activation(krT, b[:, 0:256], ACT.Copy).then_inc(free("krT"), 1)
            b = full(act, "qrT")
            nc.scalar.activation(qrT, b[:, :].rearrange("p (k t) -> p k t", k=2), ACT.Copy).then_inc(free("qrT"), 1)
            for i in range(2):
                evacuated(act, f"pool{i}")
                nc.scalar.activation(yh[:, 2 * i:2 * i + 2, :], lat_f[:, 512 * i:512 * i + 512]
                                     .rearrange("p (k t) -> p k t", k=2), ACT.Copy).then_inc(pool_hi, 1)
            attention(MLA, None)
            load_rows(0, W["ln_mix_g"][1:2, :], W["ln_mix_b"][1:2, :])
            for g in G_OO:
                other(g)
            h_high(3)
            act.wait_ge(row_ready, 6)
            load_rows(0, W["ln_ffn_g"][1:2, :], W["ln_ffn_b"][1:2, :])
            ffn(1)
            h_high(4)
            for j, g in enumerate(G_QKV[FOX]):
                evac_qkv(g, 0, j)
            unit_evacuated(act, G_F)
            hi_unit(G_F + 2)
            link(nc.scalar.activation(f_t[1], f_t[0], ACT.Abs))
            link(nc.scalar.activation(f_t[1], f_t[1], ACT.Exp, scale=-1.0))
            nc.scalar.activation(f_t[1], f_t[1], ACT.Ln, bias=1.0).then_inc(f_log, 1)
            attention(FOX, lambda g: evac_qkv(g, 1, g - G_QKV[MOBA][0]))
            attention(MOBA, lambda g: evac_qkv(g, 0, g - G_QKVS[0]))

            def gate_evac(g):
                evac(g, gates[:, 2 * (g - G_GATE[0]):2 * (g - G_GATE[0]) + 2, :])

            for st in range(HEADS + 2):
                if st < HEADS:
                    evacuated(act, ("z", st))
                    if st >= 2:
                        act.wait_ge(sp_ready, st - 1)
                    t = sig[st % 2]
                    link(nc.scalar.activation(t, zm[st % 2], ACT.Abs))
                    link(nc.scalar.activation(t, t, ACT.Exp, scale=-1.0))
                    nc.scalar.activation(t, t, ACT.Ln, bias=1.0).then_inc(soft_log, 1)
                for g in FILL["stick"].get(st, []):
                    gate_evac(g)
                if 1 <= st <= HEADS:
                    evacuated(act, ("sfx", st - 1))
                    t = wT[(st - 1) % 2]
                    nc.scalar.activation(t, t, ACT.Exp).then_inc(w_ready, 1)
                if st >= 2 and st % 2 == 1:
                    out_high("stick", (st - 2) // 2)
            load_rows(0, W["norm_final_2"].rearrange("(a n) -> a n", a=1))
            for g in G_GATE[10:]:
                gate_evac(g)
            for g in G_GATE[-2:]:
                unit_evacuated(act, g)
            for c in range(4):
                for n in range(3):
                    v = gates[:, 8 * n + 2 * c:8 * n + 2 * c + 2, :]
                    nc.scalar.activation(v, v, ACT.Sigmoid).then_inc(gate_ready, 1)
            for c in range(4):
                for n in range(3):
                    other(G_LIFT[c, n])
                act.wait_ge(mix_ready, c + 1)
                nc.scalar.activation(hh[:, 2 * c:2 * c + 2, :], mixed[:, 2 * c:2 * c + 2, :], ACT.Copy
                                     ).then_inc(mix_hi, 1)
            for g in G_WO:
                other(g)
            h_high(5)
            ffn(2)

        @block.tensor
        def _(pe):
            def begin(name):
                b, k, _ = turns[name]
                if k:
                    pe.wait_ge(bank_free[b], k)
                return bank[b]

            def done(ins, name):
                ins.then_inc(bank_full[turns[name][0]], 1)

            def product(o, sh, sl, mh, ml, first, last):
                nc.tensor.matmul(o, sh, mh, start=first, stop=False)
                nc.tensor.matmul(o, sh, ml, start=False, stop=False)
                return nc.tensor.matmul(o, sl, mh, start=False, stop=last)

            def unit_begin(g):
                pe.wait_ge(lo_up, g + 1)
                if g >= 2:
                    pe.wait_ge(bank_free[4 + g % 2], g // 2)
                return bank[4 + g % 2]

            def unit_cols(g, mh, ml, blocks=(0, P), ready=None):
                o, s, n = unit_begin(g), g % 2, units[g].get("n", UC)
                nkt = units[g].get("nkt", KD)
                for i, c in enumerate(blocks):
                    for kt in range(nkt):
                        if ready and i == 0:
                            pe.wait_ge(*ready(kt))
                        a = slice(kt * n + c, kt * n + c + P)
                        mm = product(o[:, S * i:S * (i + 1)], uh[s][:, a], ul[s][:, a], mh[:, kt, :], ml[:, kt, :],
                                     kt == 0, kt == nkt - 1)
                mm.then_inc(bank_full[4 + s], 1)

            def unit_rows(g, sth, stl, ready=None):
                o, s, n = unit_begin(g), g % 2, units[g].get("n", UC)
                nkt = units[g].get("nkt", KD)
                for tt in range(TT):
                    for kt in range(nkt):
                        if ready and tt == 0:
                            pe.wait_ge(*ready(kt))
                        a, t = slice(kt * n, kt * n + n), slice(P * tt, P * (tt + 1))
                        mm = product(o[:, n * tt:n * (tt + 1)], sth[:, kt, t], stl[:, kt, t], uh[s][:, a], ul[s][:, a],
                                     kt == 0, kt == nkt - 1)
                mm.then_inc(bank_full[4 + s], 1)

            def h_ready(n):
                return lambda kt: (h_lo, 4 * n + kt // 2 + 1)

            def transpose_rows(n, src):
                for q in range(4):
                    o = begin(("ht", n, q))
                    for i in range(2):
                        for tt in range(TT):
                            kt = 2 * q + i
                            mm = nc.tensor.transpose(o[:, S * i + P * tt:S * i + P * (tt + 1)],
                                                     src[:, tt, P * kt:P * (kt + 1)], ident)
                    done(mm, ("ht", n, q))

            def mod_columns(layer, part):
                o = begin(("modc", layer, part))
                pe.wait_ge(ada_acc, 24 * layer + 12 * part + 8)
                for j in range(16):
                    c = 24 * P * part + P * j
                    mm = nc.tensor.matmul(o[:, j:j + 1], accg[:, c:c + P], ones[:, 0:1], start=True, stop=True)
                done(mm, ("modc", layer, part))

            def mod_rows(layer, w):
                pe.wait_ge(ada_acc, 24 * layer + 12 * w + 12)
                for half in range(2):
                    o = begin(("modr", layer, w, half))
                    c = (24 * w + 16) * P + 512 * half
                    mm = nc.tensor.matmul(o[:, :], ones, accg[:, c:c + 512], start=True, stop=True)
                    done(mm, ("modr", layer, w, half))

            def score(a, h):
                o = begin(("score", a, h))
                p0, blk = DH * (h % 2), h // 2
                q, k = qT(ATT_SET[a])[p0:p0 + DH, blk, :], kT(ATT_SET[a])[p0:p0 + DH, blk, :]
                for tt, (c0, n) in enumerate(((0, P), (P, S))):
                    t = slice(P * tt, P * (tt + 1))
                    one = a in (DSA, MOBA)
                    mm = nc.tensor.matmul(o[:, c0:c0 + n], q[:, t], k[:, 0:n], start=True, stop=one)
                    if a == MLA:
                        r0 = D_ROPE * (h % 4)
                        mm = nc.tensor.matmul(o[:, c0:c0 + n], qrT[r0:r0 + D_ROPE, h // 4, t],
                                              krT[r0:r0 + D_ROPE, 0:n], start=False, stop=True,
                                              tile_position=(r0, 0))
                    if a == FOX:
                        mm = nc.tensor.matmul(o[:, c0:c0 + n], ident[0:8, h:h + 1].to_broadcast([8, P]),
                                              f_t[1][:, 0:n], start=False, stop=True)
                done(mm, ("score", a, h))

            def transpose_p(a, h):
                o = begin(("tr", a, h))
                pe.wait_ge(p_ready, att_count(a, h))
                for i in range(3):
                    mm = nc.tensor.transpose(o[:, P * i:P * (i + 1)], L[h % 2][:, P * i:P * (i + 1)], ident)
                done(mm, ("tr", a, h))

            def weighted(a, h, t, set_):
                o = begin(("pv", a, h // 2)) if h % 2 == 0 else bank[turns["pv", a, h // 2][0]]
                p0 = DH * (h % 2)
                v = vv(set_)
                nc.tensor.matmul(o[p0:p0 + DH, 0:S], v[:, 0, DH * h:DH * (h + 1)], t[:, 0:S], start=True, stop=False)
                nc.tensor.matmul(o[p0:p0 + DH, P:S], v[:, 1, DH * h:DH * (h + 1)], t[:, S:S + P],
                                 start=False, stop=True).then_inc(pv_done, 1)

            def attention(a, filler, v_units):
                for st in range(HEADS + 2):
                    if st < HEADS:
                        score(a, st)
                    for g in FILL[a].get(st, []):
                        filler(g)
                    if 1 <= st <= HEADS:
                        transpose_p(a, st - 1)
                    if st >= 2:
                        if st == 2:
                            for g in v_units:
                                unit_evacuated(pe, g)
                        evacuated(pe, ("tr", a, st - 2))
                        weighted(a, st - 2, PT[st % 2], ATT_SET[a])

            def out_split(a):
                for p in (2, 3):
                    evacuated(pe, ("pv", a, p))

            def ffn(f):
                g0, d0, nb = FFN_G0[f], FFN_D0[f], FFN_NB[f]
                n = units[g0].get("n", UC)
                act0 = sum(FFN_NB[:f])

                def up(i, k, ready=None, fixed=False):
                    b, s = 2 * i + k, (g0 + k) % 2
                    pe.wait_ge(lo_up, b + (g0 + 1))
                    pe.wait_ge(bank_free[4 + s], i + (g0 + k) // 2)
                    for j, c in enumerate(range(0, n, P)):
                        for kt in range(KD):
                            if ready and j == 0:
                                pe.wait_ge(*ready(kt))
                            a = slice(kt * n + c, kt * n + c + P)
                            mm = product(bank[4 + s][:, S * j:S * (j + 1)], uh[s][:, a], ul[s][:, a],
                                         hh[:, kt, :], hl[:, kt, :], kt == 0, kt == KD - 1)
                    mm.then_inc(bank_full[4 + s], 1)

                def downward(i, k, first, last):
                    b = 2 * i + k
                    pe.wait_ge(lo_dn, b + (d0 + 1))
                    pe.wait_ge(act_lo, b + (act0 + 1))
                    for tt in range(TT):
                        for half in range(2):
                            if first:
                                begin(("acc", f, 2 * tt + half))
                            t, c = slice(P * tt, P * (tt + 1)), slice(512 * half, 512 * (half + 1))
                            mm = product(bank[2 * tt + half][:, :], acth[k][:, t], actl[k][:, t],
                                         down[:, k, 0, c], down[:, k, 1, c], first, last)
                    mm.then_inc(down_done, 1)

                up(0, 0, ready=h_ready((1, 3, 5)[f]))
                up(0, 1)
                downward(0, 0, True, False)
                with pe.Fori(1, nb // 2) as i:
                    up(i, 0)
                    downward(i - 1, 1, False, False)
                    up(i, 1)
                    downward(i, 0, False, False)
                downward(nb // 2 - 1, 1, False, True)

            pe.wait_ge(stage_in, 16 * 12)
            pe.wait_ge(const_in, 16)
            o = begin("stage")
            for i, n in enumerate((45, P, P, 8)):
                mm = nc.tensor.transpose(o[:, P * i:P * i + n], stage[i][0:n, :], ident[0:n, 0:n])
            done(mm, "stage")
            mod_columns(0, 0)
            pe.wait_ge(x_in, 16)
            transpose_rows(0, x)
            for g in G_QI:
                unit_cols(g, hh, hl, ready=h_ready(0))
            pe.wait_ge(lo_up, G_KI + 1)
            o, s = begin("wi"), G_KI % 2
            for tt in range(TT):
                for kt in range(KD):
                    t, c = slice(P * tt, P * (tt + 1)), slice(192 * kt + 128, 192 * kt + 136)
                    mm = product(o[:, 8 * tt:8 * tt + 8], hh[:, kt, t], hl[:, kt, t], uh[s][:, c], ul[s][:, c],
                                 kt == 0, kt == KD - 1)
            done(mm, "wi")
            unit_cols(G_KI, hh, hl, blocks=(64, 0))
            for g in (G_QI[1], G_KI):
                unit_evacuated(pe, g)
            for h in range(HEADS):
                o = begin(("idx", h))
                p0 = DH * (h % 2)
                for tt, (c0, n) in enumerate(((0, P), (P, S))):
                    mm = nc.tensor.matmul(o[:, c0:c0 + n], qiT[p0:p0 + DH, h // 2, P * tt:P * (tt + 1)],
                                          kiT[p0:p0 + DH, 0:n], start=True, stop=True)
                done(mm, ("idx", h))
                if h % 2 == 0:
                    unit_cols(G_QKV[DSA][h // 2], hh, hl)
            for g in G_QKV[DSA][4:6]:
                unit_rows(g, hh, hl)
            for g in G_CX:
                unit_cols(g, hh, hl)
            for g in G_QKV[DSA][2:4]:
                unit_evacuated(pe, g)
            attention(DSA, lambda g: unit_cols(g, hh, hl), G_QKV[DSA][4:6])
            mod_rows(0, 0)
            out_split(DSA)
            pe.wait_ge(yb_lo, 4)
            for g in G_EO:
                unit_rows(g, yh, yl)
            mod_columns(0, 1)
            mod_rows(0, 1)
            pe.wait_ge(row_ready, 2)
            transpose_rows(1, x)
            ffn(0)
            mod_columns(1, 0)
            mod_columns(1, 1)
            pe.wait_ge(row_ready, 4)
            transpose_rows(2, x)
            for w in range(2):
                mod_rows(1, w)
            for g in G_Z:
                unit_rows(g, hh, hl, ready=h_ready(2))
            for g in G_U:
                unit_cols(g, hh, hl)
            pe.wait_ge(lat_norm, 1)
            for i, (k0, k1) in enumerate(((0, 2), (2, 4), (4, 5))):
                o = begin(f"latT{i}")
                for kt in range(k0, k1):
                    for tt in range(TT):
                        c = S * (kt - k0) + P * tt
                        mm = nc.tensor.transpose(o[:, c:c + P], latn[:, tt, P * kt:P * (kt + 1)], ident)
                done(mm, f"latT{i}")
            pe.wait_ge(lat_lo, 3)
            for g in G_QN:
                unit_cols(g, lat_h[:, 0:3, :], lat_l[:, 0:3, :])
            unit_rows(G_QR, lat_h[:, 0:3, :], lat_l[:, 0:3, :])
            for g in G_KN:
                unit_cols(g, lat_h[:, 3:5, :], lat_l[:, 3:5, :])
            for g in G_VV:
                unit_rows(g, lat_h[:, 3:5, :], lat_l[:, 3:5, :])
            pe.wait_ge(rot_ready, 1)
            o = begin("krT")
            for tt in range(TT):
                mm = nc.tensor.transpose(o[:, P * tt:P * (tt + 1)], krot[:, tt, :], ident)
            done(mm, "krT")
            pe.wait_ge(pool_ready, 1)
            pe.wait_ge(pw_in, 16)
            for i in range(2):
                o = begin(f"pool{i}")
                for j in range(2):
                    mm = nc.tensor.matmul(o[:, S * j:S * (j + 1)], pool_w[:, 2 * i + j, :], pooled[:, 2 * i + j, :],
                                          start=True, stop=True)
                done(mm, f"pool{i}")
            pe.wait_ge(rot_ready, 2)
            o = begin("qrT")
            for blk in range(2):
                for tt in range(TT):
                    c = S * blk + P * tt
                    mm = nc.tensor.transpose(o[:, c:c + P], qrot[:, tt, P * blk:P * (blk + 1)], ident)
            done(mm, "qrT")
            evacuated(pe, "krT")
            evacuated(pe, "qrT")
            for g in G_QN[-1:] + G_KN:
                unit_evacuated(pe, g)
            attention(MLA, None, G_VV)
            out_split(MLA)
            pe.wait_ge(pool_lo, 2)
            for g in G_OO:
                unit_rows(g, yh, yl)
            pe.wait_ge(row_ready, 6)
            transpose_rows(3, x)
            ffn(1)
            pe.wait_ge(row_ready, 10)
            transpose_rows(4, xn)
            for j, g in enumerate(G_QKV[FOX]):
                if j < 4:
                    unit_cols(g, hh, hl, ready=h_ready(4))
                else:
                    unit_rows(g, hh, hl)
            unit_cols(G_F, hh, hl, blocks=(0,))
            pe.wait_ge(c_ready, 1)
            o = begin("ccol")
            for tt in range(TT):
                mm = nc.tensor.transpose(o[:, 8 * tt:8 * tt + 8], f_t[1][:, P * tt:P * (tt + 1)], ident[0:8, 0:8])
            done(mm, "ccol")

            def projection(units_):
                return lambda g: unit_cols(g, hh, hl) if g < units_[4] else unit_rows(g, hh, hl)

            for g in G_QKV[FOX][2:4]:
                unit_evacuated(pe, g)
            attention(FOX, projection(G_QKV[MOBA]), G_QKV[FOX][4:6])
            for g in G_QKV[MOBA][2:4]:
                unit_evacuated(pe, g)
            attention(MOBA, projection(G_QKVS), G_QKV[MOBA][4:6])
            for g in G_QKVS[2:4]:
                unit_evacuated(pe, g)
            for st in range(HEADS + 2):
                if st < HEADS:
                    h = st
                    o = begin(("z", h))
                    p0, blk = DH * (h % 2), h // 2
                    q, k = qT(0)[p0:p0 + DH, blk, :], kT(0)[p0:p0 + DH, blk, :]
                    nc.tensor.matmul(o[:, 0:S], k[:, 0:P], q[:, 0:S], start=True, stop=True)
                    mm = nc.tensor.matmul(o[:, S:S + P], k[:, P:S], q[:, P:S], start=True, stop=True)
                    done(mm, ("z", h))
                for g in FILL["stick"].get(st, []):
                    unit_cols(g, hh, hl)
                if 1 <= st <= HEADS:
                    h = st - 1
                    o, t = begin(("sfx", h)), sp[h % 2]
                    pe.wait_ge(sp_ready, h + 1)
                    nc.tensor.matmul(o[:, 0:S], C("suffix"), t[:, 0:S], start=True, stop=False)
                    nc.tensor.matmul(o[:, P:S], ones, t[:, S:S + P], start=False, stop=True)
                    mm = nc.tensor.matmul(o[:, S:S + P], C("suffix"), t[:, S:S + P], start=True, stop=True)
                    done(mm, ("sfx", h))
                if st >= 2:
                    h = st - 2
                    if h == 0:
                        for g in G_QKVS[4:6]:
                            unit_evacuated(pe, g)
                    pe.wait_ge(w_ready, h + 1)
                    weighted("stick", h, wT[h % 2], 0)
            for g in G_GATE[10:]:
                unit_cols(g, hh, hl)
            out_split("stick")
            for c in range(4):
                for n in range(3):
                    unit_cols(G_LIFT[c, n], o_h[n], o_l[n])
            for g in G_WO:
                unit_rows(g, hh, hl, ready=lambda kt: (mix_lo, kt // 2 + 1))
            pe.wait_ge(row_ready, 12)
            transpose_rows(5, xn)
            ffn(2)

        @block.vector
        def _(dve):
            link = Chain(dve, dve_chain)
            V = nc.vector

            def modulation_unit(a):
                j, s = a % 24, a % 2
                dve.wait_ge(ada_in[s], 32 * (a // 2 + 1))
                modulation_part(accg[:, UC * j:UC * (j + 1)], accg[0:1, UC * j:UC * (j + 1)], s, 0, KD)

            def modulation_part(acc, acc0, s, k0, k1):
                for kt in range(k0, k1):
                    w = ada[s][:, UC * kt:UC * (kt + 1)]
                    if kt == 0:
                        link(V.tensor_scalar(acc, w, cond[:, 0:1], None, ALU.mult))
                    else:
                        link(V.scalar_tensor_tensor(acc, w, cond[:, kt:kt + 1], acc, ALU.mult, ALU.add))
                if k1 == KD:
                    V.tensor_tensor(acc0, acc0, ada[s][0:1, CHUNKW:CHUNKW + UC], ALU.add).then_inc(ada_acc, 1)

            def mod_columns(layer, part):
                o, j0, name = full(dve, ("modc", layer, part)), 24 * part, ("modc", layer, part)
                link(V.tensor_scalar(modT[:, layer, j0 + 8:j0 + 16], o[:, 8:16], 1.0, None, ALU.add))
                V.tensor_copy(modT[:, layer, j0:j0 + 8], o[:, 0:8]).then_inc(free(name), 1)
                evacuated(dve, name)

            def mod_rows(layer, w):
                for half in range(2):
                    name = ("modr", layer, w, half)
                    o = full(dve, name)
                    V.tensor_scalar(grow[:, w, 512 * half:512 * (half + 1)], o[:, :], 1.0, None, ALU.add
                                    ).then_inc(free(name), 1)
                    evacuated(dve, name)

            def h_columns(n, scale, shift):
                for q in range(4):
                    o = full(dve, ("ht", n, q))
                    if q >= 2:
                        dve.wait_ge(h_lo, 4 * n + q - 1)
                    for i in range(2):
                        kt, dst = 2 * q + i, hf[:, 512 * (q % 2) + S * i:512 * (q % 2) + S * (i + 1)]
                        if shift is None:
                            ins = V.tensor_scalar(dst, o[:, S * i:S * (i + 1)], scale[:, kt:kt + 1], None, ALU.mult)
                        else:
                            ins = V.tensor_scalar(dst, o[:, S * i:S * (i + 1)], scale[:, kt:kt + 1], shift[:, kt:kt + 1],
                                                  ALU.mult, ALU.add)
                        if i == 0:
                            link(ins)
                    ins.then_inc(free(("ht", n, q)), 1)

            def statistics():
                for tt in range(TT):
                    for half in range(2):
                        link(V.bn_stats(bnst[:, tt, 6 * half:6 * half + 6], x[:, tt, 512 * half:512 * (half + 1)]))
                    link(V.bn_aggr(mv[:, tt, :], bnst[:, tt, :]))

            def layer_norm(n, rows):
                statistics()
                V.tensor_scalar(var[:, 0:2], mv[:, :, 1], LN_EPS, None, ALU.add).then_inc(var_ready, 1)
                dve.wait_ge(rstd_ready, n + 1)
                for tt in range(TT):
                    link(V.tensor_scalar(x[:, tt, :], x[:, tt, :], mv[:, tt, 0:1], rstd[:, tt:tt + 1],
                                         ALU.subtract, ALU.mult))
                    if tt == 0:
                        dve.wait_ge(ln_in, 32 * (rows + 1))
                    link(V.tensor_tensor(x[:, tt, :], x[:, tt, :], lnrow[:, 0, :], ALU.mult))
                    V.tensor_tensor(x[:, tt, :], x[:, tt, :], lnrow[:, 1, :], ALU.add).then_inc(row_ready, 1)
                dve.wait_ge(row_ready, 2 * (rows + 1))

            def rms_scale(n):
                statistics()
                link(V.tensor_tensor(var[:, 2:4], mv[:, :, 0], mv[:, :, 0], ALU.mult))
                link(V.tensor_tensor(var[:, 2:4], var[:, 2:4], mv[:, :, 1], ALU.add))
                V.tensor_scalar(var[:, 0:2], var[:, 2:4], RMS_EPS, None, ALU.add).then_inc(var_ready, 1)
                dve.wait_ge(rstd_ready, n + 1)

            def rms_rows(n):
                rms_scale(n)
                for tt in range(TT):
                    V.tensor_scalar(xn[:, tt, :], x[:, tt, :], rstd[:, tt:tt + 1], None, ALU.mult).then_inc(row_ready, 1)

            def soft(a, h):
                o, t = full(dve, ("score", a, h)), L[h % 2]
                if h >= 2:
                    full(dve, ("tr", a, h - 2))
                for tt, (c0, n) in enumerate(((0, P), (P, S))):
                    def table(name):
                        return C(name)[:, P:S] if tt == 0 else C(name)
                    d, ps = t[:, c0:c0 + n], o[:, c0:c0 + n]
                    if a == DSA:
                        ins = V.scalar_tensor_tensor(d, distm[:, c0:c0 + n], -SLOPES[h] / SCALE, ps, ALU.mult, ALU.add)
                    elif a == MOBA:
                        ins = V.scalar_tensor_tensor(d, table("dist_causal"), -SLOPES[h] / SCALE, ps, ALU.mult, ALU.add)
                    elif a == FOX:
                        ins = V.scalar_tensor_tensor(d, ps, ccol[:, tt, h:h + 1], table("causal"), ALU.add, ALU.add)
                    else:
                        ins = V.tensor_tensor(d, ps, table("chunk"), ALU.add)
                    if tt == 0:
                        link(ins)
                    else:
                        ins.then_inc(free(("score", a, h)), 1)
                evacuated(dve, ("score", a, h))
                link(V.tensor_reduce(smax[:, h, 0:1], t[:, 0:P], AX.X, ALU.max))
                link(V.tensor_reduce(smax[:, h, 1:2], t[:, P:P + S], AX.X, ALU.max))
                V.tensor_scalar(sbias[:, h, :], smax[:, h, :], -(SCALE_MLA if a == MLA else SCALE), None, ALU.mult
                                ).then_inc(max_ready, 1)

            def normalize(a, h):
                t = L[h % 2]
                dve.wait_ge(exp_done, att_count(a, h))
                link(V.reciprocal(srec[:, h, :], ssum[:, h, :]))
                V.tensor_scalar(t[:, 0:P], t[:, 0:P], srec[:, h, 0:1], None, ALU.mult)
                V.tensor_scalar(t[:, P:P + S], t[:, P:P + S], srec[:, h, 1:2], None, ALU.mult).then_inc(p_ready, 1)

            def out_low(a, p):
                dve.wait_ge(o_hi, 4 * ATT_N[a] + p + 1)
                hi, lo = ATT_OUT[a]
                V.tensor_tensor(lo[:, p, :], bank[turns["pv", a, p][0]][:, 0:S], hi[:, p, :].bitcast(F32), ALU.subtract
                                ).then_inc(free(("pv", a, p)), 1)

            def attention(a, between=None):
                for st in range(HEADS + 2):
                    if st < HEADS:
                        soft(a, st)
                    if 1 <= st <= HEADS:
                        normalize(a, st - 1)
                    if between:
                        between(st)
                    if st >= 2 and st % 2 == 1:
                        out_low(a, (st - 2) // 2)

            def mixer_residual(gs, gated):
                for j, g in enumerate(gs):
                    o = unit_full(dve, g)[:, :].rearrange("p (t n) -> p t n", t=TT)
                    c = slice(UC * j, UC * (j + 1))
                    if gated:
                        t = tmp.rearrange("p (t n) -> p t n", t=TT)
                        V.tensor_tensor(t, o, grow[:, 0, c].unsqueeze(1).to_broadcast([P, TT, UC]), ALU.mult
                                        ).then_inc(unit_free(g), 1)
                        unit_evacuated(dve, g)
                        link(V.scalar_tensor_tensor(x[:, :, c], x[:, :, c], ALPHA, t, ALU.mult, ALU.add))
                    else:
                        V.tensor_tensor(x[:, :, c], x[:, :, c], o, ALU.add).then_inc(unit_free(g), 1)
                        unit_evacuated(dve, g)

            def ffn(f):
                g0, d0, nb = FFN_G0[f], FFN_D0[f], FFN_NB[f]
                half = units[g0]["kind"] == "pair"
                act0 = sum(FFN_NB[:f])

                def body(i, k):
                    b, s = 2 * i + k, (g0 + k) % 2
                    if half:
                        dve.wait_ge(tap_done, b + (act0 + 1))
                        for j, t in enumerate((fv[k], fg[k])):
                            for back in (1, 2):
                                w = conv_w[f][:, bass.ds(b + ((2 - back) * 44 + 22 * j), 1)]
                                ins = V.scalar_tensor_tensor(t[:, back:S], bank[4 + s][:, S * j:S * (j + 1) - back], w,
                                                             t[:, back:S], ALU.mult, ALU.add)
                                if (j, back) == (1, 2):
                                    ins.then_inc(bank_free[4 + s], 1)
                                else:
                                    link(ins)
                        if f == 0:
                            dve.wait_ge(ada_in[k], i * 32 + 32 * 13)
                            acc, acc0 = accg[:, bass.ds(b * UC, UC)], accg[0:1, bass.ds(b * UC, UC)]
                            modulation_part(acc, acc0, k, 0, 4)
                        dve.wait_ge(silu_done, b + (act0 + 1))
                        V.tensor_tensor(fv[k], fv[k], fg[k], ALU.mult).then_inc(prod_done, 1)
                        if f == 0:
                            modulation_part(acc, acc0, k, 4, KD)
                    else:
                        dve.wait_ge(bank_free[4 + s], i + ((g0 + k) // 2 + 1))
                        V.tensor_tensor(fv[k], fv[k], fv[k], ALU.mult).then_inc(prod_done, 1)
                    dve.wait_ge(act_hi, b + (act0 + 1))
                    V.tensor_tensor(actl[k], fv[k], acth[k].bitcast(F32), ALU.subtract).then_inc(act_lo, 1)

                per = 2 * (11, 3, 0)[f]
                for k in range(2):
                    body(0, k)
                with dve.Fori(1, nb // 2) as i:
                    link.enter(i, 1, per)
                    for k in range(2):
                        body(i, k)
                link.leave(nb // 2 - 1, per)
                dve.wait_ge(down_done, d0 + nb)
                for tt in range(TT):
                    for hf_ in range(2):
                        c, name = slice(512 * hf_, 512 * (hf_ + 1)), ("acc", f, 2 * tt + hf_)
                        o = bank[2 * tt + hf_]
                        if f < 2:
                            V.tensor_tensor(tmp, o[:, :], grow[:, 1, c], ALU.mult).then_inc(free(name), 1)
                            evacuated(dve, name)
                            link(V.scalar_tensor_tensor(x[:, tt, c], x[:, tt, c], ALPHA, tmp, ALU.mult, ALU.add))
                        else:
                            V.tensor_tensor(x[:, tt, c], x[:, tt, c], o[:, :], ALU.add).then_inc(free(name), 1)
                            evacuated(dve, name)

            o = full(dve, "stage")
            link(V.tensor_copy(cols[:, 0:45], o[:, 0:45]))
            link(V.tensor_copy(conv_w[0][:, 0:P], o[:, P:2 * P]))
            link(V.tensor_copy(conv_w[1][:, 0:P], o[:, 2 * P:3 * P]))
            link(V.tensor_copy(conv_w[0][:, P:132], o[:, 3 * P:3 * P + 4]))
            V.tensor_copy(conv_w[1][:, P:132], o[:, 3 * P + 4:3 * P + 8]).then_inc(free("stage"), 1)
            dve.wait_ge(cond_exp, 1)
            link(V.tensor_scalar(cexp, cexp, 1.0, None, ALU.add))
            link(V.reciprocal(cexp, cexp))
            link(V.tensor_tensor(cond, c_col, cexp, ALU.mult))
            for a in range(8):
                modulation_unit(a)
            mod_columns(0, 0)
            h_columns(0, modT[:, 0, 8:16], modT[:, 0, 0:8])
            evacuated(dve, "wi")
            for h in range(HEADS):
                evacuated(dve, ("idx", h))
                r = rel[h % 2]
                if h:
                    dve.wait_ge(idx_acc, h)
                for tt, (c0, n) in enumerate(((0, P), (P, S))):
                    w, d, t = wi[:, 8 * tt + h:8 * tt + h + 1], idx[:, c0:c0 + n], r[:, c0:c0 + n]
                    if h == 0:
                        ins = V.tensor_scalar(d, t, w, None, ALU.mult)
                    else:
                        ins = V.scalar_tensor_tensor(d, t, w, d, ALU.mult, ALU.add)
                ins.then_inc(idx_acc, 1)
                for a in ADA_IDX.get(h, []):
                    modulation_unit(a)
            dve.wait_ge(idx_acc, HEADS)
            for tt, (c0, n) in enumerate(((0, P), (P, S))):
                d = idx[:, c0:c0 + n]
                link(V.tensor_tensor(d, d, C("chunk")[:, P:S] if tt == 0 else C("chunk"), ALU.add))
                for _ in range(TOPK // 8):
                    link(V.max(top8, d))
                    link(V.match_replace(d, top8, d, REMOVED))
                m = distm[:, c0:c0 + n]
                link(V.tensor_scalar(m, d, REMOVED / 1.5, BIG, ALU.is_gt, ALU.mult))
                link(V.tensor_tensor(m, m, C("dist_chunk")[:, P:S] if tt == 0 else C("dist_chunk"), ALU.add))
            for b, g in enumerate(G_CX):
                o = unit_full(dve, g)
                dve.wait_ge(cg_ready, b + 1)
                p_ = cgx[b % 2]
                V.tensor_tensor(p_, o[:, S:2 * S], cgb[b % 2], ALU.mult).then_inc(unit_free(g), 1)
                unit_evacuated(dve, g)
                link(V.tensor_scalar(ybc[:, b, :], p_, ev_conv[:, 8 + b:9 + b], None, ALU.mult))
                for back in (1, 2):
                    w = ev_conv[:, 4 * (2 - back) + b:4 * (2 - back) + b + 1]
                    link(V.scalar_tensor_tensor(ybc[:, b, back:S], p_[:, 0:S - back], w, ybc[:, b, back:S],
                                                ALU.mult, ALU.add))

            def dsa_between(st):
                for g in FILL[DSA].get(st, []):
                    i = g - G_BG[0]
                    o = unit_full(dve, g)
                    V.tensor_tensor(ybc[:, 2 * i:2 * i + 2, :], o[:, :].rearrange("p (k t) -> p k t", k=2),
                                    ybc[:, 2 * i:2 * i + 2, :], ALU.mult).then_inc(unit_free(g), 1)
                for a in ADA_ATT[st]:
                    modulation_unit(a)

            attention(DSA, dsa_between)
            mod_rows(0, 0)
            for p in range(4):
                dve.wait_ge(yb_hi, p + 1)
                V.tensor_tensor(yl[:, 4 + p, :], ybc[:, p, :], yh[:, 4 + p, :].bitcast(F32), ALU.subtract).then_inc(yb_lo, 1)
            for a in ADA_LATE:
                modulation_unit(a)
            dve.wait_ge(x_in, 16)
            mixer_residual(G_EO, True)
            mod_columns(0, 1)
            mod_rows(0, 1)
            layer_norm(0, 0)
            h_columns(1, modT[:, 0, 32:40], modT[:, 0, 24:32])
            ffn(0)
            for a in (46, 47):
                modulation_unit(a)
            layer_norm(1, 1)
            mod_columns(1, 0)
            mod_columns(1, 1)
            h_columns(2, modT[:, 1, 8:16], modT[:, 1, 0:8])
            for w in range(2):
                mod_rows(1, w)
            dve.wait_ge(lat_sq, 4)
            link(V.tensor_scalar(var[:, 0:2], sqs[:, 0:2], 1.0 / Q_LORA, RMS_EPS, ALU.mult, ALU.add))
            V.tensor_scalar(var[:, 2:4], sqs[:, 2:4], 1.0 / KV_LORA, RMS_EPS, ALU.mult, ALU.add).then_inc(var_ready, 1)
            dve.wait_ge(rstd_ready, 3)
            for tt in range(TT):
                V.tensor_scalar(latn[:, tt, 0:Q_LORA], zrow[:, tt, 0:Q_LORA], rstd[:, tt:tt + 1], None, ALU.mult)
                ins = V.tensor_scalar(latn[:, tt, Q_LORA:640], zrow[:, tt, Q_LORA:640], rstd[:, 2 + tt:3 + tt], None, ALU.mult)
            ins.then_inc(lat_norm, 1)

            def lat_columns(i, k0, k1):
                o = full(dve, f"latT{i}")
                for kt in range(k0, k1):
                    gain = q_gain[:, kt:kt + 1] if kt < 3 else kv_gain[:, kt - 3:kt - 2]
                    c = S * (kt - k0)
                    ins = V.tensor_scalar(lat_f[:, 512 * (i % 2) + c:512 * (i % 2) + c + S], o[:, c:c + S], gain, None, ALU.mult)
                    if kt < k1 - 1:
                        link(ins)
                ins.then_inc(free(f"latT{i}"), 1)

            def lat_low(i, k0, k1):
                dve.wait_ge(lat_hi, i + 1)
                n = k1 - k0
                V.tensor_tensor(lat_l[:, k0:k1, :], lat_f[:, 512 * (i % 2):512 * (i % 2) + S * n]
                                .rearrange("p (k t) -> p k t", k=n), lat_h[:, k0:k1, :].bitcast(F32), ALU.subtract
                                ).then_inc(lat_lo, 1)

            lat_columns(0, 0, 2)
            lat_columns(1, 2, 4)
            lat_low(0, 0, 2)
            dve.wait_ge(lat_lo, 1)
            lat_columns(2, 4, 5)
            lat_low(1, 2, 4)
            lat_low(2, 4, 5)

            def rotate(src, dst, heads, tt):
                cos, sin = (C("rope")[:, 32 * tt + 16 * i:32 * tt + 16 * i + 16].unsqueeze(1).to_broadcast([P, heads, 16])
                            for i in range(2))
                x1, x2 = src[:, :, 0:16], src[:, :, 16:32]
                a, b = (r[:, 0:heads * 16].rearrange("p (h c) -> p h c", h=heads) for r in rt)
                link(V.tensor_tensor(a, x1, cos, ALU.mult))
                link(V.tensor_tensor(b, x2, sin, ALU.mult))
                link(V.tensor_tensor(dst[:, :, 0:16], a, b, ALU.subtract))
                link(V.tensor_tensor(a, x2, cos, ALU.mult))
                link(V.tensor_tensor(b, x1, sin, ALU.mult))
                return V.tensor_tensor(dst[:, :, 16:32], a, b, ALU.add)

            for tt in range(TT):
                ins = rotate(zrow[:, tt, 640:672].unsqueeze(1).to_broadcast([P, 4, D_ROPE]),
                             krot[:, tt, :].rearrange("p (h c) -> p h c", h=4), 4, tt)
                if tt == 0:
                    link(ins)
            ins.then_inc(rot_ready, 1)
            dve.wait_ge(rot_ready, 1)
            for g in G_U:
                unit_evacuated(dve, g)
            for gi, win in enumerate(WINDOWS):
                src, w, n = upad[:, gi, :], 1, 0
                while w < win:
                    dst = pp[n % 2]
                    link(V.tensor_tensor(dst[:, PAD:PAD + S], src[:, PAD:PAD + S], src[:, PAD - w:PAD + S - w], ALU.add))
                    src, w, n = dst, 2 * w, n + 1
                u = upad[:, gi, :]
                link(V.scalar_tensor_tensor(pooled[:, gi, PAD:S], src[:, 2 * PAD:PAD + S], 1.0 / win, u[:, 2 * PAD:PAD + S],
                                            ALU.mult, ALU.subtract))
                link(V.tensor_tensor(pooled[:, gi, 0:PAD], src[:, PAD:2 * PAD], C("rcount")[:, PAD * gi:PAD * (gi + 1)], ALU.mult))
                ins = V.tensor_tensor(pooled[:, gi, 0:PAD], pooled[:, gi, 0:PAD], u[:, PAD:2 * PAD], ALU.subtract)
                if gi < 3:
                    link(ins)
            ins.then_inc(pool_ready, 1)
            unit_evacuated(dve, G_QR)
            for tt in range(TT):
                ins = rotate(qrow[:, tt, :].rearrange("p (h c) -> p h c", h=HEADS),
                             qrot[:, tt, :].rearrange("p (h c) -> p h c", h=HEADS), HEADS, tt)
                if tt == 0:
                    link(ins)
            ins.then_inc(rot_ready, 1)
            dve.wait_ge(lat_lo, 3)
            for i in range(2):
                o = full(dve, f"pool{i}")
                for j in range(2):
                    ins = V.tensor_scalar(lat_f[:, 512 * i + S * j:512 * i + S * (j + 1)], o[:, S * j:S * (j + 1)],
                                          pool_scale[:, 2 * i + j:2 * i + j + 1], None, ALU.mult)
                    if j == 0:
                        link(ins)
                ins.then_inc(free(f"pool{i}"), 1)
            for i in range(2):
                dve.wait_ge(pool_hi, i + 1)
                V.tensor_tensor(yl[:, 2 * i:2 * i + 2, :], lat_f[:, 512 * i:512 * i + 512].rearrange("p (k t) -> p k t", k=2),
                                yh[:, 2 * i:2 * i + 2, :].bitcast(F32), ALU.subtract).then_inc(pool_lo, 1)
            attention(MLA)
            mixer_residual(G_OO, True)
            layer_norm(3, 2)
            h_columns(3, modT[:, 1, 32:40], modT[:, 1, 24:32])
            ffn(1)
            layer_norm(4, 3)
            rms_rows(5)
            h_columns(4, mix_gain, None)
            o = unit_full(dve, G_F)
            dve.wait_ge(stage_in, 16 * 12)
            V.tensor_scalar(f_t[0], o[0:8, 0:S], bfor, None, ALU.add).then_inc(unit_free(G_F), 1)
            dve.wait_ge(f_log, 1)
            link(V.scalar_tensor_tensor(f_t[2], f_t[0], 0.0, f_t[1], ALU.min, ALU.subtract))
            link(V.tensor_tensor_scan(f_t[3], ones[0:8, 0:1].to_broadcast([8, S]), f_t[2], 0.0, ALU.mult, ALU.add))
            V.tensor_scalar(f_t[1], f_t[3], -1.0 / SCALE, None, ALU.mult).then_inc(c_ready, 1)
            o = full(dve, "ccol")
            V.tensor_scalar(ccol, o[:, 0:16].rearrange("p (t h) -> p t h", t=TT), -1.0, None, ALU.mult).then_inc(free("ccol"), 1)
            evacuated(dve, "ccol")
            attention(FOX)
            attention(MOBA)
            for st in range(HEADS + 2):
                if st < HEADS:
                    h = st
                    o = full(dve, ("z", h))
                    if h >= 2:
                        evacuated(dve, ("sfx", h - 2))
                    V.scalar_tensor_tensor(zm[h % 2], o[:, 0:384], SCALE, C("past_T"), ALU.mult, ALU.add
                                           ).then_inc(free(("z", h)), 1)
                    dve.wait_ge(soft_log, h + 1)
                    if h >= 2:
                        full(dve, ("sfx", h - 2))
                    V.scalar_tensor_tensor(sp[h % 2], zm[h % 2], 0.0, sig[h % 2], ALU.max, ALU.add).then_inc(sp_ready, 1)
                if 1 <= st <= HEADS:
                    h = st - 1
                    o = full(dve, ("sfx", h))
                    if h >= 2:
                        dve.wait_ge(pv_done, att_count("stick", h) - 2)
                    V.tensor_tensor(wT[h % 2], zm[h % 2], o[:, 0:384], ALU.subtract).then_inc(free(("sfx", h)), 1)
                if st >= 2 and st % 2 == 1:
                    out_low("stick", (st - 2) // 2)
            for c in range(4):
                m = mixed[:, 2 * c:2 * c + 2, :]
                for n in range(3):
                    g = G_LIFT[c, n]
                    o = unit_full(dve, g)[:, :].rearrange("p (k t) -> p k t", k=2)
                    dve.wait_ge(gate_ready, 3 * c + n + 1)
                    gate = gates[:, 8 * n + 2 * c:8 * n + 2 * c + 2, :]
                    t = m if n == 0 else tmp.rearrange("p (k t) -> p k t", k=2)
                    V.tensor_tensor(t, o, gate, ALU.mult).then_inc(unit_free(g), 1)
                    unit_evacuated(dve, g)
                    if n == 1:
                        link(V.tensor_tensor(m, m, t, ALU.add))
                    if n == 2:
                        V.tensor_tensor(m, m, t, ALU.add).then_inc(mix_ready, 1)
                dve.wait_ge(mix_hi, c + 1)
                V.tensor_tensor(hl[:, 2 * c:2 * c + 2, :], m, hh[:, 2 * c:2 * c + 2, :].bitcast(F32), ALU.subtract
                                ).then_inc(mix_lo, 1)
            mixer_residual(G_WO, False)
            rms_rows(6)
            h_columns(5, mlp_gain, None)
            ffn(2)
            rms_scale(7)
            dve.wait_ge(ln_in, 32 * 4 + 16)
            for tt in range(TT):
                link(V.tensor_scalar(xn[:, tt, :], x[:, tt, :], rstd[:, tt:tt + 1], None, ALU.mult))
                V.tensor_tensor(xn[:, tt, :], xn[:, tt, :], lnrow[:, 0, :], ALU.mult).then_inc(row_ready, 1)


_INS = ["x", "c", "ada_w", "ada_b", "ln_mix_g", "ln_mix_b", "ln_ffn_g", "ln_ffn_b", "ev_w_in", "ev_conv_w", "ev_w_out",
        "od_w_in", "pool_w", "pool_scale", "q_norm_g", "w_uq", "kv_norm_g", "w_ukv", "od_w_out", "ffn_w_up", "ffn_conv_w",
        "ffn_w_down", "norm_mix_2", "w_in_2", "b_forget_2", "w_branch_2", "w_out_2", "norm_mlp_2", "w_up_2", "w_down_2",
        "norm_final_2"]


def kernel(**inputs):
    import concourse.bacc as bacc
    from concourse.bass_utils import run_bass_kernel_spmd

    nc = bacc.Bacc("TRN2", target_bir_lowering=False, num_devices=1)
    arrays, aps = {}, {}
    for name in _INS:
        a = np.ascontiguousarray(inputs[name])
        arrays[f"in_{name}"] = a
        aps[name] = nc.dram_tensor(f"in_{name}", a.shape, mybir.dt.from_np(a.dtype), kind="ExternalInput").ap()
    arrays["shape_constants"] = shape_constants()
    consts = nc.dram_tensor("shape_constants", (P, N_CONST), F32, kind="ExternalInput").ap()
    out = nc.dram_tensor("out_0", (1, S, D), F32, kind="ExternalOutput").ap()
    build(nc, aps, consts, out)
    r = run_bass_kernel_spmd(nc, [arrays], core_ids=[0])
    return r.results[0]["out_0"]
```

```python
from contextlib import ExitStack

import numpy as np
import concourse.bass as bass
from concourse import mybir

ALU = mybir.AluOpType
ACT = mybir.ActivationFunctionType
AX = mybir.AxisListType
F32 = mybir.dt.float32
F32R = mybir.dt.float32r

P = 128
S = 256
TT = S // P
D = 1024
KD = D // P
DH = 64
HEADS = 8
CHUNK = 64
TOPK = S // 4
D_FF = 2816
NB_FF = D_FF // P
D_FF2 = 4096
NB_FF2 = D_FF2 // P
Q_LORA = 384
KV_LORA = 256
D_ROPE = 32
ODD_IN = 512 + Q_LORA + KV_LORA + D_ROPE
WINDOWS = (2, 4, 8, 16)
PAD = 16
ALPHA = 4 ** 0.25
LN_EPS = 1e-5
RMS_EPS = 1e-6
SCALE = DH ** -0.5
SCALE_MLA = (64 + D_ROPE) ** -0.5
IDX_SCALE = HEADS ** -0.5 * DH ** -0.5
SLOPES = [2.0 ** (-8.0 * (h + 1) / HEADS) for h in range(HEADS)]
NEG = -1e30
BIG = 1e34
REMOVED = -3e38
UC = 256
CHUNKW = KD * UC
AC = 512
MOD_BLOCKS = 6 * D // AC

CONST_AT = {}


def shape_constants():
    t = np.arange(P)[:, None]
    s = np.arange(P)[None, :]
    zero = np.zeros((P, P), np.float32)
    causal = np.where(s <= t, 0.0, NEG)
    chunk = np.where(s // CHUNK <= t // CHUNK, 0.0, NEG)
    inv = 10000.0 ** (-np.arange(0, D_ROPE, 2, dtype=np.float32) / D_ROPE)
    ang = (np.arange(S, dtype=np.float32)[:, None] * inv[None, :].astype(np.float32)).astype(np.float32)
    cs = np.stack([np.cos(ang), np.sin(ang)], 1).reshape(TT, P, 2 * D_ROPE // 2).transpose(1, 0, 2).reshape(P, -1)
    count = np.stack([np.minimum(np.arange(PAD) + 1, w) for w in WINDOWS]).astype(np.float32)
    parts = {
        "ident": np.eye(P),
        "ones": np.ones((P, P)),
        "suffix": (t >= s).astype(np.float32),
        "past_T": np.concatenate([np.where(t < s, 0.0, NEG), zero, np.where(t < s, 0.0, NEG)], 1),
        "causal": np.concatenate([zero, causal], 1),
        "chunk": np.concatenate([zero, chunk], 1),
        "dist_chunk": np.concatenate([t - s + P, np.abs(t - s) - BIG * (chunk < 0) * -1.0], 1),
        "dist_causal": np.concatenate([t - s + P, np.where(s <= t, t - s, BIG)], 1),
        "rope": cs,
        "rcount": np.broadcast_to((1.0 / count).reshape(1, -1), (P, PAD * len(WINDOWS))),
    }
    at = 0
    cols = []
    for name, a in parts.items():
        CONST_AT[name] = (at, at + a.shape[1])
        at += a.shape[1]
        cols.append(a.astype(np.float32))
    return np.ascontiguousarray(np.concatenate(cols, 1))


N_CONST = shape_constants().shape[1]

DSA, MLA, FOX, MOBA = range(4)
ATT_SET = {DSA: 0, MLA: 0, FOX: 0, MOBA: 1}


def build(nc, W, consts, out):
    units = []

    def unit(name, src, c0, n, nkt):
        units.append(dict(name=name, width=nkt * n, n=n, nkt=nkt, src=src, c0=c0, kind="cols"))
        return len(units) - 1

    ev_in, od_in, w2in = W["ev_w_in"][0], W["od_w_in"][0], W["w_in_2"][0]
    G_QI = [unit("qi", ev_in, 1536 + UC * j, UC, KD) for j in range(2)]
    G_KI = unit("ki", ev_in, 1984, 192, KD)
    G_QKV = {DSA: [unit("qkv", ev_in, UC * j, UC, KD) for j in range(6)]}
    G_CX = []
    for b in range(4):
        G_CX.append(len(units))
        units.append(dict(name="cx", width=CHUNKW, src=ev_in, c0=(2632 + P * b, 3144 + P * b), kind="pair"))
    G_BG = [unit("bg", ev_in, 2120 + UC * j, UC, KD) for j in range(2)]
    G_EO = [unit("ev_out", W["ev_w_out"][0], UC * j, UC, KD) for j in range(4)]

    def ffn_units(f, w_up, nb, half):
        g0 = len(units)
        for b in range(nb):
            if half:
                units.append(dict(name="ffn", width=CHUNKW, src=w_up, c0=(P * b, half + P * b), kind="pair"))
            else:
                units.append(dict(name="ffn2", width=KD * P, n=P, nkt=KD, src=w_up, c0=P * b, kind="cols"))
        return g0

    FFN_G0 = [ffn_units(0, W["ffn_w_up"][0], NB_FF, D_FF)]
    G_Z = [unit("z", od_in, 512, 256, KD), unit("z", od_in, 768, 256, KD), unit("z", od_in, 1024, 160, KD)]
    G_U = [unit("u", od_in, UC * j, UC, KD) for j in range(2)]
    uq = W["w_uq"][0].rearrange("k (h c) -> k h c", h=HEADS)
    ukv = W["w_ukv"][0].rearrange("k (h c) -> k h c", h=HEADS)

    def head_unit(name, src, h0, nh, c0, nc_, nkt):
        units.append(dict(name=name, width=nkt * nh * nc_, n=nh * nc_, nh=nh, hc=nc_, h0=h0, c0=c0, nkt=nkt,
                          src=src, kind="heads"))
        return len(units) - 1

    G_QN = [head_unit("qn", uq, 4 * j, 4, 0, 64, 3) for j in range(2)]
    G_QR = head_unit("qr", uq, 0, 8, 64, 32, 3)
    G_KN = [head_unit("kn", ukv, 4 * j, 4, 0, 64, 2) for j in range(2)]
    G_VV = [head_unit("vv", ukv, 4 * j, 4, 64, 64, 2) for j in range(2)]
    G_OO = [unit("od_out", W["od_w_out"][0], UC * j, UC, KD) for j in range(4)]
    FFN_G0.append(ffn_units(1, W["ffn_w_up"][1], NB_FF, D_FF))
    G_F = unit("f", w2in, 3072, P, KD)
    G_QKV[FOX] = [unit("qkv", w2in, 1536 + UC * j, UC, KD) for j in range(6)]
    G_QKV[MOBA] = [unit("qkv", w2in, 3080 + UC * j, UC, KD) for j in range(6)]
    G_QKVS = [unit("qkv", w2in, UC * j, UC, KD) for j in range(6)]
    G_GATE = [unit("gate", w2in, 4616 + UC * j, UC, KD) for j in range(12)]
    G_LIFT = {}
    BRANCHES = (1, 2, 0)
    for c in range(4):
        for n in BRANCHES:
            G_LIFT[c, n] = unit("lift", W["w_branch_2"][0, n], UC * c, UC, 4)
    G_WO = [unit("out2", W["w_out_2"][0], UC * j, UC, KD) for j in range(4)]
    FFN_G0.append(ffn_units(2, W["w_up_2"][0], NB_FF2, 0))
    NU = len(units)
    FFN_NB = [NB_FF, NB_FF, NB_FF2]
    FFN_D0 = [0, NB_FF, 2 * NB_FF]
    FFN_DOWN = [W["ffn_w_down"][0], W["ffn_w_down"][1], W["w_down_2"][0]]

    turns = {}
    used, filled = [0] * 8, [0] * 8

    def turn(name, bank):
        filled[bank] += name[0] != "pv" and not (name[0] == "acc" and name[2] == 3)
        turns[name] = (bank, used[bank], filled[bank])
        used[bank] += 1

    def att_turns(a):
        for h in range(HEADS):
            turn(("score", a, h), h % 3)
            turn(("tr", a, h), h % 3)
            if h % 2 == 0:
                turn(("pv", a, h // 2), 6 + h // 2 % 2)

    turn("cond", 6)
    turn("stage", 6)
    turn(("modc", 0, 0), 7)

    def ht_turns(n):
        for q in range(4):
            turn(("ht", n, q), q)

    def ffn_turns(f):
        for i in range(4):
            turn(("acc", f, i), i)

    ht_turns(0)
    for h in range(HEADS):
        turn(("idx", h), h % 3)
    turn("wi", 6)
    att_turns(DSA)
    for half in range(2):
        turn(("modr", 0, 0, half), half)
    turn(("modc", 0, 1), 7)
    for half in range(2):
        turn(("modr", 0, 1, half), 6 + half)
    ht_turns(1)
    ffn_turns(0)
    turn(("modc", 1, 0), 6)
    ht_turns(2)
    for w in range(2):
        for half in range(2):
            turn(("modr", 1, w, half), 2 * w + half)
    turn("latT0", 0)
    turn("latT1", 1)
    turn("latT2", 6)
    turn("pool0", 2)
    turn("pool1", 3)
    turn("qrT", 7)
    turn("krT", 6)
    att_turns(MLA)
    ht_turns(3)
    ffn_turns(1)
    ht_turns(4)
    turn("ccol", 6)
    att_turns(FOX)
    att_turns(MOBA)
    for st in range(HEADS + 2):
        if st < HEADS:
            turn(("z", st), st % 2)
        if 1 <= st <= HEADS:
            turn(("sfx", st - 1), 2 + (st - 1) % 2)
        if st >= 2 and st % 2 == 0:
            turn(("pv", "stick", st // 2 - 1), 6 + (st // 2 - 1) % 2)
    ht_turns(5)
    ffn_turns(2)

    ctx = ExitStack()
    with ctx:
        def sb(name, shape, dt=F32):
            return ctx.enter_context(nc.sbuf_tensor(name, shape, dt))

        def sem(name):
            return ctx.enter_context(nc.semaphore(name))

        raw = [sb(f"raw{i}", [P, CHUNKW]) for i in range(2)]
        uh = [sb(f"unit_hi{i}", [P, CHUNKW], F32R) for i in range(2)]
        ul = [sb(f"unit_lo{i}", [P, CHUNKW], F32R) for i in range(2)]
        rawd = [sb(f"raw_down{i}", [P, D]) for i in range(2)]
        down = sb("down", [P, 2, 2, D], F32R)
        accg = sb("accg", [P, 6 * D])
        x = sb("x", [P, TT, D])
        hh = sb("h_hi", [P, KD, S], F32R)
        hl = sb("h_lo", [P, KD, S], F32R)
        hf = sb("h_full", [P, 4 * S])
        yh = sb("y_hi", [P, KD, S], F32R)
        yl = sb("y_lo", [P, KD, S], F32R)
        att = sb("att", [P, 2, 3072])
        ada1 = sb("ada1", [P, CHUNKW])
        cst = sb("consts", [P, N_CONST])
        work = sb("work", [P, 3072])
        grow = sb("gate_rows", [P, 2, D])
        cols = sb("cols", [P, 512])
        small = sb("small", [P, 256])

        def C(name):
            return cst[:, CONST_AT[name][0]:CONST_AT[name][1]]

        ident, ones = C("ident"), C("ones")
        ada = [att[:, 1, 0:CHUNKW], ada1[:, :]]
        kiT = att[:, 1, 2304:2560]
        qiT = hf[:, :].rearrange("p (b t) -> p b t", b=4)
        ybc = hf[:, :].rearrange("p (b t) -> p b t", b=4)

        def qT(a):
            return att[:, a, 0:1024].rearrange("p (b t) -> p b t", b=4)

        def kT(a):
            return att[:, a, 1024:2048].rearrange("p (b t) -> p b t", b=4)

        def vv(a):
            return att[:, a, 2048:3072].rearrange("p (t n) -> p t n", t=TT)

        lnrow = att[:, 0, 0:2 * D].rearrange("p (a n) -> p a n", a=2)
        xn = att[:, 1, 0:TT * D].rearrange("p (t n) -> p t n", t=TT)
        mixed = att[:, 1, 0:2 * S].rearrange("p (k t) -> p k t", k=2)
        stage = [work[:, P * i:P * (i + 1)] for i in range(4)]
        stage_c = work[0:KD, 512:512 + P]
        PCOLS = 101
        ev_conv = cols[:, 0:12]
        pool_scale = cols[:, 12:16]
        q_gain = cols[:, 16:19]
        kv_gain = cols[:, 19:21]
        mix_gain = cols[:, 21:29]
        mlp_gain = cols[:, 29:37]
        modT = cols[:, 37:37 + 64].rearrange("p (l j) -> p l j", l=2)
        conv_w = [cols[:, 112:112 + 132], cols[:, 244:244 + 132]]
        cond = cols[:, 440:448]
        wiT = work[64:72, 512:768]
        cgb = [work[:, 1536:1792], work[:, 1920:2176]]
        L = [work[:, 384 * i:384 * (i + 1)] for i in range(2)]
        PT = [work[:, 768 + 384 * i:768 + 384 * (i + 1)] for i in range(2)]
        idx = work[:, 2304:2688]
        distm = work[:, 2688:3072]
        zm = [work[:, 384 * i:384 * (i + 1)] for i in range(2)]
        sig = [work[:, 768 + 384 * i:768 + 384 * (i + 1)] for i in range(2)]
        sp = [work[:, 1536 + 384 * i:1536 + 384 * (i + 1)] for i in range(2)]
        wT = [work[:, 2304 + 384 * i:2304 + 384 * (i + 1)] for i in range(2)]
        fv = [work[:, 512 * i:512 * i + 256] for i in range(2)]
        fg = [work[:, 512 * i + 256:512 * i + 512] for i in range(2)]
        acth = [yh[:, i, :] for i in range(2)]
        actl = [yl[:, i, :] for i in range(2)]
        smax = small[:, 0:16].rearrange("p (h t) -> p h t", t=2)
        sbias = small[:, 16:32].rearrange("p (h t) -> p h t", t=2)
        ssum = small[:, 32:48].rearrange("p (h t) -> p h t", t=2)
        srec = small[:, 48:64].rearrange("p (h t) -> p h t", t=2)
        wi = small[:, 64:80]
        top8 = small[:, 80:88]
        bnst = small[:, 168:216].rearrange("p (t a) -> p t a", t=2)
        mv = small[:, 112:116].rearrange("p (t a) -> p t a", t=2)
        var = small[:, 116:120]
        rstd = small[:, 120:124]
        ssq = small[:, 124:126]
        half_neg = small[:, 216:220]
        ccol = small[:, 128:144].rearrange("p (t h) -> p t h", t=2)
        bfor = small[0:8, 144:145]
        cexp = small[:, 152:160]
        sqs = small[:, 164:168]
        zrow = accg[:, 0:1344].rearrange("p (t n) -> p t n", t=TT)
        upad = accg[:, 1344:2432].rearrange("p (g n) -> p g n", g=4)
        pp = [accg[:, 2432:2704], accg[:, 2704:2976]]
        pooled = accg[:, 2976:4000].rearrange("p (g n) -> p g n", g=4)
        qrow = accg[:, 4000:4512].rearrange("p (t n) -> p t n", t=TT)
        rt = [accg[:, 4512:4640], accg[:, 4640:4768]]
        qrot = accg[:, 4768:5280].rearrange("p (t n) -> p t n", t=TT)
        krot = accg[:, 5280:5536].rearrange("p (t n) -> p t n", t=TT)
        pool_w = accg[:, 5536:6048].rearrange("p (g n) -> p g n", g=4)
        qrT = att[:, 1, 0:512].rearrange("p (b t) -> p b t", b=2)
        krT = att[:, 1, 512:768]
        sq_scr = att[:, 1, 768:768 + Q_LORA]
        latn = att[:, 1, 1152:1152 + 1280].rearrange("p (t n) -> p t n", t=TT)
        downf = down[:, :, :, :].rearrange("p a b n -> p (a b n)")
        lat_h = downf[:, 0:1280].rearrange("p (k t) -> p k t", k=5)
        lat_l = downf[:, 1280:2560].rearrange("p (k t) -> p k t", k=5)
        lat_f = hf[:, :]
        gates = accg[:, :].rearrange("p (k t) -> p k t", k=24)
        o_h = [yh[:, 0:4, :], yh[:, 4:8, :], downf[:, 0:1024].rearrange("p (k t) -> p k t", k=4)]
        o_l = [yl[:, 0:4, :], yl[:, 4:8, :], downf[:, 1024:2048].rearrange("p (k t) -> p k t", k=4)]
        f_t = [hf[0:8, 256 * i:256 * (i + 1)] for i in range(4)]

        bank = [ctx.enter_context(nc.psum_tensor(f"bank{i}", [P, 512], F32)) for i in range(8)]

        bank_full = [sem(f"bank_full{i}") for i in range(8)]
        bank_free = [sem(f"bank_free{i}") for i in range(8)]
        raw_in = [sem(f"raw_in{i}") for i in range(2)]
        rawd_in = [sem(f"rawd_in{i}") for i in range(2)]
        ada_in = [sem(f"ada_in{i}") for i in range(2)]
        hi_up, lo_up, hi_dn, lo_dn = sem("hi_up"), sem("lo_up"), sem("hi_dn"), sem("lo_dn")
        down_done = sem("down_done")
        c_in, stage_in, const_in, x_in, ln_in, pw_in, grow_in, out_done = (sem(n) for n in (
            "c_in", "stage_in", "const_in", "x_in", "ln_in", "pool_w_in", "gate_rows_in", "out_done"))
        dve_chain, act_chain, pool_chain = sem("dve_chain"), sem("act_chain"), sem("pool_chain")
        cond_exp, ada_acc = sem("cond_exp"), sem("ada_acc")
        row_ready, h_hi, h_lo = sem("row_ready"), sem("h_hi"), sem("h_lo")
        var_ready, rstd_ready = sem("var_ready"), sem("rstd_ready")
        idx_relu, wi_rows, bg_ready = sem("idx_relu"), sem("wi_rows"), sem("bg_ready")
        max_ready, exp_done, pv_done, o_hi = (sem(n) for n in ("max_ready", "exp_done", "pv_done", "o_hi"))
        cg_ready, yb_hi = sem("cg_ready"), sem("yb_hi")
        tap_done, gate_done, silu_done, prod_done, act_hi, act_lo = (sem(n) for n in (
            "tap_done", "gate_done", "silu_done", "prod_done", "act_hi", "act_lo"))
        lat_sq, lat_norm, lat_hi, lat_lo = sem("lat_sq"), sem("lat_norm"), sem("lat_hi"), sem("lat_lo")
        pool_ready, pool_hi, pool_lo, rot_ready, pool_zero = (sem(n) for n in (
            "pool_ready", "pool_hi", "pool_lo", "rot_ready", "pool_zero"))
        f_log, c_ready = sem("f_log"), sem("c_ready")
        z_ready, soft_log, w_ready = sem("z_ready"), sem("soft_log"), sem("w_ready")
        gate_ready, mix_ready, mix_hi = sem("gate_ready"), sem("mix_ready"), sem("mix_hi")

        ATT_N = {DSA: 0, MLA: 1, FOX: 2, MOBA: 3, "stick": 4}

        ATT_OUT = {DSA: (yh[:, 0:4, :], yl[:, 0:4, :]), MLA: (yh[:, 4:8, :], yl[:, 4:8, :]),
                   FOX: (o_h[1], o_l[1]), MOBA: (o_h[2], o_l[2]), "stick": (o_h[0], o_l[0])}

        def att_count(a, h):
            return HEADS * ATT_N[a] + h + 1

        def full(eng, name):
            b, _, k = turns[name]
            eng.wait_ge(bank_full[b], k)
            return bank[b]

        def evacuated(eng, name):
            b, k, _ = turns[name]
            eng.wait_ge(bank_free[b], k + 1)

        def free(name):
            return bank_free[turns[name][0]]

        def unit_full(eng, g):
            eng.wait_ge(bank_full[4 + g % 2], g // 2 + 1)
            return bank[4 + g % 2]

        def unit_evacuated(eng, g):
            eng.wait_ge(bank_free[4 + g % 2], g // 2 + 1)

        def unit_free(g):
            return bank_free[4 + g % 2]

        class Chain:

            def __init__(self, eng, semaphore):
                self.eng, self.sem, self.base, self.k = eng, semaphore, 0, 0

            def mark(self, ins):
                self.k += 1
                ins.then_inc(self.sem, 1)
                return self.k

            def need(self, k):
                self.eng.wait_ge(self.sem, self.base + k)

            def __call__(self, ins):
                self.need(self.mark(ins))

            def enter(self, i, first, per):
                self.start = self.base + self.k
                self.base, self.k = i * per + (self.start - first * per), 0

            def leave(self, iterations, per):
                assert self.k == per, (self.k, per)
                self.base, self.k = self.start + iterations * per, 0

        FILL = {DSA: {1: [(G_BG[0], 0)], 2: [(G_BG[0], 1)], 8: [(G_BG[1], 0)], 9: [(G_BG[1], 1)]}, MLA: {}}
        for a, fill in ((FOX, G_QKV[MOBA]), (MOBA, G_QKVS)):
            halves = [(g, part) for g in fill for part in range(2)]
            FILL[a] = {st: [halves[st + 1]] for st in range(HEADS + 2)}
            FILL[a][0] = halves[:2]
            FILL[a][HEADS + 1] = halves[-2:]
        FILL["stick"] = {i: [(G_GATE[i], 0), (G_GATE[i], 1)] for i in range(10)}
        DONE = {a: {st: [g for g, part in fill if part == 1] for st, fill in f.items()} for a, f in FILL.items()}
        ADA_FIRST = range(0, 8)
        ADA_IDX = {1 + i: [8 + i] for i in range(6)}
        ADA_TOP = [14, 15]
        ADA_ATT = {2: [16], 9: [17]}
        ADA_OUT = {0: [18, 19], 1: [20, 21], 2: [22], 3: [23]}

        block = ctx.enter_context(nc.Block())

        def rows(a):
            return a.rearrange("a (b n) -> (a b) n", n=P)

        STAGED = [(stage[0][0:12, :], rows(W["ev_conv_w"][0])), (stage[0][12:16, :], rows(W["pool_scale"])),
                  (stage[0][16:19, :], rows(W["q_norm_g"])), (stage[0][19:21, :], rows(W["kv_norm_g"])),
                  (stage[0][21:29, :], rows(W["norm_mix_2"])), (stage[0][29:37, :], rows(W["norm_mlp_2"])),
                  (stage[1], rows(W["ffn_conv_w"][0])[0:P, :]), (stage[2], rows(W["ffn_conv_w"][1])[0:P, :]),
                  (stage[3][0:4, :], rows(W["ffn_conv_w"][0])[P:132, :]),
                  (stage[3][4:8, :], rows(W["ffn_conv_w"][1])[P:132, :]),
                  (bfor, W["b_forget_2"].rearrange("a n -> n a"))]
        for layer in range(2):
            for part in range(2):
                r0, at = 24 * part, 37 + 32 * layer + 16 * part
                STAGED.append((stage[0][at:at + 16, :], rows(W["ada_b"][layer:layer + 1, P * r0:P * (r0 + 16)])))

        def ada_half(a):
            layer, j, half = a // (2 * MOD_BLOCKS), a // 2 % MOD_BLOCKS, a % 2
            return W["ada_w"][layer][AC * half:AC * (half + 1), AC * j:AC * (j + 1)].rearrange("(t p) n -> p t n", p=P)

        @block.sync
        def _(sp_):
            def load_unit(g):
                u, s = units[g], g % 2
                if g >= 2:
                    sp_.wait_ge(lo_up, g - 1)
                if u["kind"] == "pair":
                    dst = raw[s][:, :].rearrange("p (t a n) -> p t a n", t=KD, a=2)
                    for a in range(2):
                        src = u["src"][:, u["c0"][a]:u["c0"][a] + P].rearrange("(t p) n -> p t n", p=P)
                        sp_.dma_start(dst[:, :, a, :], src).then_inc(raw_in[s], 16)
                elif u["kind"] == "heads":
                    nkt, n = u["nkt"], u["n"]
                    for lo, hi in ((0, 1), (1, nkt)):
                        for t in range(lo, hi):
                            dst = raw[s][:, t * n:(t + 1) * n].rearrange("p (h c) -> p h c", h=u["nh"])
                            src = u["src"][t * P:(t + 1) * P, u["h0"]:u["h0"] + u["nh"], u["c0"]:u["c0"] + u["hc"]]
                            sp_.dma_start(dst, src).then_inc(raw_in[s], 16)
                else:
                    nkt, n = u["nkt"], u["n"]
                    dst = raw[s][:, 0:nkt * n].rearrange("p (t n) -> p t n", t=nkt)
                    src = u["src"][:, u["c0"]:u["c0"] + n].rearrange("(t p) n -> p t n", p=P)
                    m = nkt // 2
                    for a, b in ((0, m), (m, nkt)):
                        sp_.dma_start(dst[:, a:b, :], src[:, a:b, :]).then_inc(raw_in[s], 16)

            def load_ada(a):
                s = a % 2
                if a >= 2:
                    sp_.wait_ge(ada_acc, a - 1)
                sp_.dma_start(ada[s].rearrange("p (t n) -> p t n", t=KD // 2), ada_half(a)).then_inc(ada_in[s], 16)

            for a in range(2):
                load_ada(a)
            sp_.dma_start(x[:, :, :], W["x"][0].rearrange("(t p) n -> p t n", p=P)).then_inc(x_in, 16)
            for a in range(2, 6):
                load_ada(a)
            load_unit(0)
            for a in range(6, 8):
                load_ada(a)
            for g in range(1, G_QKV[DSA][2]):
                load_unit(g)
            for h in range(HEADS):
                for a in ADA_IDX.get(h, []):
                    load_ada(a)
                if h % 2 == 0:
                    load_unit(G_QKV[DSA][2 + h // 2])
            for a in ADA_TOP:
                load_ada(a)
            for g in G_CX + G_BG:
                load_unit(g)
            for st in range(HEADS + 2):
                for a in ADA_ATT.get(st, []):
                    load_ada(a)
                for g in DONE[DSA].get(st, []):
                    load_unit(g + 2)
            for j, g in enumerate(G_EO):
                for a in ADA_OUT[j]:
                    load_ada(a)
                load_unit(g + 2)

            def load_up(f, b, i, k):
                g0 = FFN_G0[f]
                s, u = (g0 + k) % 2, units[g0]
                sp_.wait_ge(lo_up, b + (g0 - 1))
                if u["kind"] == "pair":
                    dst = raw[s][:, :].rearrange("p (t a n) -> p t a n", t=KD, a=2)
                    for a in range(2):
                        src = u["src"][:, bass.ds(b * P + a * D_FF, P)].rearrange("(t p) n -> p t n", p=P)
                        sp_.dma_start(dst[:, :, a, :], src).then_inc(raw_in[s], 16)
                else:
                    dst = raw[s][:, 0:KD * P].rearrange("p (t n) -> p t n", t=KD)
                    for a in range(2):
                        src = u["src"][a * 512:(a + 1) * 512, bass.ds(b * P, P)].rearrange("(t p) n -> p t n", p=P)
                        sp_.dma_start(dst[:, 4 * a:4 * a + 4, :], src).then_inc(raw_in[s], 16)

            def load_down(f, b, k):
                d0 = FFN_D0[f]
                if not (isinstance(b, int) and d0 + b < 2):
                    sp_.wait_ge(lo_dn, b + (d0 - 1))
                sp_.dma_start(rawd[k][:, :], FFN_DOWN[f][bass.ds(b * P, P), :]).then_inc(rawd_in[k], 16)

            def load_all_ffn(f):
                if f == 0:
                    load_ada(2 * MOD_BLOCKS)
                else:
                    for k in range(2):
                        load_up(f, k, 0, k)
                load_down(f, 0, 0)
                with sp_.Fori(1, FFN_NB[f] // 2) as i:
                    for k in range(2):
                        load_up(f, 2 * i + k, i, k)
                        load_down(f, 2 * i + (k - 1), 1 - k)
                load_down(f, FFN_NB[f] - 1, 1)

            load_all_ffn(0)
            for g in G_Z[:2]:
                load_unit(g)
            load_ada(4 * MOD_BLOCKS - 1)
            for g in G_Z[2:] + G_U:
                load_unit(g)
            for g in G_QN:
                load_unit(g)
            evacuated(sp_, ("modr", 1, 1, 1))
            sp_.dma_start(pool_w, W["pool_w"][0].rearrange("g c d -> c g d")).then_inc(pw_in, 16)
            for g in [G_QR] + G_KN + G_VV + G_OO:
                load_unit(g)
            load_all_ffn(1)
            for g in range(G_F, FFN_G0[2]):
                load_unit(g)
            load_all_ffn(2)
            for tt in range(TT):
                sp_.wait_ge(row_ready, 13 + tt)
                sp_.dma_start(out[0, P * tt:P * (tt + 1), :], xn[:, tt, :]).then_inc(out_done, 16)
            sp_.wait_ge(out_done, 16 * TT)

        raw_loads = [0, 0]
        raw_need = []
        for g, u in enumerate(units):
            raw_loads[g % 2] += 16 * (u["nkt"] if u["kind"] == "heads" else 2)
            raw_need.append(raw_loads[g % 2])

        @block.gpsimd
        def _(pool):
            def lo_unit(g):
                if g >= NU:
                    return
                pool.wait_ge(hi_up, g + 1)
                w = units[g]["width"]
                nc.gpsimd.tensor_tensor(ul[g % 2][:, 0:w], raw[g % 2][:, 0:w], uh[g % 2][:, 0:w].bitcast(F32),
                                        ALU.subtract).then_inc(lo_up, 1)

            def lo_down(d):
                pool.wait_ge(hi_dn, d + 1)
                s = d % 2
                nc.gpsimd.tensor_tensor(down[:, s, 1, :], rawd[s][:, :], down[:, s, 0, :].bitcast(F32),
                                        ALU.subtract).then_inc(lo_dn, 1)

            def power(n, src, w, eps):
                pool.wait_ge(var_ready, n + 1)
                nc.gpsimd.tensor_scalar(rstd[:, 0:w], src, eps, None, ALU.add).then_inc(pool_chain, 1)
                pool.wait_ge(pool_chain, n + 2)
                nc.gpsimd.tensor_tensor(rstd[:, 0:w], rstd[:, 0:w], half_neg[:, 0:w], ALU.pow).then_inc(rstd_ready, 1)

            def h_low(n):
                for q in range(4):
                    pool.wait_ge(h_hi, 4 * n + q + 1)
                    nc.gpsimd.tensor_tensor(hl[:, 2 * q:2 * q + 2, :],
                                            hf[:, 512 * (q % 2):512 * (q % 2) + 512].rearrange("p (k t) -> p k t", k=2),
                                            hh[:, 2 * q:2 * q + 2, :].bitcast(F32), ALU.subtract).then_inc(h_lo, 1)

            def ffn(f):
                g0, d0, nb = FFN_G0[f], FFN_D0[f], FFN_NB[f]
                w = units[g0]["width"]
                lo_down(d0)

                def body(i, k):
                    b = 2 * i + k
                    s = (g0 + k) % 2
                    pool.wait_ge(hi_up, b + (g0 + 3))
                    nc.gpsimd.tensor_tensor(ul[s][:, 0:w], raw[s][:, 0:w], uh[s][:, 0:w].bitcast(F32),
                                            ALU.subtract).then_inc(lo_up, 1)
                    pool.wait_ge(hi_dn, b + (d0 + 2))
                    nc.gpsimd.tensor_tensor(down[:, 1 - k, 1, :], rawd[1 - k][:, :], down[:, 1 - k, 0, :].bitcast(F32),
                                            ALU.subtract).then_inc(lo_dn, 1)

                with pool.Fori(0, nb // 2 - 1) as i:
                    for k in range(2):
                        body(i, k)
                lo_unit(g0 + nb)
                lo_down(d0 + nb - 1)
                lo_unit(g0 + nb + 1)

            nc.gpsimd.memset(half_neg, -0.5).then_inc(pool_chain, 1)
            lo_unit(0)
            lo_unit(1)
            h_low(0)
            for g in range(2, G_EO[-1] + 3):
                lo_unit(g)
            power(0, mv[:, :, 1], 2, LN_EPS)
            h_low(1)
            ffn(0)
            power(1, mv[:, :, 1], 2, LN_EPS)
            h_low(2)
            for g in range(G_Z[0] + 2, G_U[-1]):
                lo_unit(g)
            evacuated(pool, ("modr", 1, 0, 1))
            for pad in (upad[:, :, 0:PAD], pp[0][:, 0:PAD], pp[1][:, 0:PAD]):
                nc.gpsimd.memset(pad, 0.0).then_inc(pool_zero, 1)
            power(2, var, 4, RMS_EPS)
            lo_unit(G_U[-1])
            for g in range(G_Z[-1] + 3, G_OO[-1] + 3):
                lo_unit(g)
            power(3, mv[:, :, 1], 2, LN_EPS)
            h_low(3)
            ffn(1)
            power(4, mv[:, :, 1], 2, LN_EPS)
            power(5, ssq, 2, D * RMS_EPS)
            h_low(4)
            for g in range(G_F + 2, G_WO[-1] + 3):
                lo_unit(g)
            power(6, var[:, 0:2], 2, RMS_EPS)
            h_low(5)
            ffn(2)
            power(7, var[:, 0:2], 2, RMS_EPS)

        @block.scalar
        def _(act):
            link = Chain(act, act_chain)

            def hi_unit(g):
                if g >= NU:
                    return
                s, w = g % 2, units[g]["width"]
                act.wait_ge(raw_in[s], raw_need[g])
                if g >= 2:
                    act.wait_ge(bank_full[4 + s], g // 2)
                nc.scalar.activation(uh[s][:, 0:w], raw[s][:, 0:w], ACT.Copy).then_inc(hi_up, 1)

            def hi_down(d):
                s = d % 2
                act.wait_ge(rawd_in[s], 16 * (d // 2 + 1))
                if d >= 2:
                    act.wait_ge(down_done, d - 1)
                nc.scalar.activation(down[:, s, 0, :], rawd[s][:, :], ACT.Copy).then_inc(hi_dn, 1)

            def h_high(n):
                for q in range(4):
                    evacuated(act, ("ht", n, q))
                    nc.scalar.activation(hh[:, 2 * q:2 * q + 2, :],
                                         hf[:, 512 * (q % 2):512 * (q % 2) + 512].rearrange("p (k t) -> p k t", k=2),
                                         ACT.Copy).then_inc(h_hi, 1)

            def evac(g, dst, scale=1.0):
                b = unit_full(act, g)
                nc.scalar.activation(dst, b[:, :].rearrange("p (k t) -> p k t", k=2), ACT.Copy, scale=scale
                                     ).then_inc(unit_free(g), 1)
                hi_unit(g + 2)

            def evac_qkv(g, a, j):
                evac(g, qT(a)[:, 2 * j:2 * j + 2, :] if j < 2 else kT(a)[:, 2 * j - 4:2 * j - 2, :] if j < 4
                     else vv(a)[:, :, UC * (j - 4):UC * (j - 3)], SCALE if j < 2 else 1.0)

            def other(g):
                unit_full(act, g)
                hi_unit(g + 2)

            def exps(a, h):
                act.wait_ge(max_ready, att_count(a, h))
                b = bank[turns["score", a, h][0]]
                for tt, (c0, n) in enumerate(((0, P), (P, S))):
                    ins = nc.scalar.activation(b[:, c0:c0 + n], b[:, c0:c0 + n], ACT.Exp, bias=sbias[:, h, tt:tt + 1],
                                               accum_out=ssum[:, h, tt:tt + 1])
                ins.then_inc(exp_done, 1)

            def evac_pt(a, h):
                b = full(act, ("tr", a, h))
                if att_count(a, h) > 2:
                    act.wait_ge(pv_done, att_count(a, h) - 2)
                nc.scalar.activation(PT[h % 2], b[:, 0:384], ACT.Copy).then_inc(free(("tr", a, h)), 1)

            def out_high(a, p):
                act.wait_ge(pv_done, att_count(a, 2 * p + 1))
                b = bank[turns["pv", a, p][0]]
                nc.scalar.activation(ATT_OUT[a][0][:, p, :], b[:, 0:256], ACT.Copy).then_inc(o_hi, 1)

            def attention(a, filler):
                for st in range(HEADS + 2):
                    if st < HEADS:
                        exps(a, st)
                    if 1 <= st <= HEADS:
                        evac_pt(a, st - 1)
                    if st >= 2 and st % 2 == 1:
                        out_high(a, (st - 2) // 2)
                    for g in DONE[a].get(st, []):
                        filler(g)

            def load_rows(a, *srcs):
                for i, src in enumerate(srcs):
                    act.dma_start(lnrow[:, i, :], src.partition_broadcast(P)).then_inc(ln_in, 16)

            def load_gates(layer, w):
                act.dma_start(grow[:, w, :], W["ada_b"][layer:layer + 1, (3 * w + 2) * D:(3 * w + 3) * D]
                              .partition_broadcast(P)).then_inc(grow_in, 16)

            def ffn(f):
                g0, d0, nb = FFN_G0[f], FFN_D0[f], FFN_NB[f]
                w = units[g0]["width"]
                half = units[g0]["kind"] == "pair"
                act0 = sum(FFN_NB[:f])
                hi_down(d0)

                def body(i, k, fixed):
                    b, s = 2 * i + k, (g0 + k) % 2
                    prod = bank[6][:, S * k:S * (k + 1)]

                    def act_high():
                        nc.scalar.activation(acth[k], prod, ACT.Copy).then_inc(act_hi, 1)

                    act.wait_ge(bank_full[4 + s], i + ((g0 + k) // 2 + 1))
                    if half:
                        cw = conv_w[f]
                        nc.scalar.activation(fv[k], bank[4 + s][:, 0:256], ACT.Copy,
                                             scale=cw[:, bass.ds(b + 2 * 44, 1)])
                        nc.scalar.activation(fg[k], bank[4 + s][:, 256:512], ACT.Copy,
                                             scale=cw[:, bass.ds(b + (2 * 44 + 22), 1)]).then_inc(tap_done, 1)
                    else:
                        nc.scalar.activation(fv[k], bank[4 + s][:, 0:256], ACT.Relu).then_inc(tap_done, 1)
                        act.wait_ge(bank_free[4 + s], i + ((g0 + k) // 2 + 1))
                        act_high()
                    if fixed:
                        hi_unit(g0 + b + 2)
                    else:
                        act.wait_ge(raw_in[s], i * 32 + (raw_need[g0 + k] + 32))
                        nc.scalar.activation(uh[s][:, 0:w], raw[s][:, 0:w], ACT.Copy).then_inc(hi_up, 1)
                    if half:
                        act.wait_ge(gate_done, b + (act0 + 1))
                        if not (fixed and act0 + b == 0):
                            act.wait_ge(act_lo, b + act0)
                        nc.scalar.activation(prod, fg[k], ACT.Silu).then_inc(silu_done, 1)
                        if f == 0:
                            act.wait_ge(ada_acc, b + 2 * MOD_BLOCKS)
                            act.dma_start(ada[1 - k].rearrange("p (t n) -> p t n", t=KD // 2),
                                          W["ada_w"][1][AC * (1 - k):AC * (2 - k), bass.ds(i * AC + AC * k, AC)]
                                          .rearrange("(t p) n -> p t n", p=P)).then_inc(ada_in[1 - k], 16)
                        act.wait_ge(prod_done, b + (act0 + 1))
                        act_high()
                    if fixed:
                        if b + 1 < nb:
                            hi_down(d0 + b + 1)
                    else:
                        act.wait_ge(rawd_in[1 - k], i * 16 + (16 * ((d0 + k + 1) // 2) + 16))
                        act.wait_ge(down_done, b + d0)
                        nc.scalar.activation(down[:, 1 - k, 0, :], rawd[1 - k][:, :], ACT.Copy).then_inc(hi_dn, 1)

                for k in range(2):
                    body(0, k, True)
                with act.Fori(1, nb // 2 - 1) as i:
                    for k in range(2):
                        body(i, k, False)
                for k in range(2):
                    body(nb // 2 - 1, k, True)

            act.dma_start(stage_c, W["c"].rearrange("a (b n) -> (a b) n", n=P)).then_inc(c_in, 16)
            i0, i1 = CONST_AT["ident"]
            act.dma_start(cst[:, i0:i1], consts[:, i0:i1]).then_inc(c_in, 16)
            for dst, src in STAGED:
                act.dma_start(dst, src).then_inc(stage_in, 16)
            act.dma_start(cst[:, i1:], consts[:, i1:]).then_inc(const_in, 16)
            load_gates(0, 0)
            load_gates(0, 1)
            b = full(act, "cond")
            nc.scalar.activation(cond, b[:, 0:KD], ACT.Exp, scale=-1.0).then_inc(cond_exp, 1)
            hi_unit(0)
            hi_unit(1)
            h_high(0)
            for j in range(2):
                evac(G_QI[j], qiT[:, 2 * j:2 * j + 2, :])
            b = unit_full(act, G_KI)
            nc.scalar.activation(wiT, b[64:72, 0:256], ACT.Copy, scale=IDX_SCALE).then_inc(wi_rows, 1)
            nc.scalar.activation(kiT[0:64, :], b[0:64, 0:256], ACT.Copy)
            nc.scalar.activation(kiT[64:128, :], b[64:128, 256:512], ACT.Copy).then_inc(unit_free(G_KI), 1)
            hi_unit(G_KI + 2)
            b = full(act, "wi")
            nc.scalar.activation(wi, b[:, 0:16], ACT.Copy).then_inc(free("wi"), 1)
            for h in range(HEADS):
                b = full(act, ("idx", h))
                nc.scalar.activation(b[:, 0:384], b[:, 0:384], ACT.Relu).then_inc(idx_relu, 1)
                if h % 2 == 0:
                    evac_qkv(G_QKV[DSA][h // 2], 0, h // 2)
            for j in range(4, 6):
                evac_qkv(G_QKV[DSA][j], 0, j)

            def cg(i, g):
                b = unit_full(act, g)
                if i >= 2:
                    unit_evacuated(act, g - 2)
                nc.scalar.activation(cgb[i % 2], b[:, 0:256], ACT.Copy).then_inc(cg_ready, 1)
                hi_unit(g + 2)

            for i, g in enumerate(G_CX):
                cg(i, g)

            def gated(g):
                act.wait_ge(bg_ready, g - G_BG[0] + 1)
                i = 2 * (g - G_BG[0])
                nc.scalar.activation(yh[:, 4 + i:6 + i, :], bank[4 + g % 2][:, :].rearrange("p (k t) -> p k t", k=2), ACT.Copy
                                     ).then_inc(yb_hi, 1)
                hi_unit(g + 2)

            attention(DSA, gated)
            load_rows(0, W["ln_mix_g"][0:1, :], W["ln_mix_b"][0:1, :])
            for g in G_EO:
                other(g)
            h_high(1)
            act.wait_ge(row_ready, 2)
            load_gates(1, 0)
            load_rows(0, W["ln_ffn_g"][0:1, :], W["ln_ffn_b"][0:1, :])
            ffn(0)
            h_high(2)
            load_gates(1, 1)
            evacuated(act, ("modc", 1, 0))
            at = 0
            for g in G_Z:
                n = units[g]["n"]
                b = unit_full(act, g)
                nc.scalar.activation(zrow[:, :, at:at + n], b[:, 0:2 * n].rearrange("p (t n) -> p t n", t=TT),
                                     ACT.Copy).then_inc(unit_free(g), 1)
                hi_unit(g + 2)
                at += n
            for g in G_Z[1:]:
                unit_evacuated(act, g)
            act.wait_ge(ada_acc, 4 * MOD_BLOCKS - 1)
            for tt in range(TT):
                nc.scalar.activation(sq_scr, zrow[:, tt, 0:Q_LORA], ACT.Square, accum_out=sqs[:, tt:tt + 1]
                                     ).then_inc(lat_sq, 1)
                act.wait_ge(lat_sq, 2 * tt + 1)
                nc.scalar.activation(sq_scr[:, 0:KV_LORA], zrow[:, tt, Q_LORA:Q_LORA + KV_LORA], ACT.Square,
                                     accum_out=sqs[:, 2 + tt:3 + tt]).then_inc(lat_sq, 1)
                act.wait_ge(lat_sq, 2 * tt + 2)
            act.wait_ge(pool_zero, 3)
            evac(G_U[0], upad[:, 0:2, PAD:PAD + S])
            for i, (k0, k1) in enumerate(((0, 2), (2, 4), (4, 5))):
                evacuated(act, f"latT{i}")
                n = k1 - k0
                nc.scalar.activation(lat_h[:, k0:k1, :], lat_f[:, 512 * (i % 2):512 * (i % 2) + 256 * n]
                                     .rearrange("p (k t) -> p k t", k=n), ACT.Copy).then_inc(lat_hi, 1)
            evac(G_U[1], upad[:, 2:4, PAD:PAD + S])
            for j, g in enumerate(G_QN):
                evac(g, qT(0)[:, 2 * j:2 * j + 2, :], SCALE_MLA)
            evacuated(act, ("modr", 1, 1, 1))
            evac(G_QR, qrow)
            for j, g in enumerate(G_KN):
                evac(g, kT(0)[:, 2 * j:2 * j + 2, :])
            for j, g in enumerate(G_VV):
                evac(g, vv(0)[:, :, UC * j:UC * (j + 1)])
            b = full(act, "krT")
            nc.scalar.activation(krT, b[:, 0:256], ACT.Copy).then_inc(free("krT"), 1)
            b = full(act, "qrT")
            nc.scalar.activation(qrT, b[:, :].rearrange("p (k t) -> p k t", k=2), ACT.Copy, scale=SCALE_MLA
                                 ).then_inc(free("qrT"), 1)
            for i in range(2):
                evacuated(act, f"pool{i}")
                nc.scalar.activation(yh[:, 2 * i:2 * i + 2, :], lat_f[:, 512 * i:512 * i + 512]
                                     .rearrange("p (k t) -> p k t", k=2), ACT.Copy).then_inc(pool_hi, 1)
            attention(MLA, None)
            load_rows(0, W["ln_mix_g"][1:2, :], W["ln_mix_b"][1:2, :])
            for g in G_OO:
                other(g)
            h_high(3)
            act.wait_ge(row_ready, 6)
            load_rows(0, W["ln_ffn_g"][1:2, :], W["ln_ffn_b"][1:2, :])
            ffn(1)
            for tt in range(TT):
                act.wait_ge(row_ready, 7 + tt)
                ins = nc.scalar.activation(xn[:, tt, :], x[:, tt, :], ACT.Square, accum_out=ssq[:, tt:tt + 1])
            ins.then_inc(var_ready, 1)
            h_high(4)
            unit_evacuated(act, G_F)
            hi_unit(G_F + 2)
            link(nc.scalar.activation(f_t[1], f_t[0], ACT.Abs))
            link(nc.scalar.activation(f_t[1], f_t[1], ACT.Exp, scale=-1.0))
            nc.scalar.activation(f_t[1], f_t[1], ACT.Ln, bias=1.0).then_inc(f_log, 1)
            for j, g in enumerate(G_QKV[FOX]):
                evac_qkv(g, 0, j)
            attention(FOX, lambda g: evac_qkv(g, 1, g - G_QKV[MOBA][0]))
            attention(MOBA, lambda g: evac_qkv(g, 0, g - G_QKVS[0]))

            def gate_evac(g):
                evac(g, gates[:, 2 * (g - G_GATE[0]):2 * (g - G_GATE[0]) + 2, :])

            for st in range(HEADS + 2):
                if st < HEADS:
                    act.wait_ge(z_ready, st + 1)
                    b, t = bank[turns["z", st][0]], sig[st % 2]
                    link(nc.scalar.activation(t, zm[st % 2], ACT.Abs))
                    link(nc.scalar.activation(t, t, ACT.Exp, scale=-1.0))
                    nc.scalar.activation(b[:, 0:384], t, ACT.Ln, bias=1.0).then_inc(soft_log, 1)
                if 1 <= st <= HEADS:
                    evacuated(act, ("sfx", st - 1))
                    t = wT[(st - 1) % 2]
                    nc.scalar.activation(t, t, ACT.Exp).then_inc(w_ready, 1)
                if st >= 2 and st % 2 == 1:
                    out_high("stick", (st - 2) // 2)
                for g in DONE["stick"][st]:
                    gate_evac(g)
            load_rows(0, W["norm_final_2"].rearrange("(a n) -> a n", a=1))
            for g in G_GATE[10:]:
                gate_evac(g)
            for g in G_GATE[-2:]:
                unit_evacuated(act, g)
            for c in range(4):
                for n in BRANCHES:
                    v = gates[:, 8 * n + 2 * c:8 * n + 2 * c + 2, :]
                    nc.scalar.activation(v, v, ACT.Sigmoid).then_inc(gate_ready, 1)
                    other(G_LIFT[c, n])
                act.wait_ge(mix_ready, c + 1)
                g = G_LIFT[c, BRANCHES[-1]]
                nc.scalar.activation(hh[:, 2 * c:2 * c + 2, :], bank[4 + g % 2][:, :].rearrange("p (k t) -> p k t", k=2),
                                     ACT.Copy).then_inc(mix_hi, 1)
            for g in G_WO:
                other(g)
            h_high(5)
            ffn(2)

        @block.tensor
        def _(pe):
            def begin(name):
                b, k, _ = turns[name]
                if k:
                    pe.wait_ge(bank_free[b], k)
                return bank[b]

            def done(ins, name):
                ins.then_inc(bank_full[turns[name][0]], 1)

            def product(o, sh, sl, mh, ml, first, last):
                nc.tensor.matmul(o, sh, mh, start=first, stop=False)
                nc.tensor.matmul(o, sh, ml, start=False, stop=False)
                return nc.tensor.matmul(o, sl, mh, start=False, stop=last)

            def unit_begin(g):
                pe.wait_ge(lo_up, g + 1)
                if g >= 2:
                    pe.wait_ge(bank_free[4 + g % 2], g // 2)
                return bank[4 + g % 2]

            def unit_cols(g, mh, ml, blocks=(0, P), ready=None, part=None):
                o = bank[4 + g % 2] if part else unit_begin(g)
                s, n = g % 2, units[g].get("n", UC)
                nkt = units[g].get("nkt", KD)
                for i, c in enumerate(blocks):
                    if part not in (None, i):
                        continue
                    for kt in range(nkt):
                        if ready and i == 0:
                            pe.wait_ge(*ready(kt))
                        a = slice(kt * n + c, kt * n + c + P)
                        mm = product(o[:, S * i:S * (i + 1)], uh[s][:, a], ul[s][:, a], mh[:, kt, :], ml[:, kt, :],
                                     kt == 0, kt == nkt - 1)
                if part != 0:
                    mm.then_inc(bank_full[4 + s], 1)

            def unit_rows(g, sth, stl, ready=None, order=None, part=None):
                o = bank[4 + g % 2] if part else unit_begin(g)
                s, n = g % 2, units[g].get("n", UC)
                order = order or range(units[g].get("nkt", KD))
                for tt in range(TT):
                    if part not in (None, tt):
                        continue
                    for i, kt in enumerate(order):
                        if ready and tt == 0:
                            pe.wait_ge(*ready(kt))
                        a, t = slice(kt * n, kt * n + n), slice(P * tt, P * (tt + 1))
                        mm = product(o[:, n * tt:n * (tt + 1)], sth[:, kt, t], stl[:, kt, t], uh[s][:, a], ul[s][:, a],
                                     i == 0, i == len(order) - 1)
                if part != 0:
                    mm.then_inc(bank_full[4 + s], 1)

            def h_ready(n):
                return lambda kt: (h_lo, 4 * n + kt // 2 + 1)

            def transpose_rows(n, src, ready=None):
                o = [begin(("ht", n, q)) for q in range(4)]
                for tt in range(TT):
                    if ready is not None:
                        pe.wait_ge(row_ready, ready + tt)
                    for kt in range(KD):
                        c = S * (kt % 2) + P * tt
                        mm = nc.tensor.transpose(o[kt // 2][:, c:c + P], src[:, tt, P * kt:P * (kt + 1)], ident)
                        if tt == 1 and kt % 2 == 1:
                            done(mm, ("ht", n, kt // 2))

            def mod_columns(layer, parts):
                name = ("modc", layer, parts[0])
                o = begin(name)
                for i, part in enumerate(parts):
                    for j in range(16):
                        block = 6 * part + j // 4
                        if j % 4 == 0:
                            pe.wait_ge(ada_acc, 2 * (MOD_BLOCKS * layer + block) + 2)
                        c = AC * block + P * (j % 4)
                        mm = nc.tensor.matmul(o[:, 16 * i + j:16 * i + j + 1], accg[:, c:c + P], ones[:, 0:1],
                                              start=True, stop=True)
                done(mm, name)

            def mod_rows(layer, w):
                for half in range(2):
                    block = 6 * w + 4 + half
                    pe.wait_ge(ada_acc, 2 * (MOD_BLOCKS * layer + block) + 2)
                    o = begin(("modr", layer, w, half))
                    mm = nc.tensor.matmul(o[:, :], ones, accg[:, AC * block:AC * (block + 1)], start=True, stop=True)
                    done(mm, ("modr", layer, w, half))

            def score(a, h):
                o = begin(("score", a, h))
                p0, blk = DH * (h % 2), h // 2
                q, k = qT(ATT_SET[a])[p0:p0 + DH, blk, :], kT(ATT_SET[a])[p0:p0 + DH, blk, :]
                for tt, (c0, n) in enumerate(((0, P), (P, S))):
                    t = slice(P * tt, P * (tt + 1))
                    one = a in (DSA, MOBA)
                    mm = nc.tensor.matmul(o[:, c0:c0 + n], q[:, t], k[:, 0:n], start=True, stop=one)
                    if a == MLA:
                        r0 = D_ROPE * (h % 4)
                        mm = nc.tensor.matmul(o[:, c0:c0 + n], qrT[r0:r0 + D_ROPE, h // 4, t],
                                              krT[r0:r0 + D_ROPE, 0:n], start=False, stop=True,
                                              tile_position=(r0, 0))
                    if a == FOX:
                        mm = nc.tensor.matmul(o[:, c0:c0 + n], ident[0:8, h:h + 1].to_broadcast([8, P]),
                                              f_t[1][:, 0:n], start=False, stop=True)
                done(mm, ("score", a, h))

            def transpose_p(a, h):
                o = begin(("tr", a, h))
                for i in range(3):
                    mm = nc.tensor.transpose(o[:, P * i:P * (i + 1)], L[h % 2][:, P * i:P * (i + 1)], ident)
                done(mm, ("tr", a, h))

            def weighted(a, h, t, set_):
                o = begin(("pv", a, h // 2)) if h % 2 == 0 else bank[turns["pv", a, h // 2][0]]
                p0 = DH * (h % 2)
                v = vv(set_)
                nc.tensor.matmul(o[p0:p0 + DH, 0:S], v[:, 0, DH * h:DH * (h + 1)], t[:, 0:S], start=True, stop=False)
                nc.tensor.matmul(o[p0:p0 + DH, P:S], v[:, 1, DH * h:DH * (h + 1)], t[:, S:S + P],
                                 start=False, stop=True).then_inc(pv_done, 1)

            def attention(a, filler, v_units):
                score(a, 0)
                for st in range(HEADS + 2):
                    if st + 1 < HEADS:
                        score(a, st + 1)
                    if 1 <= st <= HEADS:
                        transpose_p(a, st - 1)
                    if st >= 2:
                        if st == 2:
                            for g in v_units:
                                unit_evacuated(pe, g)
                        evacuated(pe, ("tr", a, st - 2))
                        weighted(a, st - 2, PT[st % 2], ATT_SET[a])
                    for g, part in FILL[a].get(st, []):
                        filler(g, part)

            def out_split(a):
                for p in (2, 3):
                    evacuated(pe, ("pv", a, p))

            def ffn(f):
                g0, d0, nb = FFN_G0[f], FFN_D0[f], FFN_NB[f]
                n = units[g0].get("n", UC)
                act0 = sum(FFN_NB[:f])

                def up(i, k, ready=None, fixed=False):
                    b, s = 2 * i + k, (g0 + k) % 2
                    pe.wait_ge(lo_up, b + (g0 + 1))
                    pe.wait_ge(bank_free[4 + s], i + (g0 + k) // 2)
                    for j, c in enumerate(range(0, n, P)):
                        for kt in range(KD):
                            if ready and j == 0:
                                pe.wait_ge(*ready(kt))
                            a = slice(kt * n + c, kt * n + c + P)
                            mm = product(bank[4 + s][:, S * j:S * (j + 1)], uh[s][:, a], ul[s][:, a],
                                         hh[:, kt, :], hl[:, kt, :], kt == 0, kt == KD - 1)
                    mm.then_inc(bank_full[4 + s], 1)

                def downward(i, k, first, last):
                    b = 2 * i + k
                    pe.wait_ge(lo_dn, b + (d0 + 1))
                    pe.wait_ge(act_lo, b + (act0 + 1))
                    for tt in range(TT):
                        for half in range(2):
                            if first:
                                begin(("acc", f, 2 * tt + half))
                            t, c = slice(P * tt, P * (tt + 1)), slice(512 * half, 512 * (half + 1))
                            mm = product(bank[2 * tt + half][:, :], acth[k][:, t], actl[k][:, t],
                                         down[:, k, 0, c], down[:, k, 1, c], first, last)
                            if last and (tt, half) != (1, 1):
                                done(mm, ("acc", f, 2 * tt + half))
                    mm.then_inc(down_done, 1)

                up(0, 0, ready=h_ready((1, 3, 5)[f]))
                up(0, 1)
                downward(0, 0, True, False)
                with pe.Fori(1, nb // 2) as i:
                    up(i, 0)
                    downward(i - 1, 1, False, False)
                    up(i, 1)
                    downward(i, 0, False, False)
                downward(nb // 2 - 1, 1, False, True)

            pe.wait_ge(c_in, 32)
            o = begin("cond")
            mm = nc.tensor.transpose(o[:, 0:KD], stage_c, ident[0:KD, 0:KD])
            done(mm, "cond")
            pe.wait_ge(stage_in, 16 * len(STAGED))
            o = begin("stage")
            for i, n in enumerate((PCOLS, P, P, 8)):
                mm = nc.tensor.transpose(o[:, P * i:P * i + n], stage[i][0:n, :], ident[0:n, 0:n])
            done(mm, "stage")
            pe.wait_ge(const_in, 16)
            pe.wait_ge(x_in, 16)
            transpose_rows(0, x)
            mod_columns(0, (0,))
            for g in G_QI:
                unit_cols(g, hh, hl, ready=h_ready(0))
            unit_cols(G_KI, hh, hl, blocks=(64, 0))
            pe.wait_ge(wi_rows, 1)
            o = begin("wi")
            for tt in range(TT):
                mm = nc.tensor.transpose(o[:, 8 * tt:8 * tt + 8], wiT[:, P * tt:P * (tt + 1)], ident[64:72, 64:72])
            done(mm, "wi")
            for g in (G_QI[1], G_KI):
                unit_evacuated(pe, g)
            for h in range(HEADS):
                o = begin(("idx", h))
                p0 = DH * (h % 2)
                for tt, (c0, n) in enumerate(((0, P), (P, S))):
                    mm = nc.tensor.matmul(o[:, c0:c0 + n], qiT[p0:p0 + DH, h // 2, P * tt:P * (tt + 1)],
                                          kiT[p0:p0 + DH, 0:n], start=True, stop=True)
                done(mm, ("idx", h))
                if h % 2 == 0:
                    unit_cols(G_QKV[DSA][h // 2], hh, hl)
            for g in G_QKV[DSA][4:6]:
                unit_rows(g, hh, hl)
            for g in G_CX:
                unit_cols(g, hh, hl)
            for g in G_QKV[DSA][2:4]:
                unit_evacuated(pe, g)
            attention(DSA, lambda g, part: unit_cols(g, hh, hl, part=part), G_QKV[DSA][4:6])
            mod_rows(0, 0)
            out_split(DSA)
            for g in G_BG:
                unit_evacuated(pe, g)
            for g in G_EO:
                unit_rows(g, yh, yl, order=(4, 5, 6, 7, 0, 1, 2, 3))
            mod_columns(0, (1,))
            mod_rows(0, 1)
            transpose_rows(1, x, 1)
            ffn(0)
            mod_columns(1, (0, 1))
            transpose_rows(2, x, 3)
            for g in G_Z:
                unit_rows(g, hh, hl, ready=h_ready(2))
            mod_rows(1, 0)
            unit_cols(G_U[0], hh, hl)
            pe.wait_ge(lat_norm, 1)
            for i, (k0, k1) in enumerate(((0, 2), (2, 4), (4, 5))):
                o = begin(f"latT{i}")
                for kt in range(k0, k1):
                    for tt in range(TT):
                        c = S * (kt - k0) + P * tt
                        mm = nc.tensor.transpose(o[:, c:c + P], latn[:, tt, P * kt:P * (kt + 1)], ident)
                done(mm, f"latT{i}")
            unit_cols(G_U[1], hh, hl)
            mod_rows(1, 1)
            pe.wait_ge(lat_lo, 3)
            for g in G_QN:
                unit_cols(g, lat_h[:, 0:3, :], lat_l[:, 0:3, :])
            unit_rows(G_QR, lat_h[:, 0:3, :], lat_l[:, 0:3, :])
            for g in G_KN:
                unit_cols(g, lat_h[:, 3:5, :], lat_l[:, 3:5, :])
            for g in G_VV:
                unit_rows(g, lat_h[:, 3:5, :], lat_l[:, 3:5, :])
            pe.wait_ge(rot_ready, 1)
            o = begin("krT")
            for tt in range(TT):
                mm = nc.tensor.transpose(o[:, P * tt:P * (tt + 1)], krot[:, tt, :], ident)
            done(mm, "krT")
            pe.wait_ge(pool_ready, 1)
            pe.wait_ge(pw_in, 16)
            for i in range(2):
                o = begin(f"pool{i}")
                for j in range(2):
                    mm = nc.tensor.matmul(o[:, S * j:S * (j + 1)], pool_w[:, 2 * i + j, :], pooled[:, 2 * i + j, :],
                                          start=True, stop=True)
                done(mm, f"pool{i}")
            pe.wait_ge(rot_ready, 2)
            o = begin("qrT")
            for blk in range(2):
                for tt in range(TT):
                    c = S * blk + P * tt
                    mm = nc.tensor.transpose(o[:, c:c + P], qrot[:, tt, P * blk:P * (blk + 1)], ident)
            done(mm, "qrT")
            evacuated(pe, "krT")
            evacuated(pe, "qrT")
            for g in G_QN[-1:] + G_KN:
                unit_evacuated(pe, g)
            attention(MLA, None, G_VV)
            out_split(MLA)
            pe.wait_ge(pool_lo, 2)
            for g in G_OO:
                unit_rows(g, yh, yl)
            transpose_rows(3, x, 5)
            ffn(1)
            transpose_rows(4, xn, 9)
            unit_cols(G_F, hh, hl, blocks=(0,), ready=h_ready(4))
            for j, g in enumerate(G_QKV[FOX]):
                if j < 4:
                    unit_cols(g, hh, hl)
                else:
                    unit_rows(g, hh, hl)
            pe.wait_ge(c_ready, 1)
            o = begin("ccol")
            for tt in range(TT):
                mm = nc.tensor.transpose(o[:, 8 * tt:8 * tt + 8], f_t[1][:, P * tt:P * (tt + 1)], ident[0:8, 0:8])
            done(mm, "ccol")

            def projection(units_):
                return lambda g, part: (unit_cols if g < units_[4] else unit_rows)(g, hh, hl, part=part)

            for g in G_QKV[FOX][2:4]:
                unit_evacuated(pe, g)
            attention(FOX, projection(G_QKV[MOBA]), G_QKV[FOX][4:6])
            for g in G_QKV[MOBA][2:4]:
                unit_evacuated(pe, g)
            attention(MOBA, projection(G_QKVS), G_QKV[MOBA][4:6])
            for g in G_QKVS[2:4]:
                unit_evacuated(pe, g)
            def logits(h):
                o = begin(("z", h))
                p0, blk = DH * (h % 2), h // 2
                q, k = qT(0)[p0:p0 + DH, blk, :], kT(0)[p0:p0 + DH, blk, :]
                nc.tensor.matmul(o[:, 0:S], k[:, 0:P], q[:, 0:S], start=True, stop=True)
                mm = nc.tensor.matmul(o[:, S:S + P], k[:, P:S], q[:, P:S], start=True, stop=True)
                done(mm, ("z", h))

            logits(0)
            for st in range(HEADS + 2):
                if st + 1 < HEADS:
                    logits(st + 1)
                if 1 <= st <= HEADS:
                    h = st - 1
                    o, t = begin(("sfx", h)), sp[h % 2]
                    evacuated(pe, ("z", h))
                    nc.tensor.matmul(o[:, 0:S], C("suffix"), t[:, 0:S], start=True, stop=False)
                    nc.tensor.matmul(o[:, P:S], ones, t[:, S:S + P], start=False, stop=True)
                    mm = nc.tensor.matmul(o[:, S:S + P], C("suffix"), t[:, S:S + P], start=True, stop=True)
                    done(mm, ("sfx", h))
                if st >= 2:
                    h = st - 2
                    if h == 0:
                        for g in G_QKVS[4:6]:
                            unit_evacuated(pe, g)
                    pe.wait_ge(w_ready, h + 1)
                    weighted("stick", h, wT[h % 2], 0)
                for g, part in FILL["stick"][st]:
                    unit_cols(g, hh, hl, part=part)
            for g in G_GATE[10:]:
                unit_cols(g, hh, hl)
            out_split(MOBA)
            for c in range(4):
                for n in BRANCHES:
                    if (c, n) == (0, 0):
                        out_split("stick")
                    unit_cols(G_LIFT[c, n], o_h[n], o_l[n])

            def mixed_ready(kt):
                g = G_LIFT[kt // 2, BRANCHES[-1]]
                return bank_free[4 + g % 2], g // 2 + 1

            for g in G_WO:
                unit_rows(g, hh, hl, ready=mixed_ready)
            transpose_rows(5, xn, 11)
            ffn(2)

        @block.vector
        def _(dve):
            link = Chain(dve, dve_chain)
            V = nc.vector

            def modulation_add(s, kt, q, acc, out_):
                w, dst = ada[s][:, AC * q:AC * (q + 1)], out_ if kt == KD - 1 else acc
                if kt == 0:
                    return V.tensor_scalar(dst, w, cond[:, 0:1], None, ALU.mult)
                return V.scalar_tensor_tensor(dst, w, cond[:, kt:kt + 1], acc, ALU.mult, ALU.add)

            def modulation_half(a, acc):
                s, block = a % 2, a // 2 % MOD_BLOCKS
                dve.wait_ge(ada_in[s], 16 * (a // 2 + 1))
                if a:
                    dve.wait_ge(ada_acc, a)
                for q in range(KD // 2):
                    ins = modulation_add(s, KD // 2 * s + q, q, acc, accg[:, AC * block:AC * (block + 1)])
                    if q < KD // 2 - 1:
                        link(ins)
                ins.then_inc(ada_acc, 1)

            def mod_columns(layer, parts):
                name = ("modc", layer, parts[0])
                o = full(dve, name)
                for i, part in enumerate(parts):
                    sh, sc = (modT[:, layer, 16 * part + 8 * k:16 * part + 8 * k + 8] for k in range(2))
                    link(V.scalar_tensor_tensor(sc, o[:, 16 * i + 8:16 * i + 16], 1.0, sc, ALU.add, ALU.add))
                    ins = V.tensor_tensor(sh, o[:, 16 * i:16 * i + 8], sh, ALU.add)
                    if part != parts[-1]:
                        link(ins)
                ins.then_inc(free(name), 1)
                evacuated(dve, name)

            def mod_rows(layer, w):
                dve.wait_ge(grow_in, 32 if layer == 0 else 16 * (3 + w))
                for half in range(2):
                    name = ("modr", layer, w, half)
                    o, c = full(dve, name), slice(512 * half, 512 * (half + 1))
                    V.scalar_tensor_tensor(grow[:, w, c], o[:, :], 1.0, grow[:, w, c], ALU.add, ALU.add
                                           ).then_inc(free(name), 1)
                for half in range(2):
                    evacuated(dve, ("modr", layer, w, half))

            def h_columns(n, scale, shift):
                for q in range(4):
                    o = full(dve, ("ht", n, q))
                    if q >= 2:
                        dve.wait_ge(h_lo, 4 * n + q - 1)
                    for i in range(2):
                        kt, dst = 2 * q + i, hf[:, 512 * (q % 2) + S * i:512 * (q % 2) + S * (i + 1)]
                        if shift is None:
                            ins = V.tensor_scalar(dst, o[:, S * i:S * (i + 1)], scale[:, kt:kt + 1], None, ALU.mult)
                        else:
                            ins = V.tensor_scalar(dst, o[:, S * i:S * (i + 1)], scale[:, kt:kt + 1], shift[:, kt:kt + 1],
                                                  ALU.mult, ALU.add)
                        if i == 0:
                            link(ins)
                    ins.then_inc(free(("ht", n, q)), 1)

            def chunk_statistics(tt, i, n):
                return V.bn_stats(bnst[:, tt, 6 * i:6 * i + 6], x[:, tt, n * i:n * (i + 1)])

            def aggregate(tt, chunks):
                link(V.bn_aggr(mv[:, tt, :], bnst[:, tt, 0:6 * chunks]))

            def layer_norm(n, rows):
                dve.wait_ge(ln_in, 32 * (rows + 1))
                dve.wait_ge(var_ready, n + 1)
                for tt in range(TT):
                    ins = V.scalar_tensor_tensor(x[:, tt, :], x[:, tt, :], mv[:, tt, 0:1], lnrow[:, 0, :],
                                                 ALU.subtract, ALU.mult)
                    if tt < TT - 1:
                        link.mark(ins)
                    else:
                        link(ins)
                dve.wait_ge(rstd_ready, n + 1)
                for tt in range(TT):
                    V.scalar_tensor_tensor(x[:, tt, :], x[:, tt, :], rstd[:, tt:tt + 1], lnrow[:, 1, :],
                                           ALU.mult, ALU.add).then_inc(row_ready, 1)
                dve.wait_ge(row_ready, 2 * (rows + 1))

            def rms_variance():
                for tt in range(TT):
                    ins = V.scalar_tensor_tensor(var[:, tt:tt + 1], mv[:, tt, 0:1], mv[:, tt, 0:1], mv[:, tt, 1:2],
                                                 ALU.mult, ALU.add)
                ins.then_inc(var_ready, 1)

            def rms_rows(n, scale):
                dve.wait_ge(rstd_ready, n + 1)
                for tt in range(TT):
                    V.tensor_scalar(xn[:, tt, :], x[:, tt, :], rstd[:, tt:tt + 1], scale, ALU.mult, ALU.mult
                                    ).then_inc(row_ready, 1)

            def soft(a, h):
                o = full(dve, ("score", a, h))
                marks = []
                for tt, (c0, n) in enumerate(((0, P), (P, S))):
                    def table(name):
                        return C(name)[:, P:S] if tt == 0 else C(name)
                    ps = o[:, c0:c0 + n]
                    if a == DSA:
                        ins = V.scalar_tensor_tensor(ps, distm[:, c0:c0 + n], -SLOPES[h], ps, ALU.mult, ALU.add)
                    elif a == MOBA:
                        ins = V.scalar_tensor_tensor(ps, table("dist_causal"), -SLOPES[h], ps, ALU.mult, ALU.add)
                    elif a == FOX:
                        ins = V.scalar_tensor_tensor(ps, ps, ccol[:, tt, h:h + 1], table("causal"), ALU.add, ALU.add)
                    else:
                        ins = V.tensor_tensor(ps, ps, table("chunk"), ALU.add)
                    marks.append(link.mark(ins))
                for tt, (c0, n) in enumerate(((0, P), (P, S))):
                    link.need(marks[tt])
                    ins = V.tensor_reduce(sbias[:, h, tt:tt + 1], o[:, c0:c0 + n], AX.X, ALU.max, negate=True)
                ins.then_inc(max_ready, 1)

            def normalize(a, h):
                o, t = bank[turns["score", a, h][0]], L[h % 2]
                dve.wait_ge(exp_done, att_count(a, h))
                if h >= 2:
                    full(dve, ("tr", a, h - 2))
                link(V.reciprocal(srec[:, h, :], ssum[:, h, :]))
                V.tensor_scalar(t[:, 0:P], o[:, 0:P], srec[:, h, 0:1], None, ALU.mult)
                V.tensor_scalar(t[:, P:P + S], o[:, P:P + S], srec[:, h, 1:2], None, ALU.mult
                                ).then_inc(free(("score", a, h)), 1)

            def out_low(a, p):
                dve.wait_ge(o_hi, 4 * ATT_N[a] + p + 1)
                hi, lo = ATT_OUT[a]
                V.tensor_tensor(lo[:, p, :], bank[turns["pv", a, p][0]][:, 0:S], hi[:, p, :].bitcast(F32), ALU.subtract
                                ).then_inc(free(("pv", a, p)), 1)

            def attention(a, between=None):
                for st in range(HEADS + 2):
                    if st < HEADS:
                        soft(a, st)
                    if 1 <= st <= HEADS:
                        normalize(a, st - 1)
                    if st >= 2 and st % 2 == 1:
                        out_low(a, (st - 2) // 2)
                    if between:
                        between(st)

            def mixer_residual(gs, w, before=None):
                for j, g in enumerate(gs):
                    if before:
                        before(j)
                    o = unit_full(dve, g)[:, :].rearrange("p (t n) -> p t n", t=TT)
                    c = slice(UC * j, UC * (j + 1))
                    if w is not None:
                        link(V.tensor_tensor(o, o, grow[:, w, c].unsqueeze(1).to_broadcast([P, TT, UC]), ALU.mult))
                        V.scalar_tensor_tensor(x[:, :, c], x[:, :, c], ALPHA, o, ALU.mult, ALU.add).then_inc(unit_free(g), 1)
                    else:
                        V.tensor_tensor(x[:, :, c], x[:, :, c], o, ALU.add).then_inc(unit_free(g), 1)
                    unit_evacuated(dve, g)
                    for tt in range(TT):
                        ins = chunk_statistics(tt, j, UC)
                link(ins)
                for tt in range(TT):
                    ins = V.bn_aggr(mv[:, tt, :], bnst[:, tt, :])
                if w is None:
                    link(ins)
                    rms_variance()
                else:
                    ins.then_inc(var_ready, 1)

            def ffn(f):
                g0, d0, nb = FFN_G0[f], FFN_D0[f], FFN_NB[f]
                half = units[g0]["kind"] == "pair"
                act0 = sum(FFN_NB[:f])

                def body(i, k):
                    b, s = 2 * i + k, (g0 + k) % 2
                    prod = bank[6][:, S * k:S * (k + 1)]

                    def tap(j, back):
                        t = (fv[k], fg[k])[j]
                        w = conv_w[f][:, bass.ds(b + ((2 - back) * 44 + 22 * j), 1)]
                        return V.scalar_tensor_tensor(t[:, back:S], bank[4 + s][:, S * j:S * (j + 1) - back], w,
                                                      t[:, back:S], ALU.mult, ALU.add)

                    def modulation(q):
                        ins = modulation_add(k, KD // 2 * k + q, q, bank[7][:, :], accg[:, bass.ds(i * AC, AC)])
                        if q < KD // 2 - 1:
                            return link.mark(ins)
                        ins.then_inc(ada_acc, 1)

                    dve.wait_ge(tap_done, b + (act0 + 1))
                    if half:
                        gate = link.mark(tap(1, 1))
                        value = link.mark(tap(0, 1))
                        link.need(gate)
                        tap(1, 2).then_inc(gate_done, 1)
                        link.need(value)
                        tap(0, 2).then_inc(bank_free[4 + s], 1)
                        if f == 0:
                            dve.wait_ge(ada_in[k], i * 16 + 16 * (MOD_BLOCKS + 1))
                            dve.wait_ge(ada_acc, b + 2 * MOD_BLOCKS)
                            step = modulation(0)
                        dve.wait_ge(silu_done, b + (act0 + 1))
                        dve.wait_ge(bank_free[4 + s], i + ((g0 + k) // 2 + 1))
                        V.tensor_tensor(prod, fv[k], prod, ALU.mult).then_inc(prod_done, 1)
                        if f == 0:
                            link.need(step)
                            step = modulation(1)
                    else:
                        V.tensor_tensor(prod, bank[4 + s][:, 0:S], fv[k], ALU.mult).then_inc(bank_free[4 + s], 1)
                    dve.wait_ge(act_hi, b + (act0 + 1))
                    V.tensor_tensor(actl[k], prod, acth[k].bitcast(F32), ALU.subtract).then_inc(act_lo, 1)
                    if f == 0:
                        for q in (2, 3):
                            link.need(step)
                            step = modulation(q)

                per = 2 * (5, 2, 0)[f]
                for k in range(2):
                    body(0, k)
                with dve.Fori(1, nb // 2) as i:
                    link.enter(i, 1, per)
                    for k in range(2):
                        body(i, k)
                link.leave(nb // 2 - 1, per)
                chunks = [(tt, i) for tt in range(TT) for i in range(2)]

                def gated(j):
                    o = bank[j]
                    if j < 3:
                        full(dve, ("acc", f, j))
                    else:
                        dve.wait_ge(down_done, d0 + nb)
                    return link.mark(V.tensor_tensor(o[:, :], o[:, :], grow[:, 1, 512 * (j % 2):512 * (j % 2 + 1)], ALU.mult))

                mark = gated(0) if f < 2 else None
                for j, (tt, i) in enumerate(chunks):
                    c, o = slice(512 * i, 512 * (i + 1)), bank[j]
                    if f < 2:
                        after = gated(j + 1) if j < 3 else None
                        link.need(mark)
                        V.scalar_tensor_tensor(x[:, tt, c], x[:, tt, c], ALPHA, o[:, :], ALU.mult, ALU.add
                                               ).then_inc(free(("acc", f, j)), 1)
                        mark = after
                    else:
                        if j < 3:
                            full(dve, ("acc", f, j))
                        else:
                            dve.wait_ge(down_done, d0 + nb)
                        V.tensor_tensor(x[:, tt, c], x[:, tt, c], o[:, :], ALU.add).then_inc(free(("acc", f, j)), 1)
                    evacuated(dve, ("acc", f, j))
                    link(chunk_statistics(tt, i, 512))
                for tt in range(TT):
                    ins = V.bn_aggr(mv[:, tt, :], bnst[:, tt, 0:12])
                if f < 2:
                    ins.then_inc(var_ready, 1)
                else:
                    link(ins)
                    rms_variance()

            dve.wait_ge(cond_exp, 1)
            link(V.tensor_scalar(cond, cond, 1.0, None, ALU.add))
            link(V.reciprocal(cond, cond))
            V.tensor_tensor(cond, bank[turns["cond"][0]][:, 0:KD], cond, ALU.mult).then_inc(free("cond"), 1)
            evacuated(dve, "cond")
            for a in ADA_FIRST[:4]:
                modulation_half(a, bank[5][:, :])
            o = full(dve, "stage")
            link(V.tensor_copy(cols[:, 0:PCOLS], o[:, 0:PCOLS]))
            link(V.tensor_copy(conv_w[0][:, 0:P], o[:, P:2 * P]))
            link(V.tensor_copy(conv_w[1][:, 0:P], o[:, 2 * P:3 * P]))
            link(V.tensor_copy(conv_w[0][:, P:132], o[:, 3 * P:3 * P + 4]))
            V.tensor_copy(conv_w[1][:, P:132], o[:, 3 * P + 4:3 * P + 8]).then_inc(free("stage"), 1)
            for a in ADA_FIRST[4:]:
                modulation_half(a, bank[5][:, :])
            mod_columns(0, (0,))
            h_columns(0, modT[:, 0, 8:16], modT[:, 0, 0:8])
            evacuated(dve, "wi")
            for h in range(HEADS):
                dve.wait_ge(idx_relu, h + 1)
                r = bank[turns["idx", h][0]]
                if h:
                    evacuated(dve, ("idx", h - 1))
                for tt, (c0, n) in enumerate(((0, P), (P, S))):
                    w, d, t = wi[:, 8 * tt + h:8 * tt + h + 1], idx[:, c0:c0 + n], r[:, c0:c0 + n]
                    if h == 0:
                        ins = V.tensor_scalar(d, t, w, None, ALU.mult)
                    else:
                        ins = V.scalar_tensor_tensor(d, t, w, d, ALU.mult, ALU.add)
                ins.then_inc(free(("idx", h)), 1)
                for a in ADA_IDX.get(h, []):
                    modulation_half(a, bank[3][:, :])
            evacuated(dve, ("idx", HEADS - 1))
            dve.wait_ge(const_in, 16)
            for tt, (c0, n) in enumerate(((0, P), (P, S))):
                d = idx[:, c0:c0 + n]
                link(V.tensor_tensor(d, d, C("chunk")[:, P:S] if tt == 0 else C("chunk"), ALU.add))
                for _ in range(TOPK // 8):
                    link(V.max(top8, d))
                    link(V.match_replace(d, top8, d, REMOVED))
                m = distm[:, c0:c0 + n]
                link(V.tensor_scalar(m, d, REMOVED / 1.5, BIG, ALU.is_gt, ALU.mult))
                link(V.tensor_tensor(m, m, C("dist_chunk")[:, P:S] if tt == 0 else C("dist_chunk"), ALU.add))
                modulation_half(ADA_TOP[tt], bank[3][:, :])
            for b, g in enumerate(G_CX):
                o = unit_full(dve, g)
                dve.wait_ge(cg_ready, b + 1)
                p_ = o[:, S:2 * S]
                link(V.tensor_tensor(p_, p_, cgb[b % 2], ALU.mult))
                link(V.tensor_scalar(ybc[:, b, :], p_, ev_conv[:, 8 + b:9 + b], None, ALU.mult))
                for back in (1, 2):
                    w = ev_conv[:, 4 * (2 - back) + b:4 * (2 - back) + b + 1]
                    ins = V.scalar_tensor_tensor(ybc[:, b, back:S], p_[:, 0:S - back], w, ybc[:, b, back:S],
                                                 ALU.mult, ALU.add)
                    if back == 1:
                        link(ins)
                ins.then_inc(unit_free(g), 1)
            unit_evacuated(dve, G_CX[-1])

            def dsa_between(st):
                for g in DONE[DSA].get(st, []):
                    i = g - G_BG[0]
                    o = unit_full(dve, g)[:, :].rearrange("p (k t) -> p k t", k=2)
                    V.tensor_tensor(o, o, ybc[:, 2 * i:2 * i + 2, :], ALU.mult).then_inc(bg_ready, 1)
                    dve.wait_ge(yb_hi, i + 1)
                    V.tensor_tensor(yl[:, 4 + 2 * i:6 + 2 * i, :], o, yh[:, 4 + 2 * i:6 + 2 * i, :].bitcast(F32),
                                    ALU.subtract).then_inc(unit_free(g), 1)
                for a in ADA_ATT.get(st, []):
                    modulation_half(a, bank[3][:, :])

            attention(DSA, dsa_between)
            mod_rows(0, 0)
            dve.wait_ge(x_in, 16)

            def later_modulation(j):
                for a in ADA_OUT[j]:
                    modulation_half(a, bank[3][:, :])

            mixer_residual(G_EO, 0, later_modulation)
            layer_norm(0, 0)
            mod_columns(0, (1,))
            h_columns(1, modT[:, 0, 24:32], modT[:, 0, 16:24])
            mod_rows(0, 1)
            ffn(0)
            layer_norm(1, 1)
            mod_columns(1, (0, 1))
            h_columns(2, modT[:, 1, 8:16], modT[:, 1, 0:8])
            for a in (46, 47):
                modulation_half(a, bank[7][:, :])
            mod_rows(1, 0)
            dve.wait_ge(lat_sq, 4)
            link(V.tensor_scalar(var[:, 0:2], sqs[:, 0:2], 1.0 / Q_LORA, RMS_EPS, ALU.mult, ALU.add))
            V.tensor_scalar(var[:, 2:4], sqs[:, 2:4], 1.0 / KV_LORA, RMS_EPS, ALU.mult, ALU.add).then_inc(var_ready, 1)
            dve.wait_ge(rstd_ready, 3)
            for tt in range(TT):
                V.tensor_scalar(latn[:, tt, 0:Q_LORA], zrow[:, tt, 0:Q_LORA], rstd[:, tt:tt + 1], None, ALU.mult)
                ins = V.tensor_scalar(latn[:, tt, Q_LORA:640], zrow[:, tt, Q_LORA:640], rstd[:, 2 + tt:3 + tt], None, ALU.mult)
            ins.then_inc(lat_norm, 1)

            def lat_columns(i, k0, k1):
                o = full(dve, f"latT{i}")
                for kt in range(k0, k1):
                    gain = q_gain[:, kt:kt + 1] if kt < 3 else kv_gain[:, kt - 3:kt - 2]
                    c = S * (kt - k0)
                    ins = V.tensor_scalar(lat_f[:, 512 * (i % 2) + c:512 * (i % 2) + c + S], o[:, c:c + S], gain, None, ALU.mult)
                    if kt < k1 - 1:
                        link(ins)
                ins.then_inc(free(f"latT{i}"), 1)

            def lat_low(i, k0, k1):
                dve.wait_ge(lat_hi, i + 1)
                n = k1 - k0
                V.tensor_tensor(lat_l[:, k0:k1, :], lat_f[:, 512 * (i % 2):512 * (i % 2) + S * n]
                                .rearrange("p (k t) -> p k t", k=n), lat_h[:, k0:k1, :].bitcast(F32), ALU.subtract
                                ).then_inc(lat_lo, 1)

            lat_columns(0, 0, 2)
            lat_columns(1, 2, 4)
            lat_low(0, 0, 2)
            dve.wait_ge(lat_lo, 1)
            lat_columns(2, 4, 5)
            lat_low(1, 2, 4)
            lat_low(2, 4, 5)
            mod_rows(1, 1)

            def rotate(src, dst, heads, tt):
                cos, sin = (C("rope")[:, 32 * tt + 16 * i:32 * tt + 16 * i + 16].unsqueeze(1).to_broadcast([P, heads, 16])
                            for i in range(2))
                x1, x2 = src[:, :, 0:16], src[:, :, 16:32]
                a, b = (r[:, 0:heads * 16].rearrange("p (h c) -> p h c", h=heads) for r in rt)
                link(V.tensor_tensor(a, x1, cos, ALU.mult))
                link(V.tensor_tensor(b, x2, sin, ALU.mult))
                link(V.tensor_tensor(dst[:, :, 0:16], a, b, ALU.subtract))
                link(V.tensor_tensor(a, x2, cos, ALU.mult))
                link(V.tensor_tensor(b, x1, sin, ALU.mult))
                return V.tensor_tensor(dst[:, :, 16:32], a, b, ALU.add)

            for tt in range(TT):
                ins = rotate(zrow[:, tt, 640:672].unsqueeze(1).to_broadcast([P, 4, D_ROPE]),
                             krot[:, tt, :].rearrange("p (h c) -> p h c", h=4), 4, tt)
                if tt == 0:
                    link(ins)
            ins.then_inc(rot_ready, 1)
            dve.wait_ge(rot_ready, 1)
            for g in G_U:
                unit_evacuated(dve, g)
            for gi, win in enumerate(WINDOWS):
                src, w, n = upad[:, gi, :], 1, 0
                while w < win:
                    dst = pp[n % 2]
                    link(V.tensor_tensor(dst[:, PAD:PAD + S], src[:, PAD:PAD + S], src[:, PAD - w:PAD + S - w], ALU.add))
                    src, w, n = dst, 2 * w, n + 1
                u = upad[:, gi, :]
                link(V.scalar_tensor_tensor(pooled[:, gi, PAD:S], src[:, 2 * PAD:PAD + S], 1.0 / win, u[:, 2 * PAD:PAD + S],
                                            ALU.mult, ALU.subtract))
                link(V.tensor_tensor(pooled[:, gi, 0:PAD], src[:, PAD:2 * PAD], C("rcount")[:, PAD * gi:PAD * (gi + 1)], ALU.mult))
                ins = V.tensor_tensor(pooled[:, gi, 0:PAD], pooled[:, gi, 0:PAD], u[:, PAD:2 * PAD], ALU.subtract)
                if gi < 3:
                    link(ins)
            ins.then_inc(pool_ready, 1)
            unit_evacuated(dve, G_QR)
            for tt in range(TT):
                ins = rotate(qrow[:, tt, :].rearrange("p (h c) -> p h c", h=HEADS),
                             qrot[:, tt, :].rearrange("p (h c) -> p h c", h=HEADS), HEADS, tt)
                if tt == 0:
                    link(ins)
            ins.then_inc(rot_ready, 1)
            dve.wait_ge(lat_lo, 3)
            for i in range(2):
                o = full(dve, f"pool{i}")
                for j in range(2):
                    ins = V.tensor_scalar(lat_f[:, 512 * i + S * j:512 * i + S * (j + 1)], o[:, S * j:S * (j + 1)],
                                          pool_scale[:, 2 * i + j:2 * i + j + 1], None, ALU.mult)
                    if j == 0:
                        link(ins)
                ins.then_inc(free(f"pool{i}"), 1)
            for i in range(2):
                dve.wait_ge(pool_hi, i + 1)
                V.tensor_tensor(yl[:, 2 * i:2 * i + 2, :], lat_f[:, 512 * i:512 * i + 512].rearrange("p (k t) -> p k t", k=2),
                                yh[:, 2 * i:2 * i + 2, :].bitcast(F32), ALU.subtract).then_inc(pool_lo, 1)
            attention(MLA)
            mixer_residual(G_OO, 0)
            layer_norm(3, 2)
            h_columns(3, modT[:, 1, 24:32], modT[:, 1, 16:24])
            ffn(1)
            layer_norm(4, 3)
            rms_rows(5, D ** 0.5)
            h_columns(4, mix_gain, None)
            o = unit_full(dve, G_F)
            dve.wait_ge(stage_in, 16 * len(STAGED))
            V.tensor_scalar(f_t[0], o[0:8, 0:S], bfor, None, ALU.add).then_inc(unit_free(G_F), 1)
            dve.wait_ge(f_log, 1)
            link(V.scalar_tensor_tensor(f_t[2], f_t[0], 0.0, f_t[1], ALU.min, ALU.subtract))
            link(V.tensor_tensor_scan(f_t[3], ones[0:8, 0:1].to_broadcast([8, S]), f_t[2], 0.0, ALU.mult, ALU.add))
            V.tensor_scalar(f_t[1], f_t[3], -1.0, None, ALU.mult).then_inc(c_ready, 1)
            o = full(dve, "ccol")
            V.tensor_scalar(ccol, o[:, 0:16].rearrange("p (t h) -> p t h", t=TT), -1.0, None, ALU.mult).then_inc(free("ccol"), 1)
            evacuated(dve, "ccol")
            attention(FOX)
            attention(MOBA)
            for st in range(HEADS + 2):
                if st < HEADS:
                    h = st
                    o = full(dve, ("z", h))
                    if h >= 2:
                        evacuated(dve, ("sfx", h - 2))
                    V.tensor_tensor(zm[h % 2], o[:, 0:384], C("past_T"), ALU.add).then_inc(z_ready, 1)
                    dve.wait_ge(soft_log, h + 1)
                    if h >= 2:
                        full(dve, ("sfx", h - 2))
                    V.scalar_tensor_tensor(sp[h % 2], zm[h % 2], 0.0, o[:, 0:384], ALU.max, ALU.add
                                           ).then_inc(free(("z", h)), 1)
                if 1 <= st <= HEADS:
                    h = st - 1
                    o = full(dve, ("sfx", h))
                    if h >= 2:
                        dve.wait_ge(pv_done, att_count("stick", h) - 2)
                    V.tensor_tensor(wT[h % 2], zm[h % 2], o[:, 0:384], ALU.subtract).then_inc(free(("sfx", h)), 1)
                if st >= 2 and st % 2 == 1:
                    out_low("stick", (st - 2) // 2)
            for c in range(4):
                for i, n in enumerate(BRANCHES):
                    g = G_LIFT[c, n]
                    o = unit_full(dve, g)[:, :].rearrange("p (k t) -> p k t", k=2)
                    dve.wait_ge(gate_ready, 3 * c + i + 1)
                    gate = gates[:, 8 * n + 2 * c:8 * n + 2 * c + 2, :]
                    if i == 0:
                        V.tensor_tensor(mixed, o, gate, ALU.mult).then_inc(unit_free(g), 1)
                        continue
                    link(V.tensor_tensor(o, o, gate, ALU.mult))
                    if i == 1:
                        unit_evacuated(dve, G_LIFT[c, BRANCHES[0]])
                        V.tensor_tensor(mixed, mixed, o, ALU.add).then_inc(unit_free(g), 1)
                        unit_evacuated(dve, g)
                    else:
                        V.tensor_tensor(o, mixed, o, ALU.add).then_inc(mix_ready, 1)
                        dve.wait_ge(mix_hi, c + 1)
                        V.tensor_tensor(hl[:, 2 * c:2 * c + 2, :], o, hh[:, 2 * c:2 * c + 2, :].bitcast(F32), ALU.subtract
                                        ).then_inc(unit_free(g), 1)
            mixer_residual(G_WO, None)
            rms_rows(6, 1.0)
            h_columns(5, mlp_gain, None)
            ffn(2)
            dve.wait_ge(rstd_ready, 8)
            dve.wait_ge(ln_in, 32 * 4 + 16)
            for tt in range(TT):
                V.scalar_tensor_tensor(xn[:, tt, :], x[:, tt, :], rstd[:, tt:tt + 1], lnrow[:, 0, :], ALU.mult, ALU.mult
                                       ).then_inc(row_ready, 1)


_INS = ["x", "c", "ada_w", "ada_b", "ln_mix_g", "ln_mix_b", "ln_ffn_g", "ln_ffn_b", "ev_w_in", "ev_conv_w", "ev_w_out",
        "od_w_in", "pool_w", "pool_scale", "q_norm_g", "w_uq", "kv_norm_g", "w_ukv", "od_w_out", "ffn_w_up", "ffn_conv_w",
        "ffn_w_down", "norm_mix_2", "w_in_2", "b_forget_2", "w_branch_2", "w_out_2", "norm_mlp_2", "w_up_2", "w_down_2",
        "norm_final_2"]


def kernel(**inputs):
    import concourse.bacc as bacc
    from concourse.bass_utils import run_bass_kernel_spmd

    nc = bacc.Bacc("TRN2", target_bir_lowering=False, num_devices=1)
    arrays, aps = {}, {}
    for name in _INS:
        a = np.ascontiguousarray(inputs[name])
        arrays[f"in_{name}"] = a
        aps[name] = nc.dram_tensor(f"in_{name}", a.shape, mybir.dt.from_np(a.dtype), kind="ExternalInput").ap()
    arrays["shape_constants"] = shape_constants()
    consts = nc.dram_tensor("shape_constants", (P, N_CONST), F32, kind="ExternalInput").ap()
    out = nc.dram_tensor("out_0", (1, S, D), F32, kind="ExternalOutput").ap()
    build(nc, aps, consts, out)
    r = run_bass_kernel_spmd(nc, [arrays], core_ids=[0])
    return r.results[0]["out_0"]
```

```python
from contextlib import ExitStack

import numpy as np
import concourse.bass as bass
from concourse import mybir

ALU = mybir.AluOpType
ACT = mybir.ActivationFunctionType
AX = mybir.AxisListType
F32 = mybir.dt.float32
F32R = mybir.dt.float32r

P = 128
S = 256
TT = S // P
D = 1024
KD = D // P
DH = 64
HEADS = 8
CHUNK = 64
TOPK = S // 4
D_FF = 2816
NB_FF = D_FF // P
D_FF2 = 4096
NB_FF2 = D_FF2 // P
Q_LORA = 384
KV_LORA = 256
D_ROPE = 32
ODD_IN = 512 + Q_LORA + KV_LORA + D_ROPE
WINDOWS = (2, 4, 8, 16)
PAD = 16
ALPHA = 4 ** 0.25
LN_EPS = 1e-5
RMS_EPS = 1e-6
SCALE = DH ** -0.5
SCALE_MLA = (64 + D_ROPE) ** -0.5
IDX_SCALE = HEADS ** -0.5 * DH ** -0.5
SLOPES = [2.0 ** (-8.0 * (h + 1) / HEADS) for h in range(HEADS)]
NEG = -1e30
BIG = 1e34
REMOVED = -3e38
UC = 256
CHUNKW = KD * UC
AC = 512
MOD_BLOCKS = 6 * D // AC

CONST_AT = {}


def shape_constants():
    t = np.arange(P)[:, None]
    s = np.arange(P)[None, :]
    zero = np.zeros((P, P), np.float32)
    causal = np.where(s <= t, 0.0, NEG)
    chunk = np.where(s // CHUNK <= t // CHUNK, 0.0, NEG)
    inv = 10000.0 ** (-np.arange(0, D_ROPE, 2, dtype=np.float32) / D_ROPE)
    ang = (np.arange(S, dtype=np.float32)[:, None] * inv[None, :].astype(np.float32)).astype(np.float32)
    cs = np.stack([np.cos(ang), np.sin(ang)], 1).reshape(TT, P, 2 * D_ROPE // 2).transpose(1, 0, 2).reshape(P, -1)
    count = np.stack([np.minimum(np.arange(PAD) + 1, w) for w in WINDOWS]).astype(np.float32)
    parts = {
        "ident": np.eye(P),
        "ones": np.ones((P, P)),
        "suffix": (t >= s).astype(np.float32),
        "past_T": np.concatenate([np.where(t < s, 0.0, NEG), zero, np.where(t < s, 0.0, NEG)], 1),
        "causal": np.concatenate([zero, causal], 1),
        "chunk": np.concatenate([zero, chunk], 1),
        "dist_chunk": np.concatenate([t - s + P, np.abs(t - s) - BIG * (chunk < 0) * -1.0], 1),
        "dist_causal": np.concatenate([t - s + P, np.where(s <= t, t - s, BIG)], 1),
        "rope": cs,
        "rcount": np.broadcast_to((1.0 / count).reshape(1, -1), (P, PAD * len(WINDOWS))),
    }
    at = 0
    cols = []
    for name, a in parts.items():
        CONST_AT[name] = (at, at + a.shape[1])
        at += a.shape[1]
        cols.append(a.astype(np.float32))
    return np.ascontiguousarray(np.concatenate(cols, 1))


N_CONST = shape_constants().shape[1]

DSA, MLA, FOX, MOBA = range(4)
ATT_SET = {DSA: 0, MLA: 0, FOX: 0, MOBA: 1}


def build(nc, W, consts, out):
    units = []

    def unit(name, src, c0, n, nkt):
        units.append(dict(name=name, width=nkt * n, n=n, nkt=nkt, src=src, c0=c0, kind="cols"))
        return len(units) - 1

    def slot(g):
        return CHUNKW // 2 * (g // 2 % 2) if units[g]["width"] <= CHUNKW // 2 and units[g]["name"] != "ffn2" else 0

    def before(g):
        a, w = slot(g), units[g]["width"]
        p = g - 2
        while p >= 0 and not (slot(p) < a + w and a < slot(p) + units[p]["width"]):
            p -= 2
        return p

    def landing(g):
        return g % 2 + 2 * (slot(g) > 0)

    ev_in, od_in, w2in = W["ev_w_in"][0], W["od_w_in"][0], W["w_in_2"][0]
    G_QI = [unit("qi", ev_in, 1536 + UC * j, UC, KD) for j in range(2)]
    G_KI = unit("ki", ev_in, 1984, 192, KD)
    G_QKV = {DSA: [unit("qkv", ev_in, UC * j, UC, KD) for j in range(6)]}
    G_CX = []
    for b in range(4):
        G_CX.append(len(units))
        units.append(dict(name="cx", width=CHUNKW, src=ev_in, c0=(2632 + P * b, 3144 + P * b), kind="pair"))
    G_BG = [unit("bg", ev_in, 2120 + UC * j, UC, KD) for j in range(2)]
    G_EO = [unit("ev_out", W["ev_w_out"][0], UC * j, UC, KD) for j in range(4)]

    def ffn_units(f, w_up, nb, half):
        g0 = len(units)
        for b in range(nb):
            if half:
                units.append(dict(name="ffn", width=CHUNKW, src=w_up, c0=(P * b, half + P * b), kind="pair"))
            else:
                units.append(dict(name="ffn2", width=KD * P, n=P, nkt=KD, src=w_up, c0=P * b, kind="cols"))
        return g0

    FFN_G0 = [ffn_units(0, W["ffn_w_up"][0], NB_FF, D_FF)]
    G_Z = [unit("z", od_in, 512, 256, KD), unit("z", od_in, 768, 256, KD), unit("z", od_in, 1024, 160, KD)]
    G_U = [unit("u", od_in, UC * j, UC, KD) for j in range(2)]
    uq = W["w_uq"][0].rearrange("k (h c) -> k h c", h=HEADS)
    ukv = W["w_ukv"][0].rearrange("k (h c) -> k h c", h=HEADS)

    def head_unit(name, src, h0, nh, c0, nc_, nkt):
        units.append(dict(name=name, width=nkt * nh * nc_, n=nh * nc_, nh=nh, hc=nc_, h0=h0, c0=c0, nkt=nkt,
                          src=src, kind="heads"))
        return len(units) - 1

    G_QN = [head_unit("qn", uq, 4 * j, 4, 0, 64, 3) for j in range(2)]
    G_QR = head_unit("qr", uq, 0, 8, 64, 32, 3)
    G_KN = [head_unit("kn", ukv, 4 * j, 4, 0, 64, 2) for j in range(2)]
    G_VV = [head_unit("vv", ukv, 4 * j, 4, 64, 64, 2) for j in range(2)]
    G_OO = [unit("od_out", W["od_w_out"][0], UC * j, UC, KD) for j in range(4)]
    FFN_G0.append(ffn_units(1, W["ffn_w_up"][1], NB_FF, D_FF))
    G_F = unit("f", w2in, 3072, P, KD)
    G_QKV[FOX] = [unit("qkv", w2in, 1536 + UC * j, UC, KD) for j in range(6)]
    G_QKV[MOBA] = [unit("qkv", w2in, 3080 + UC * j, UC, KD) for j in range(6)]
    G_QKVS = [unit("qkv", w2in, UC * j, UC, KD) for j in range(6)]
    G_GATE = [unit("gate", w2in, 4616 + UC * j, UC, KD) for j in range(12)]
    G_LIFT = {}
    BRANCHES = (1, 2, 0)
    for c in range(4):
        for n in BRANCHES:
            G_LIFT[c, n] = unit("lift", W["w_branch_2"][0, n], UC * c, UC, 4)
    G_WO = [unit("out2", W["w_out_2"][0], UC * j, UC, KD) for j in range(4)]
    FFN_G0.append(ffn_units(2, W["w_up_2"][0], NB_FF2, 0))
    NU = len(units)
    FFN_NB = [NB_FF, NB_FF, NB_FF2]
    FFN_D0 = [0, NB_FF, 2 * NB_FF]
    FFN_DOWN = [W["ffn_w_down"][0], W["ffn_w_down"][1], W["w_down_2"][0]]

    turns = {}
    used, filled = [0] * 8, [0] * 8

    def turn(name, bank):
        filled[bank] += name[0] != "pv" and not (name[0] == "acc" and name[2] == 3)
        turns[name] = (bank, used[bank], filled[bank])
        used[bank] += 1

    def att_turns(a):
        for h in range(HEADS):
            turn(("score", a, h), h % 4)
            turn(("tr", a, h), h % 4)
            if h % 2 == 0:
                turn(("pv", a, h // 2), 6 + h // 2 % 2)

    turn("cond", 6)
    turn("stage", 6)
    turn(("modc", 0, 0), 6)

    def ht_turns(n):
        for q in range(4):
            turn(("ht", n, q), q)

    def ffn_turns(f):
        for i in range(4):
            turn(("acc", f, i), i)

    ht_turns(0)
    for h in range(HEADS):
        turn(("idx", h), h % 3)
    turn("wi", 6)
    att_turns(DSA)
    for half in range(2):
        turn(("modr", 0, 0, half), half)
    turn(("modc", 0, 1), 2)
    ht_turns(1)
    ffn_turns(0)
    turn(("modc", 1, 0), 7)
    ht_turns(2)
    for half in range(2):
        turn(("modr", 1, 0, half), half)
    turn("latT0", 0)
    turn("latT1", 1)
    turn("latT2", 6)
    turn("qrT", 7)
    turn("krT", 6)
    att_turns(MLA)
    turn(("modc", 1, 1), 7)
    ht_turns(3)
    ffn_turns(1)
    ht_turns(4)
    turn("ccol", 6)
    att_turns(FOX)
    att_turns(MOBA)
    for st in range(HEADS + 2):
        if st < HEADS:
            turn(("z", st), st % 2)
        if 1 <= st <= HEADS:
            turn(("sfx", st - 1), 2 + (st - 1) % 2)
        if st >= 2 and st % 2 == 0:
            turn(("pv", "stick", st // 2 - 1), 6 + (st // 2 - 1) % 2)
    ht_turns(5)
    ffn_turns(2)

    ctx = ExitStack()
    with ctx:
        def sb(name, shape, dt=F32):
            return ctx.enter_context(nc.sbuf_tensor(name, shape, dt))

        def sem(name):
            return ctx.enter_context(nc.semaphore(name))

        raw = [sb(f"raw{i}", [P, CHUNKW]) for i in range(2)]
        uh = [sb(f"unit_hi{i}", [P, CHUNKW], F32R) for i in range(2)]
        ul = [sb(f"unit_lo{i}", [P, CHUNKW], F32R) for i in range(2)]
        rawd = [sb(f"raw_down{i}", [P, D]) for i in range(2)]
        down = sb("down", [P, 2, 2, D], F32R)
        accg = sb("accg", [P, 6 * D])
        x = sb("x", [P, TT, D])
        hh = sb("h_hi", [P, KD, S], F32R)
        hl = sb("h_lo", [P, KD, S], F32R)
        hf = sb("h_full", [P, KD, S])
        yh = sb("y_hi", [P, KD, S], F32R)
        yl = sb("y_lo", [P, KD, S], F32R)
        att = sb("att", [P, 2, 3072])
        ada1 = sb("ada1", [P, CHUNKW])
        cst = sb("consts", [P, N_CONST])
        work = sb("work", [P, 3072])
        grow = sb("gate_rows", [P, 2, D])
        cols = sb("cols", [P, 512])
        small = sb("small", [P, 256])

        def C(name):
            return cst[:, CONST_AT[name][0]:CONST_AT[name][1]]

        ident, ones = C("ident"), C("ones")
        ada = [att[:, 1, 0:CHUNKW], ada1[:, :], att[:, 0, 0:CHUNKW], accg[:, 4 * D:4 * D + CHUNKW]]
        kiT = att[:, 1, 2304:2560]
        hff = hf[:, :, :].rearrange("p k t -> p (k t)")
        qiT = hf[:, 0:4, :]
        ybc = hf[:, 0:4, :]

        def qT(a):
            return att[:, a, 0:1024].rearrange("p (b t) -> p b t", b=4)

        def kT(a):
            return att[:, a, 1024:2048].rearrange("p (b t) -> p b t", b=4)

        def vv(a):
            return att[:, a, 2048:3072].rearrange("p (t n) -> p t n", t=TT)

        lnrow = att[:, 0, 0:2 * D].rearrange("p (a n) -> p a n", a=2)
        xn = att[:, 1, 0:TT * D].rearrange("p (t n) -> p t n", t=TT)
        mixed = att[:, 1, 0:2 * S].rearrange("p (k t) -> p k t", k=2)
        stage = [work[:, P * i:P * (i + 1)] for i in range(4)]
        stage_c = work[0:KD, 512:512 + P]
        PCOLS = 101
        ev_conv = cols[:, 0:12]
        pool_scale = cols[:, 12:16]
        q_gain = cols[:, 16:19]
        kv_gain = cols[:, 19:21]
        mix_gain = cols[:, 21:29]
        mlp_gain = cols[:, 29:37]
        modT = cols[:, 37:37 + 64].rearrange("p (l j) -> p l j", l=2)
        conv_w = [cols[:, 112:112 + 132], cols[:, 244:244 + 132]]
        cond = cols[:, 440:448]
        wiT = work[64:72, 512:768]
        cgb = [work[:, 1536:1792], work[:, 1920:2176]]
        L = [work[:, 384 * i:384 * (i + 1)] for i in range(2)]
        PT = [work[:, 768 + 384 * i:768 + 384 * (i + 1)] for i in range(2)]
        idx = work[:, 2304:2688]
        distm = work[:, 2688:3072]
        zm = [work[:, 384 * i:384 * (i + 1)] for i in range(2)]
        sig = [work[:, 768 + 384 * i:768 + 384 * (i + 1)] for i in range(2)]
        sp = [work[:, 1536 + 384 * i:1536 + 384 * (i + 1)] for i in range(2)]
        wT = [work[:, 2304 + 384 * i:2304 + 384 * (i + 1)] for i in range(2)]
        fv = [work[:, 512 * i:512 * i + 256] for i in range(2)]
        fg = [work[:, 512 * i + 256:512 * i + 512] for i in range(2)]
        acth = [yh[:, i, :] for i in range(2)]
        actl = [yl[:, i, :] for i in range(2)]
        smax = small[:, 0:16].rearrange("p (h t) -> p h t", t=2)
        sbias = small[:, 16:32].rearrange("p (h t) -> p h t", t=2)
        ssum = small[:, 32:48].rearrange("p (h t) -> p h t", t=2)
        srec = small[:, 48:64].rearrange("p (h t) -> p h t", t=2)
        wi = small[:, 64:80]
        top8 = small[:, 80:88]
        bnst = small[:, 168:216].rearrange("p (t a) -> p t a", t=2)
        mv = small[:, 112:116].rearrange("p (t a) -> p t a", t=2)
        var = small[:, 116:120]
        rstd = small[:, 120:124]
        ssq = small[:, 124:126]
        half_neg = small[:, 216:220]
        ccol = small[:, 128:144].rearrange("p (t h) -> p t h", t=2)
        bfor = small[0:8, 144:145]
        table_scratch = small[:, 152:153]
        sqs = small[:, 164:168]
        zrow = accg[:, 0:1344].rearrange("p (t n) -> p t n", t=TT)
        upad = accg[:, 1344:2432].rearrange("p (g n) -> p g n", g=4)
        pp = [accg[:, 2432:2704], accg[:, 2704:2976]]
        pooled = accg[:, 2976:4000].rearrange("p (g n) -> p g n", g=4)
        qrow = work[:, 1536:2048].rearrange("p (t n) -> p t n", t=TT)
        rt = [work[:, 2048:2176], work[:, 2176:2304]]
        qrot = work[:, 2304:2816].rearrange("p (t n) -> p t n", t=TT)
        krot = work[:, 2816:3072].rearrange("p (t n) -> p t n", t=TT)
        pool_w = ada1[:, 0:512].rearrange("p (g n) -> p g n", g=4)
        qrT = att[:, 1, 0:512].rearrange("p (b t) -> p b t", b=2)
        krT = att[:, 1, 512:768]
        sq_scr = att[:, 1, 768:768 + Q_LORA]
        latn = att[:, 1, 1152:1152 + 1280].rearrange("p (t n) -> p t n", t=TT)
        downf = down[:, :, :, :].rearrange("p a b n -> p (a b n)")
        lat_h = downf[:, 0:1280].rearrange("p (k t) -> p k t", k=5)
        lat_l = downf[:, 1280:2560].rearrange("p (k t) -> p k t", k=5)
        lat_f = hff[:, 0:4 * S]
        gates = accg[:, :].rearrange("p (k t) -> p k t", k=24)
        o_h = [yh[:, 0:4, :], yh[:, 4:8, :], downf[:, 0:1024].rearrange("p (k t) -> p k t", k=4)]
        o_l = [yl[:, 0:4, :], yl[:, 4:8, :], downf[:, 1024:2048].rearrange("p (k t) -> p k t", k=4)]
        f_t = [hf[0:8, i, :] for i in range(4)]

        bank = [ctx.enter_context(nc.psum_tensor(f"bank{i}", [P, 512], F32)) for i in range(8)]

        bank_full = [sem(f"bank_full{i}") for i in range(8)]
        bank_free = [sem(f"bank_free{i}") for i in range(8)]
        raw_in = [sem(f"raw_in{i}") for i in range(4)]
        rawd_in = [sem(f"rawd_in{i}") for i in range(2)]
        ada_in = [sem(f"ada_in{i}") for i in range(2)]
        mod_in = [sem(f"mod_in{i}") for i in range(2)]
        hi_up, lo_up, hi_dn, lo_dn = sem("hi_up"), sem("lo_up"), sem("hi_dn"), sem("lo_dn")
        down_done = sem("down_done")
        c_in, stage_in, const_in, x_in, ln_in, pw_in, out_done = (sem(n) for n in (
            "c_in", "stage_in", "const_in", "x_in", "ln_in", "pool_w_in", "out_done"))
        grow_in = [sem(f"gate_rows_in{i}") for i in range(2)]
        dve_chain, act_chain, pool_chain = sem("dve_chain"), sem("act_chain"), sem("pool_chain")
        cond_exp, ada_acc = sem("cond_exp"), sem("ada_acc")
        mod_done, mod_row, gate_rows = sem("mod_done"), sem("mod_row"), sem("gate_rows")
        row_ready, h_hi = sem("row_ready"), sem("h_hi")
        h_lo = [sem("h_lo_even"), sem("h_lo_odd")]
        var_ready, rstd_ready = sem("var_ready"), sem("rstd_ready")
        idx_relu, wi_rows, bg_ready = sem("idx_relu"), sem("wi_rows"), sem("bg_ready")
        max_ready, exp_done, pv_done, o_hi = (sem(n) for n in ("max_ready", "exp_done", "pv_done", "o_hi"))
        cg_ready, yb_hi = sem("cg_ready"), sem("yb_hi")
        tap_done, gate_done, silu_done, prod_done, act_hi, act_lo = (sem(n) for n in (
            "tap_done", "gate_done", "silu_done", "prod_done", "act_hi", "act_lo"))
        lat_sq, lat_norm, lat_hi, lat_lo = sem("lat_sq"), sem("lat_norm"), sem("lat_hi"), sem("lat_lo")
        pool_ready, pool_hi, pool_lo, rot_ready, pool_zero = (sem(n) for n in (
            "pool_ready", "pool_hi", "pool_lo", "rot_ready", "pool_zero"))
        pool_mixed, pool_scaled = sem("pool_mixed"), sem("pool_scaled")
        f_log, c_ready = sem("f_log"), sem("c_ready")
        z_ready, soft_log, w_ready = sem("z_ready"), sem("soft_log"), sem("w_ready")
        gate_ready, mix_ready, mix_hi = sem("gate_ready"), sem("mix_ready"), sem("mix_hi")

        ATT_N = {DSA: 0, MLA: 1, FOX: 2, MOBA: 3, "stick": 4}

        ATT_OUT = {DSA: (yh[:, 0:4, :], yl[:, 0:4, :]), MLA: (yh[:, 4:8, :], yl[:, 4:8, :]),
                   FOX: (o_h[1], o_l[1]), MOBA: (o_h[2], o_l[2]), "stick": (o_h[0], o_l[0])}

        def att_count(a, h):
            return HEADS * ATT_N[a] + h + 1

        def full(eng, name):
            b, _, k = turns[name]
            eng.wait_ge(bank_full[b], k)
            return bank[b]

        def evacuated(eng, name):
            b, k, _ = turns[name]
            eng.wait_ge(bank_free[b], k + 1)

        def free(name):
            return bank_free[turns[name][0]]

        def unit_full(eng, g):
            eng.wait_ge(bank_full[4 + g % 2], g // 2 + 1)
            return bank[4 + g % 2]

        def unit_evacuated(eng, g):
            eng.wait_ge(bank_free[4 + g % 2], g // 2 + 1)

        def unit_free(g):
            return bank_free[4 + g % 2]

        class Chain:

            def __init__(self, eng, semaphore):
                self.eng, self.sem, self.base, self.k = eng, semaphore, 0, 0

            def mark(self, ins):
                self.k += 1
                ins.then_inc(self.sem, 1)
                return self.k

            def need(self, k):
                self.eng.wait_ge(self.sem, self.base + k)

            def __call__(self, ins):
                self.need(self.mark(ins))

            def enter(self, i, first, per):
                self.start = self.base + self.k
                self.base, self.k = i * per + (self.start - first * per), 0

            def leave(self, iterations, per):
                assert self.k == per, (self.k, per)
                self.base, self.k = self.start + iterations * per, 0

        FILL = {DSA: {1: [(G_BG[0], 0)], 2: [(G_BG[0], 1)], 3: [(G_BG[1], 0)], 4: [(G_BG[1], 1)]}, MLA: {0: [(None, 0)], 1: [(None, 1)]}}
        for a, fill in ((FOX, G_QKV[MOBA]), (MOBA, G_QKVS)):
            halves = [(g, part) for g in fill for part in range(2)]
            FILL[a] = {st: [halves[st + 1]] for st in range(HEADS + 2)}
            FILL[a][0] = halves[:2]
            FILL[a][HEADS + 1] = halves[-2:]
        FILL["stick"] = {i: [(G_GATE[i], 0), (G_GATE[i], 1)] for i in range(10)}
        DONE = {a: {st + 2 * (a == DSA): [g for g, part in fill if g is not None and part == 1] for st, fill in f.items()}
                for a, f in FILL.items()}
        MOD_PE = (2, 3)
        MOD_START = 2 * MOD_PE[0]
        SUM_FIRST = [4, 5]
        SUM_IDX = {0: [6], 2: [7], 4: [8], 6: [9]}
        SUM_CONV = [10, 11]
        SUM_EVEN = [12, 13, 14, 15]
        MOD_FFN = 16
        SUM_AFTER = [MOD_FFN + NB_FF, MOD_FFN + NB_FF + 1]
        MOD_FFN1 = MOD_FFN + NB_FF + 2

        def half_at(a):
            a += 2 * len(MOD_PE) if a >= MOD_START else 0
            return a // (2 * MOD_BLOCKS), a // 2 % MOD_BLOCKS, a % 2

        def block_at(layer, j):
            i = (j + 2 * layer) % MOD_BLOCKS if layer or j < MOD_BLOCKS - 2 else j - (MOD_BLOCKS - 2)
            return slice(AC * i, AC * (i + 1))

        def summed(eng, layer, j):
            n = 2 * (MOD_BLOCKS * layer + j + 1)
            eng.wait_ge(ada_acc, n if n <= MOD_START else n - 2 * len(MOD_PE))

        block = ctx.enter_context(nc.Block())

        def rows(a):
            return a.rearrange("a (b n) -> (a b) n", n=P)

        STAGED = [(stage[0][0:12, :], rows(W["ev_conv_w"][0])), (stage[0][12:16, :], rows(W["pool_scale"])),
                  (stage[0][16:19, :], rows(W["q_norm_g"])), (stage[0][19:21, :], rows(W["kv_norm_g"])),
                  (stage[0][21:29, :], rows(W["norm_mix_2"])), (stage[0][29:37, :], rows(W["norm_mlp_2"])),
                  (stage[1], rows(W["ffn_conv_w"][0])[0:P, :]), (stage[2], rows(W["ffn_conv_w"][1])[0:P, :]),
                  (stage[3][0:4, :], rows(W["ffn_conv_w"][0])[P:132, :]),
                  (stage[3][4:8, :], rows(W["ffn_conv_w"][1])[P:132, :]),
                  (bfor, W["b_forget_2"].rearrange("a n -> n a"))]
        for layer in range(2):
            for part in range(2):
                r0, at = 24 * part, 37 + 32 * layer + 16 * part
                STAGED.append((stage[0][at:at + 16, :], rows(W["ada_b"][layer:layer + 1, P * r0:P * (r0 + 16)])))

        def ada_half(a):
            return half_of(*half_at(a))

        def half_of(layer, j, half):
            return W["ada_w"][layer][AC * half:AC * (half + 1), AC * j:AC * (j + 1)].rearrange("(t p) n -> p t n", p=P)

        def load_gates(eng, layer, w):
            eng.dma_start(grow[:, w, :], W["ada_b"][layer:layer + 1, (3 * w + 2) * D:(3 * w + 3) * D]
                          .partition_broadcast(P)).then_inc(grow_in[layer], 16)

        @block.sync
        def _(sp_):
            def load_unit(g):
                u, s, at, landed = units[g], g % 2, slot(g), raw_in[landing(g)]
                if before(g) >= 0:
                    sp_.wait_ge(lo_up, before(g) + 1)
                if u["kind"] == "pair":
                    dst = raw[s][:, :].rearrange("p (t a n) -> p t a n", t=KD, a=2)
                    for a in range(2):
                        src = u["src"][:, u["c0"][a]:u["c0"][a] + P].rearrange("(t p) n -> p t n", p=P)
                        sp_.dma_start(dst[:, :, a, :], src).then_inc(landed, 16)
                elif u["kind"] == "heads":
                    nkt, n = u["nkt"], u["n"]
                    for t in range(nkt):
                        dst = raw[s][:, at + t * n:at + (t + 1) * n].rearrange("p (h c) -> p h c", h=u["nh"])
                        src = u["src"][t * P:(t + 1) * P, u["h0"]:u["h0"] + u["nh"], u["c0"]:u["c0"] + u["hc"]]
                        sp_.dma_start(dst, src).then_inc(landed, 16)
                else:
                    nkt, n = u["nkt"], u["n"]
                    dst = raw[s][:, at:at + nkt * n].rearrange("p (t n) -> p t n", t=nkt)
                    src = u["src"][:, u["c0"]:u["c0"] + n].rearrange("(t p) n -> p t n", p=P)
                    m = nkt // 2
                    for a, b in ((0, m), (m, nkt)):
                        sp_.dma_start(dst[:, a:b, :], src[:, a:b, :]).then_inc(landed, 16)

            def load_mod(e):
                if e >= 2:
                    sp_.wait_ge(mod_done, e - 1)
                s = e % 2
                sp_.dma_start(ada[2 + s].rearrange("p (t n) -> p t n", t=KD // 2), half_of(0, MOD_PE[e // 2], s)
                              ).then_inc(mod_in[s], 16)

            def load_ada(a):
                s = a % 2
                if a >= 2:
                    sp_.wait_ge(ada_acc, a - 1)
                sp_.dma_start(ada[s].rearrange("p (t n) -> p t n", t=KD // 2), ada_half(a)).then_inc(ada_in[s], 16)

            sp_.dma_start(stage_c, W["c"].rearrange("a (b n) -> (a b) n", n=P)).then_inc(c_in, 16)
            i0, i1 = CONST_AT["ident"][0], CONST_AT["ones"][1]
            sp_.dma_start(cst[:, i0:i1], consts[:, i0:i1]).then_inc(c_in, 16)
            for a in range(MOD_START):
                load_ada(a)
                load_mod(a)
                if a == MOD_START - 2:
                    sp_.dma_start(x[:, :, :], W["x"][0].rearrange("(t p) n -> p t n", p=P)).then_inc(x_in, 16)
            for g in range(2):
                load_unit(g)
            for a in SUM_FIRST:
                load_ada(a)
            for g in range(2, G_QKV[DSA][2]):
                load_unit(g)
            for h in range(HEADS):
                if h % 2 == 0:
                    load_unit(G_QKV[DSA][2 + h // 2])
                for a in SUM_IDX.get(h, []):
                    load_ada(a)
            for i, g in enumerate(G_CX + G_BG):
                load_unit(g)
                if i < 2:
                    load_ada(SUM_CONV[i])
            for a in SUM_EVEN[:2]:
                load_ada(a)
            for g in G_EO:
                load_unit(g)
            for a in SUM_EVEN[2:]:
                load_ada(a)
            for k in range(2):
                load_unit(FFN_G0[0] + k)

            def load_up(f, b, i, k):
                g0 = FFN_G0[f]
                s, u = (g0 + k) % 2, units[g0]
                sp_.wait_ge(lo_up, b + (g0 - 1))
                if u["kind"] == "pair":
                    dst = raw[s][:, :].rearrange("p (t a n) -> p t a n", t=KD, a=2)
                    for a in range(2):
                        src = u["src"][:, bass.ds(b * P + a * D_FF, P)].rearrange("(t p) n -> p t n", p=P)
                        sp_.dma_start(dst[:, :, a, :], src).then_inc(raw_in[s], 16)
                else:
                    dst = raw[s][:, 0:KD * P].rearrange("p (t n) -> p t n", t=KD)
                    for a in range(2):
                        src = u["src"][a * 512:(a + 1) * 512, bass.ds(b * P, P)].rearrange("(t p) n -> p t n", p=P)
                        sp_.dma_start(dst[:, 4 * a:4 * a + 4, :], src).then_inc(raw_in[s], 16)

            def load_down(f, b, k):
                d0 = FFN_D0[f]
                if not (isinstance(b, int) and d0 + b < 2):
                    sp_.wait_ge(lo_dn, b + (d0 - 1))
                sp_.dma_start(rawd[k][:, :], FFN_DOWN[f][bass.ds(b * P, P), :]).then_inc(rawd_in[k], 16)

            def load_all_ffn(f):
                if f == 0:
                    load_ada(MOD_FFN)
                if f == 1:
                    sp_.wait_ge(pv_done, att_count(MLA, HEADS - 1))
                    load_ada(MOD_FFN1)
                if f > 0:
                    for k in range(2):
                        load_up(f, k, 0, k)
                load_down(f, 0, 0)
                with sp_.Fori(1, FFN_NB[f] // 2) as i:
                    for k in range(2):
                        load_up(f, 2 * i + k, i, k)
                        load_down(f, 2 * i + (k - 1), 1 - k)
                load_down(f, FFN_NB[f] - 1, 1)

            load_all_ffn(0)
            for g in G_Z[:2]:
                load_unit(g)
            load_ada(SUM_AFTER[1])
            for g in G_Z[2:] + G_U:
                load_unit(g)
            for g in G_QN:
                load_unit(g)
            sp_.wait_ge(ada_acc, SUM_AFTER[1] + 1)
            sp_.dma_start(pool_w, W["pool_w"][0].rearrange("g c d -> c g d")).then_inc(pw_in, 16)
            for g in [G_QR] + G_KN + G_VV + G_OO:
                load_unit(g)
            load_all_ffn(1)
            for g in range(G_F, FFN_G0[2]):
                load_unit(g)
            load_all_ffn(2)
            for tt in range(TT):
                sp_.wait_ge(row_ready, 13 + tt)
                sp_.dma_start(out[0, P * tt:P * (tt + 1), :], xn[:, tt, :]).then_inc(out_done, 16)
            sp_.wait_ge(out_done, 16 * TT)

        raw_loads = [0] * len(raw_in)
        raw_need = []
        for g, u in enumerate(units):
            raw_loads[landing(g)] += 16 * (u["nkt"] if u["kind"] == "heads" else 2)
            raw_need.append(raw_loads[landing(g)])

        @block.gpsimd
        def _(pool):
            def lo_unit(g):
                if g >= NU:
                    return
                pool.wait_ge(hi_up, g + 1)
                w = slice(slot(g), slot(g) + units[g]["width"])
                nc.gpsimd.tensor_tensor(ul[g % 2][:, w], raw[g % 2][:, w], uh[g % 2][:, w].bitcast(F32),
                                        ALU.subtract).then_inc(lo_up, 1)

            def lo_down(d):
                pool.wait_ge(hi_dn, d + 1)
                s = d % 2
                nc.gpsimd.tensor_tensor(down[:, s, 1, :], rawd[s][:, :], down[:, s, 0, :].bitcast(F32),
                                        ALU.subtract).then_inc(lo_dn, 1)

            def power(n, src, w, eps):
                pool.wait_ge(var_ready, n + 1)
                nc.gpsimd.tensor_scalar(rstd[:, 0:w], src, eps, None, ALU.add).then_inc(pool_chain, 1)
                pool.wait_ge(pool_chain, n + 2)
                nc.gpsimd.tensor_tensor(rstd[:, 0:w], rstd[:, 0:w], half_neg[:, 0:w], ALU.pow).then_inc(rstd_ready, 1)

            def h_low(n):
                for q in (0, 2):
                    pool.wait_ge(h_hi, 4 * n + q + 1)
                    k = slice(2 * q, 2 * q + 2)
                    nc.gpsimd.tensor_tensor(hl[:, k, :], hf[:, k, :], hh[:, k, :].bitcast(F32), ALU.subtract
                                            ).then_inc(h_lo[0], 1)

            def ffn(f):
                g0, d0, nb = FFN_G0[f], FFN_D0[f], FFN_NB[f]
                w = units[g0]["width"]
                lo_down(d0)

                def body(i, k):
                    b = 2 * i + k
                    s = (g0 + k) % 2
                    pool.wait_ge(hi_up, b + (g0 + 3))
                    nc.gpsimd.tensor_tensor(ul[s][:, 0:w], raw[s][:, 0:w], uh[s][:, 0:w].bitcast(F32),
                                            ALU.subtract).then_inc(lo_up, 1)
                    pool.wait_ge(hi_dn, b + (d0 + 2))
                    nc.gpsimd.tensor_tensor(down[:, 1 - k, 1, :], rawd[1 - k][:, :], down[:, 1 - k, 0, :].bitcast(F32),
                                            ALU.subtract).then_inc(lo_dn, 1)

                with pool.Fori(0, nb // 2 - 1) as i:
                    for k in range(2):
                        body(i, k)
                lo_unit(g0 + nb)
                lo_down(d0 + nb - 1)

            nc.gpsimd.memset(half_neg, -0.5).then_inc(pool_chain, 1)
            for dst, src in STAGED:
                pool.dma_start(dst, src).then_inc(stage_in, 16)
            lo_unit(0)
            lo_unit(1)
            i1 = CONST_AT["ones"][1]
            pool.dma_start(cst[:, i1:], consts[:, i1:]).then_inc(const_in, 16)
            for w in range(2):
                load_gates(pool, 0, w)
            for g in range(2, G_EO[-1] + 2):
                lo_unit(g)
            power(0, mv[:, :, 1], 2, LN_EPS)
            lo_unit(G_EO[-1] + 2)
            h_low(1)
            ffn(0)
            power(1, mv[:, :, 1], 2, LN_EPS)
            lo_unit(G_Z[1])
            h_low(2)
            for g in range(G_Z[0] + 2, G_U[-1]):
                lo_unit(g)
            evacuated(pool, ("modr", 1, 0, 1))
            for pad in (upad[:, :, 0:PAD], pp[0][:, 0:PAD], pp[1][:, 0:PAD]):
                nc.gpsimd.memset(pad, 0.0).then_inc(pool_zero, 1)
            power(2, var, 4, RMS_EPS)
            lo_unit(G_U[-1])
            for g in range(G_Z[-1] + 3, G_OO[-1] + 2):
                lo_unit(g)
            power(3, mv[:, :, 1], 2, LN_EPS)
            lo_unit(G_OO[-1] + 2)
            h_low(3)
            ffn(1)
            power(4, mv[:, :, 1], 2, LN_EPS)
            lo_unit(G_F + 1)
            power(5, ssq, 2, D * RMS_EPS)
            h_low(4)
            for g in range(G_F + 2, G_WO[-1] + 2):
                lo_unit(g)
            power(6, var[:, 0:2], 2, RMS_EPS)
            lo_unit(G_WO[-1] + 2)
            h_low(5)
            ffn(2)
            power(7, var[:, 0:2], 2, RMS_EPS)

        @block.scalar
        def _(act):
            link = Chain(act, act_chain)

            def hi_unit(g):
                if g >= NU:
                    return
                s, w = g % 2, slice(slot(g), slot(g) + units[g]["width"])
                act.wait_ge(raw_in[landing(g)], raw_need[g])
                if before(g) >= 0:
                    act.wait_ge(bank_full[4 + s], before(g) // 2 + 1)
                nc.scalar.activation(uh[s][:, w], raw[s][:, w], ACT.Copy).then_inc(hi_up, 1)

            def hi_down(d):
                s = d % 2
                act.wait_ge(rawd_in[s], 16 * (d // 2 + 1))
                if d >= 2:
                    act.wait_ge(down_done, d - 1)
                nc.scalar.activation(down[:, s, 0, :], rawd[s][:, :], ACT.Copy).then_inc(hi_dn, 1)

            def h_high(n, columns, scale, shift):
                evacuated(act, columns)
                def whole(q):
                    o = full(act, ("ht", n, q))
                    for i in range(2):
                        kt = 2 * q + i
                        dst, src = hf[:, kt, :], o[:, S * i:S * (i + 1)]
                        if shift is None:
                            ins = nc.scalar.activation(dst, src, ACT.Copy, scale=scale[:, kt:kt + 1])
                        else:
                            ins = nc.scalar.activation(dst, src, ACT.Identity, scale=scale[:, kt:kt + 1],
                                                       bias=shift[:, kt:kt + 1])
                    ins.then_inc(free(("ht", n, q)), 1)

                def high(q):
                    evacuated(act, ("ht", n, q))
                    k = slice(2 * q, 2 * q + 2)
                    nc.scalar.activation(hh[:, k, :], hf[:, k, :], ACT.Copy).then_inc(h_hi, 1)

                whole(1)
                high(0)
                high(1)
                whole(3)
                high(2)
                high(3)

            def evac(g, dst, scale=1.0, then=True):
                b = unit_full(act, g)
                nc.scalar.activation(dst, b[:, :].rearrange("p (k t) -> p k t", k=2), ACT.Copy, scale=scale
                                     ).then_inc(unit_free(g), 1)
                if then:
                    hi_unit(g + 2)

            def evac_qkv(g, a, j):
                evac(g, qT(a)[:, 2 * j:2 * j + 2, :] if j < 2 else kT(a)[:, 2 * j - 4:2 * j - 2, :] if j < 4
                     else vv(a)[:, :, UC * (j - 4):UC * (j - 3)], SCALE if j < 2 else 1.0)

            def other(g):
                unit_full(act, g)
                hi_unit(g + 2)

            def exps(a, h):
                act.wait_ge(max_ready, att_count(a, h))
                b = bank[turns["score", a, h][0]]
                for tt, (c0, n) in enumerate(((0, P), (P, S))):
                    ins = nc.scalar.activation(b[:, c0:c0 + n], b[:, c0:c0 + n], ACT.Exp, bias=sbias[:, h, tt:tt + 1],
                                               accum_out=ssum[:, h, tt:tt + 1])
                ins.then_inc(exp_done, 1)

            def evac_pt(a, h):
                b = full(act, ("tr", a, h))
                if att_count(a, h) > 2:
                    act.wait_ge(pv_done, att_count(a, h) - 2)
                nc.scalar.activation(PT[h % 2], b[:, 0:384], ACT.Copy).then_inc(free(("tr", a, h)), 1)

            def out_high(a, p):
                act.wait_ge(pv_done, att_count(a, 2 * p + 1))
                b = bank[turns["pv", a, p][0]]
                nc.scalar.activation(ATT_OUT[a][0][:, p, :], b[:, 0:256], ACT.Copy).then_inc(o_hi, 1)

            def attention(a, filler):
                for st in range(HEADS + 2):
                    if st < HEADS:
                        exps(a, st)
                    if 1 <= st <= HEADS:
                        evac_pt(a, st - 1)
                    if st >= 4 and st % 2 == 0:
                        out_high(a, (st - 4) // 2)
                    for g in DONE[a].get(st, []):
                        filler(g)
                out_high(a, HEADS // 2 - 1)

            def load_rows(a, *srcs):
                for i, src in enumerate(srcs):
                    act.dma_start(lnrow[:, i, :], src.partition_broadcast(P)).then_inc(ln_in, 16)

            def ffn(f):
                g0, d0, nb = FFN_G0[f], FFN_D0[f], FFN_NB[f]
                w = units[g0]["width"]
                half = units[g0]["kind"] == "pair"
                act0 = sum(FFN_NB[:f])
                hi_down(d0)

                def body(i, k, fixed):
                    b, s = 2 * i + k, (g0 + k) % 2
                    prod = bank[6][:, S * k:S * (k + 1)]

                    def act_high():
                        nc.scalar.activation(acth[k], prod, ACT.Copy).then_inc(act_hi, 1)

                    act.wait_ge(bank_full[4 + s], i + ((g0 + k) // 2 + 1))
                    if half:
                        cw = conv_w[f]
                        nc.scalar.activation(fv[k], bank[4 + s][:, 0:256], ACT.Copy,
                                             scale=cw[:, bass.ds(b + 2 * 44, 1)])
                        nc.scalar.activation(fg[k], bank[4 + s][:, 256:512], ACT.Copy,
                                             scale=cw[:, bass.ds(b + (2 * 44 + 22), 1)]).then_inc(tap_done, 1)
                    else:
                        nc.scalar.activation(fv[k], bank[4 + s][:, 0:256], ACT.Relu).then_inc(tap_done, 1)
                        act.wait_ge(bank_free[4 + s], i + ((g0 + k) // 2 + 1))
                        act_high()
                    last = fixed and b == nb - 1
                    if last:
                        pass
                    elif fixed:
                        hi_unit(g0 + b + 2)
                    else:
                        act.wait_ge(raw_in[s], i * 32 + (raw_need[g0 + k] + 32))
                        nc.scalar.activation(uh[s][:, 0:w], raw[s][:, 0:w], ACT.Copy).then_inc(hi_up, 1)
                    if half:
                        act.wait_ge(gate_done, b + (act0 + 1))
                        if not (fixed and act0 + b == 0):
                            act.wait_ge(act_lo, b + act0)
                        nc.scalar.activation(prod, fg[k], ACT.Silu).then_inc(silu_done, 1)
                        if f == 0 or b < 3 and fixed:
                            act.wait_ge(ada_acc, b + (MOD_FFN, MOD_FFN1)[f])
                            act.dma_start(ada[1 - k].rearrange("p (t n) -> p t n", t=KD // 2),
                                          ada_half((MOD_FFN, MOD_FFN1)[f] + b + 1) if fixed else
                                          W["ada_w"][1][AC * (1 - k):AC * (2 - k), bass.ds(i * AC + (k - 2) * AC, AC)]
                                          .rearrange("(t p) n -> p t n", p=P)).then_inc(ada_in[1 - k], 16)
                        act.wait_ge(prod_done, b + (act0 + 1))
                        act_high()
                    if last:
                        hi_unit(g0 + b + 2)
                    elif fixed:
                        hi_down(d0 + b + 1)
                    else:
                        act.wait_ge(rawd_in[1 - k], i * 16 + (16 * ((d0 + k + 1) // 2) + 16))
                        act.wait_ge(down_done, b + d0)
                        nc.scalar.activation(down[:, 1 - k, 0, :], rawd[1 - k][:, :], ACT.Copy).then_inc(hi_dn, 1)

                peeled = 2 if half else 1
                for b in range(2 * peeled):
                    body(b // 2, b % 2, True)
                with act.Fori(peeled, nb // 2 - 1) as i:
                    for k in range(2):
                        body(i, k, False)
                for k in range(2):
                    body(nb // 2 - 1, k, True)

            b = full(act, "cond")
            nc.scalar.activation(cond, b[:, 0:KD], ACT.Exp, scale=-1.0).then_inc(cond_exp, 1)
            for i, j in enumerate(MOD_PE):
                if i == 1:
                    hi_unit(0)
                act.wait_ge(mod_done, 2 * i + 2)
                nc.scalar.activation(accg[0:1, AC * j:AC * (j + 1)], bank[4 + i][0:1, :], ACT.Copy).then_inc(mod_row, 1)
            h_high(0, ("modc", 0, 0), modT[:, 0, 8:16], modT[:, 0, 0:8])
            hi_unit(1)
            for j in range(2):
                evac(G_QI[j], qiT[:, 2 * j:2 * j + 2, :])
            b = unit_full(act, G_KI)
            nc.scalar.activation(wiT, b[64:72, 0:256], ACT.Copy, scale=IDX_SCALE).then_inc(wi_rows, 1)
            nc.scalar.activation(kiT[0:64, :], b[0:64, 0:256], ACT.Copy)
            nc.scalar.activation(kiT[64:128, :], b[64:128, 256:512], ACT.Copy).then_inc(unit_free(G_KI), 1)
            hi_unit(G_KI + 2)
            b = full(act, "wi")
            nc.scalar.activation(wi, b[:, 0:16], ACT.Copy).then_inc(free("wi"), 1)
            for h in range(HEADS):
                b = full(act, ("idx", h))
                nc.scalar.activation(b[:, 0:384], b[:, 0:384], ACT.Relu).then_inc(idx_relu, 1)
                if h % 2 == 0:
                    evac_qkv(G_QKV[DSA][h // 2], 0, h // 2)
            for j in range(4, 6):
                evac_qkv(G_QKV[DSA][j], 0, j)

            def cg(i, g):
                b = unit_full(act, g)
                if i >= 2:
                    unit_evacuated(act, g - 2)
                nc.scalar.activation(cgb[i % 2], b[:, 0:256], ACT.Copy).then_inc(cg_ready, 1)
                hi_unit(g + 2)

            for i, g in enumerate(G_CX):
                cg(i, g)

            def gated(g):
                act.wait_ge(bg_ready, g - G_BG[0] + 1)
                i = 2 * (g - G_BG[0])
                nc.scalar.activation(yh[:, 4 + i:6 + i, :], bank[4 + g % 2][:, :].rearrange("p (k t) -> p k t", k=2), ACT.Copy
                                     ).then_inc(yb_hi, 1)
                hi_unit(g + 2)

            attention(DSA, gated)
            load_rows(0, W["ln_mix_g"][0:1, :], W["ln_mix_b"][0:1, :])
            for g in G_EO:
                other(g)
            h_high(1, ("modc", 0, 1), modT[:, 0, 24:32], modT[:, 0, 16:24])
            act.wait_ge(row_ready, 2)
            load_gates(act, 1, 0)
            load_rows(0, W["ln_ffn_g"][0:1, :], W["ln_ffn_b"][0:1, :])
            ffn(0)
            h_high(2, ("modc", 1, 0), modT[:, 1, 8:16], modT[:, 1, 0:8])
            load_gates(act, 1, 1)
            evacuated(act, ("modc", 1, 0))
            at = 0
            for g in G_Z:
                n = units[g]["n"]
                b = unit_full(act, g)
                nc.scalar.activation(zrow[:, :, at:at + n], b[:, 0:2 * n].rearrange("p (t n) -> p t n", t=TT),
                                     ACT.Copy).then_inc(unit_free(g), 1)
                if g != G_Z[-1]:
                    hi_unit(g + 2)
                at += n
            for g in G_Z[1:]:
                unit_evacuated(act, g)
            act.wait_ge(ada_acc, SUM_AFTER[0] + 1)
            for tt in range(TT):
                nc.scalar.activation(sq_scr, zrow[:, tt, 0:Q_LORA], ACT.Square, accum_out=sqs[:, tt:tt + 1]
                                     ).then_inc(lat_sq, 1)
                act.wait_ge(lat_sq, 2 * tt + 1)
                nc.scalar.activation(sq_scr[:, 0:KV_LORA], zrow[:, tt, Q_LORA:Q_LORA + KV_LORA], ACT.Square,
                                     accum_out=sqs[:, 2 + tt:3 + tt]).then_inc(lat_sq, 1)
                act.wait_ge(lat_sq, 2 * tt + 2)
            hi_unit(G_Z[-1] + 2)
            act.wait_ge(pool_zero, 3)
            evac(G_U[0], upad[:, 0:2, PAD:PAD + S])
            for i, (k0, k1) in enumerate(((0, 2), (2, 4), (4, 5))):
                evacuated(act, f"latT{i}")
                n = k1 - k0
                nc.scalar.activation(lat_h[:, k0:k1, :], lat_f[:, 512 * (i % 2):512 * (i % 2) + 256 * n]
                                     .rearrange("p (k t) -> p k t", k=n), ACT.Copy).then_inc(lat_hi, 1)
            evac(G_U[1], upad[:, 2:4, PAD:PAD + S])
            for j, g in enumerate(G_QN):
                evac(g, qT(0)[:, 2 * j:2 * j + 2, :], SCALE_MLA)
            evac(G_QR, qrow)
            for j, g in enumerate(G_KN):
                evac(g, kT(0)[:, 2 * j:2 * j + 2, :])
            for j, g in enumerate(G_VV):
                evac(g, vv(0)[:, :, UC * j:UC * (j + 1)], then=False)
            b = full(act, "krT")
            nc.scalar.activation(krT, b[:, 0:256], ACT.Copy).then_inc(free("krT"), 1)
            b = full(act, "qrT")
            nc.scalar.activation(qrT, b[:, :].rearrange("p (k t) -> p k t", k=2), ACT.Copy, scale=SCALE_MLA
                                 ).then_inc(free("qrT"), 1)
            nc.scalar.activation(table_scratch, cond[:, 0:1], ACT.Exp)

            def mla_filler(i):
                if i >= 2:
                    return hi_unit(G_OO[i - 2])
                act.wait_ge(pool_scaled, i + 1)
                nc.scalar.activation(yh[:, 2 * i:2 * i + 2, :], lat_f[:, 512 * i:512 * i + 512]
                                     .rearrange("p (k t) -> p k t", k=2), ACT.Copy).then_inc(pool_hi, 1)

            DONE[MLA] = {2: [0], 3: [1], 6: [2], 7: [3]}
            attention(MLA, mla_filler)
            load_rows(0, W["ln_mix_g"][1:2, :], W["ln_mix_b"][1:2, :])
            for g in G_OO:
                other(g)
            h_high(3, ("modc", 1, 1), modT[:, 1, 24:32], modT[:, 1, 16:24])
            act.wait_ge(row_ready, 6)
            load_rows(0, W["ln_ffn_g"][1:2, :], W["ln_ffn_b"][1:2, :])
            ffn(1)
            for tt in range(TT):
                act.wait_ge(row_ready, 7 + tt)
                ins = nc.scalar.activation(xn[:, tt, :], x[:, tt, :], ACT.Square, accum_out=ssq[:, tt:tt + 1])
            ins.then_inc(var_ready, 1)
            h_high(4, "stage", mix_gain, None)
            unit_evacuated(act, G_F)
            hi_unit(G_F + 2)
            link(nc.scalar.activation(f_t[1], f_t[0], ACT.Abs))
            link(nc.scalar.activation(f_t[1], f_t[1], ACT.Exp, scale=-1.0))
            nc.scalar.activation(f_t[1], f_t[1], ACT.Ln, bias=1.0).then_inc(f_log, 1)
            for j, g in enumerate(G_QKV[FOX]):
                evac_qkv(g, 0, j)
            attention(FOX, lambda g: evac_qkv(g, 1, g - G_QKV[MOBA][0]))
            attention(MOBA, lambda g: evac_qkv(g, 0, g - G_QKVS[0]))

            def gate_evac(g):
                evac(g, gates[:, 2 * (g - G_GATE[0]):2 * (g - G_GATE[0]) + 2, :])

            for st in range(HEADS + 2):
                if st < HEADS:
                    act.wait_ge(z_ready, st + 1)
                    b, t = bank[turns["z", st][0]], sig[st % 2]
                    link(nc.scalar.activation(t, zm[st % 2], ACT.Abs))
                    link(nc.scalar.activation(t, t, ACT.Exp, scale=-1.0))
                    nc.scalar.activation(b[:, 0:384], t, ACT.Ln, bias=1.0).then_inc(soft_log, 1)
                if 1 <= st <= HEADS:
                    evacuated(act, ("sfx", st - 1))
                    t = wT[(st - 1) % 2]
                    nc.scalar.activation(t, t, ACT.Exp).then_inc(w_ready, 1)
                if st >= 2 and st % 2 == 1:
                    out_high("stick", (st - 2) // 2)
                for g in DONE["stick"][st]:
                    gate_evac(g)
            load_rows(0, W["norm_final_2"].rearrange("(a n) -> a n", a=1))
            for g in G_GATE[10:]:
                gate_evac(g)
            for g in G_GATE[-2:]:
                unit_evacuated(act, g)
            for c in range(4):
                for n in BRANCHES:
                    for m in (BRANCHES if (c, n) == (3, BRANCHES[0]) else () if c == 3 else (n,)):
                        v = gates[:, 8 * m + 2 * c:8 * m + 2 * c + 2, :]
                        nc.scalar.activation(v, v, ACT.Sigmoid).then_inc(gate_ready, 1)
                    if (c, n) != (3, BRANCHES[-1]):
                        other(G_LIFT[c, n])
                act.wait_ge(mix_ready, c + 1)
                g = G_LIFT[c, BRANCHES[-1]]
                nc.scalar.activation(hh[:, 2 * c:2 * c + 2, :], bank[4 + g % 2][:, :].rearrange("p (k t) -> p k t", k=2),
                                     ACT.Copy).then_inc(mix_hi, 1)
            other(G_LIFT[3, BRANCHES[-1]])
            for g in G_WO:
                other(g)
            h_high(5, "stage", mlp_gain, None)
            ffn(2)

        @block.tensor
        def _(pe):
            def begin(name):
                b, k, _ = turns[name]
                if k:
                    pe.wait_ge(bank_free[b], k)
                return bank[b]

            def done(ins, name):
                ins.then_inc(bank_full[turns[name][0]], 1)

            def product(o, sh, sl, mh, ml, first, last):
                nc.tensor.matmul(o, sh, mh, start=first, stop=False)
                nc.tensor.matmul(o, sh, ml, start=False, stop=False)
                return nc.tensor.matmul(o, sl, mh, start=False, stop=last)

            def unit_begin(g):
                pe.wait_ge(hi_up, g + 1)
                if g >= 2:
                    pe.wait_ge(bank_free[4 + g % 2], g // 2)
                return bank[4 + g % 2]

            def unit_cols(g, mh, ml, blocks=(0, P), ready=None, part=None, high=None):
                o = bank[4 + g % 2] if part else unit_begin(g)
                s, n = g % 2, units[g].get("n", UC)
                nkt = units[g].get("nkt", KD)
                for i, c in enumerate(blocks):
                    if part not in (None, i):
                        continue
                    for kt in range(nkt):
                        if ready and i == 0:
                            pe.wait_ge(*(high or ready)(kt))
                        a = slice(slot(g) + kt * n + c, slot(g) + kt * n + c + P)
                        if i == 0:
                            nc.tensor.matmul(o[:, 0:S], uh[s][:, a], mh[:, kt, :], start=kt == 0, stop=False)
                            if not high:
                                nc.tensor.matmul(o[:, 0:S], uh[s][:, a], ml[:, kt, :], start=False, stop=False)
                        else:
                            mm = product(o[:, S * i:S * (i + 1)], uh[s][:, a], ul[s][:, a], mh[:, kt, :], ml[:, kt, :],
                                         kt == 0, kt == nkt - 1)
                    if i == 0:
                        for kt in range(nkt if high else 0):
                            pe.wait_ge(*ready(kt))
                            a = slice(slot(g) + kt * n + c, slot(g) + kt * n + c + P)
                            nc.tensor.matmul(o[:, 0:S], uh[s][:, a], ml[:, kt, :], start=False, stop=False)
                        pe.wait_ge(lo_up, g + 1)
                        for kt in range(nkt):
                            a = slice(slot(g) + kt * n + c, slot(g) + kt * n + c + P)
                            mm = nc.tensor.matmul(o[:, 0:S], ul[s][:, a], mh[:, kt, :], start=False, stop=kt == nkt - 1)
                if part != 0:
                    mm.then_inc(bank_full[4 + s], 1)

            def unit_rows(g, sth, stl, ready=None, order=None, part=None, high=None):
                o = bank[4 + g % 2] if part else unit_begin(g)
                s, n = g % 2, units[g].get("n", UC)
                order = order or range(units[g].get("nkt", KD))
                for tt in range(TT):
                    if part not in (None, tt):
                        continue
                    for i, kt in enumerate(order):
                        if ready and tt == 0:
                            pe.wait_ge(*(high or ready)(kt))
                        a, t = slice(slot(g) + kt * n, slot(g) + kt * n + n), slice(P * tt, P * (tt + 1))
                        c, last = o[:, n * tt:n * (tt + 1)], i == len(order) - 1
                        if tt == 0:
                            nc.tensor.matmul(c, sth[:, kt, t], uh[s][:, a], start=i == 0, stop=False)
                            if not high:
                                nc.tensor.matmul(c, stl[:, kt, t], uh[s][:, a], start=False, stop=False)
                        else:
                            mm = product(c, sth[:, kt, t], stl[:, kt, t], uh[s][:, a], ul[s][:, a], i == 0, last)
                    if tt == 0:
                        for kt in order if high else ():
                            pe.wait_ge(*ready(kt))
                            nc.tensor.matmul(c, stl[:, kt, t], uh[s][:, slot(g) + kt * n:slot(g) + kt * n + n],
                                             start=False, stop=False)
                        pe.wait_ge(lo_up, g + 1)
                        for i, kt in enumerate(order):
                            nc.tensor.matmul(c, sth[:, kt, t], ul[s][:, slot(g) + kt * n:slot(g) + kt * n + n],
                                             start=False, stop=i == len(order) - 1)
                if part != 0:
                    mm.then_inc(bank_full[4 + s], 1)

            def keep_warm(n):
                for _ in range(n):
                    nc.tensor.matmul(bank[6][:, :], ident, cst[:, 0:512], start=True, stop=True)

            def h_ready(n):
                return lambda kt: (h_lo[kt // 2 % 2], 2 * n + kt // 4 + 1)

            def h_high_ready(n):
                return lambda kt: (h_hi, 4 * n + kt // 2 + 1)

            def transpose_rows(n, src, ready=None):
                o = [begin(("ht", n, q)) for q in range(4)]
                for tt in range(TT):
                    if ready is not None:
                        pe.wait_ge(row_ready, ready + tt)
                    for kt in range(KD):
                        c = S * (kt % 2) + P * tt
                        mm = nc.tensor.transpose(o[kt // 2][:, c:c + P], src[:, tt, P * kt:P * (kt + 1)], ident)
                        if tt == 1 and kt % 2 == 1:
                            done(mm, ("ht", n, kt // 2))

            def mod_columns(layer, parts, first=True, js=range(16)):
                name = ("modc", layer, parts[0])
                o = begin(name) if first else bank[turns[name][0]]
                for i, part in enumerate(parts):
                    for j in js:
                        block = 6 * part + j // 4
                        k = P
                        if (layer, part) == (0, 0) and block in MOD_PE:
                            k = 1
                            pe.wait_ge(mod_row, MOD_PE.index(block) + 1)
                        elif j % 4 == 0:
                            summed(pe, layer, block)
                        c = block_at(layer, block).start + P * (j % 4)
                        mm = nc.tensor.matmul(o[:, 16 * i + j:16 * i + j + 1], accg[0:k, c:c + P], ones[0:k, 0:1],
                                              start=True, stop=True)
                if j == 15:
                    done(mm, name)

            def mod_half(e):
                i, s = e // 2, e % 2
                pe.wait_ge(mod_in[s], 16 * (i + 1))
                for q in range(KD // 2):
                    kt = KD // 2 * s + q
                    mm = nc.tensor.matmul(bank[4 + i][0:1, :], cond[:, kt:kt + 1], ada[2 + s][:, AC * q:AC * (q + 1)],
                                          start=kt == 0, stop=kt == KD - 1)
                mm.then_inc(mod_done, 1)

            def late_rows(f):
                for half in range(2):
                    g = FFN_G0[f] + NB_FF - 2 + half
                    unit_evacuated(pe, g)
                    nc.tensor.matmul(bank[4 + g % 2][:, :], ones, accg[:, block_at(f, MOD_BLOCKS - 2 + half)],
                                     start=True, stop=True).then_inc(gate_rows, 1)

            def mod_rows(layer, w):
                for half in range(2):
                    block = 6 * w + 4 + half
                    summed(pe, layer, block)
                    o = begin(("modr", layer, w, half))
                    mm = nc.tensor.matmul(o[:, :], ones, accg[:, block_at(layer, block)], start=True, stop=True)
                    done(mm, ("modr", layer, w, half))

            def score(a, h):
                o = begin(("score", a, h))
                p0, blk = DH * (h % 2), h // 2
                q, k = qT(ATT_SET[a])[p0:p0 + DH, blk, :], kT(ATT_SET[a])[p0:p0 + DH, blk, :]
                for tt, (c0, n) in enumerate(((0, P), (P, S))):
                    t = slice(P * tt, P * (tt + 1))
                    one = a in (DSA, MOBA)
                    mm = nc.tensor.matmul(o[:, c0:c0 + n], q[:, t], k[:, 0:n], start=True, stop=one)
                    if a == MLA:
                        r0 = D_ROPE * (h % 4)
                        mm = nc.tensor.matmul(o[:, c0:c0 + n], qrT[r0:r0 + D_ROPE, h // 4, t],
                                              krT[r0:r0 + D_ROPE, 0:n], start=False, stop=True,
                                              tile_position=(r0, 0))
                    if a == FOX:
                        mm = nc.tensor.matmul(o[:, c0:c0 + n], ident[0:8, h:h + 1].to_broadcast([8, P]),
                                              f_t[1][:, 0:n], start=False, stop=True)
                done(mm, ("score", a, h))

            def transpose_p(a, h):
                o = begin(("tr", a, h))
                for i in range(3):
                    mm = nc.tensor.transpose(o[:, P * i:P * (i + 1)], L[h % 2][:, P * i:P * (i + 1)], ident)
                done(mm, ("tr", a, h))

            def weighted(a, h, t, set_):
                o = begin(("pv", a, h // 2)) if h % 2 == 0 else bank[turns["pv", a, h // 2][0]]
                p0 = DH * (h % 2)
                v = vv(set_)
                nc.tensor.matmul(o[p0:p0 + DH, 0:S], v[:, 0, DH * h:DH * (h + 1)], t[:, 0:S], start=True, stop=False)
                nc.tensor.matmul(o[p0:p0 + DH, P:S], v[:, 1, DH * h:DH * (h + 1)], t[:, S:S + P],
                                 start=False, stop=True).then_inc(pv_done, 1)

            def attention(a, filler, v_units):
                score(a, 0)
                score(a, 1)
                for st in range(HEADS + 2):
                    if st + 2 < HEADS:
                        score(a, st + 2)
                    if 1 <= st <= HEADS:
                        transpose_p(a, st - 1)
                    if st >= 2:
                        if st == 2:
                            for g in v_units:
                                unit_evacuated(pe, g)
                        evacuated(pe, ("tr", a, st - 2))
                        weighted(a, st - 2, PT[st % 2], ATT_SET[a])
                    for g, part in FILL[a].get(st, []):
                        filler(g, part)

            def out_split(a):
                for p in (2, 3):
                    evacuated(pe, ("pv", a, p))

            def ffn(f):
                g0, d0, nb = FFN_G0[f], FFN_D0[f], FFN_NB[f]
                n = units[g0].get("n", UC)
                act0 = sum(FFN_NB[:f])

                def up(i, k, ready=None, high=None):
                    b, s = 2 * i + k, (g0 + k) % 2
                    pe.wait_ge(lo_up, b + (g0 + 1))
                    pe.wait_ge(bank_free[4 + s], i + (g0 + k) // 2)
                    for j, c in enumerate(range(0, n, P)):
                        for kt in range(KD):
                            a, o = slice(kt * n + c, kt * n + c + P), bank[4 + s][:, S * j:S * (j + 1)]
                            if ready and j == 0:
                                pe.wait_ge(*high(kt))
                                nc.tensor.matmul(o, uh[s][:, a], hh[:, kt, :], start=kt == 0, stop=False)
                                nc.tensor.matmul(o, ul[s][:, a], hh[:, kt, :], start=False, stop=False)
                            else:
                                mm = product(o, uh[s][:, a], ul[s][:, a], hh[:, kt, :], hl[:, kt, :], kt == 0, kt == KD - 1)
                        for kt in range(KD if ready and j == 0 else 0):
                            pe.wait_ge(*ready(kt))
                            mm = nc.tensor.matmul(o, uh[s][:, kt * n + c:kt * n + c + P], hl[:, kt, :],
                                                  start=False, stop=kt == KD - 1)
                    mm.then_inc(bank_full[4 + s], 1)

                def downward(i, k, first, last):
                    b = 2 * i + k
                    pe.wait_ge(lo_dn, b + (d0 + 1))
                    pe.wait_ge(act_lo, b + (act0 + 1))
                    for tt in range(TT):
                        for half in range(2):
                            if first:
                                begin(("acc", f, 2 * tt + half))
                            t, c = slice(P * tt, P * (tt + 1)), slice(512 * half, 512 * (half + 1))
                            mm = product(bank[2 * tt + half][:, :], acth[k][:, t], actl[k][:, t],
                                         down[:, k, 0, c], down[:, k, 1, c], first, last)
                            if last and (tt, half) != (1, 1):
                                done(mm, ("acc", f, 2 * tt + half))
                    mm.then_inc(down_done, 1)

                up(0, 0, ready=h_ready((1, 3, 5)[f]), high=h_high_ready((1, 3, 5)[f]))
                up(0, 1)
                downward(0, 0, True, False)
                with pe.Fori(1, nb // 2) as i:
                    up(i, 0)
                    downward(i - 1, 1, False, False)
                    up(i, 1)
                    downward(i, 0, False, False)
                if f < 2:
                    late_rows(f)
                downward(nb // 2 - 1, 1, False, True)

            pe.wait_ge(c_in, 32)
            o = begin("cond")
            mm = nc.tensor.transpose(o[:, 0:KD], stage_c, ident[0:KD, 0:KD])
            done(mm, "cond")
            evacuated(pe, "cond")
            for half in range(3):
                mod_half(half)
            pe.wait_ge(stage_in, 16 * len(STAGED))
            o = begin("stage")
            for i, n in enumerate((PCOLS, P, P, 8)):
                mm = nc.tensor.transpose(o[:, P * i:P * i + n], stage[i][0:n, :], ident[0:n, 0:n])
            done(mm, "stage")
            pe.wait_ge(x_in, 16)
            transpose_rows(0, x)
            mod_columns(0, (0,), js=[0, 1, 2, 3, 8, 9, 10, 11])
            mod_half(3)
            mod_columns(0, (0,), first=False, js=[4, 5, 6, 7, 12, 13, 14, 15])
            for g in G_QI:
                unit_cols(g, hh, hl, ready=h_ready(0), high=h_high_ready(0))
            unit_cols(G_KI, hh, hl, blocks=(64, 0))
            pe.wait_ge(wi_rows, 1)
            o = begin("wi")
            for tt in range(TT):
                mm = nc.tensor.transpose(o[:, 8 * tt:8 * tt + 8], wiT[:, P * tt:P * (tt + 1)], ident[64:72, 64:72])
            done(mm, "wi")
            for g in (G_QI[1], G_KI):
                unit_evacuated(pe, g)
            for h in range(HEADS):
                o = begin(("idx", h))
                p0 = DH * (h % 2)
                for tt, (c0, n) in enumerate(((0, P), (P, S))):
                    mm = nc.tensor.matmul(o[:, c0:c0 + n], qiT[p0:p0 + DH, h // 2, P * tt:P * (tt + 1)],
                                          kiT[p0:p0 + DH, 0:n], start=True, stop=True)
                done(mm, ("idx", h))
                if h % 2 == 0:
                    unit_cols(G_QKV[DSA][h // 2], hh, hl)
            for g in G_QKV[DSA][4:6]:
                unit_rows(g, hh, hl)
            for g in G_CX:
                unit_cols(g, hh, hl)
            for g in G_QKV[DSA][2:4]:
                unit_evacuated(pe, g)
            pe.wait_ge(const_in, 16)
            attention(DSA, lambda g, part: unit_cols(g, hh, hl, part=part), G_QKV[DSA][4:6])
            mod_rows(0, 0)

            def even_ready(kt):
                if kt >= 4:
                    g = G_BG[(kt - 4) // 2]
                    return bank_free[4 + g % 2], g // 2 + 1
                b, k, _ = turns["pv", DSA, kt]
                return bank_free[b], k + 1

            for g in G_EO:
                unit_rows(g, yh, yl, order=(4, 5, 6, 7, 0, 1, 2, 3), ready=even_ready)
            mod_columns(0, (1,), js=range(8))
            keep_warm(1)
            mod_columns(0, (1,), first=False, js=range(8, 16))
            keep_warm(3)
            transpose_rows(1, x, 1)
            ffn(0)
            pe.wait_ge(ada_acc, MOD_FFN + NB_FF)
            mod_columns(1, (0,))
            keep_warm(9)
            transpose_rows(2, x, 3)
            for g in G_Z:
                unit_rows(g, hh, hl, ready=h_ready(2), high=h_high_ready(2))
            mod_rows(1, 0)
            unit_cols(G_U[0], hh, hl)
            pe.wait_ge(lat_norm, 1)
            for i, (k0, k1) in enumerate(((0, 2), (2, 4), (4, 5))):
                o = begin(f"latT{i}")
                for kt in range(k0, k1):
                    for tt in range(TT):
                        c = S * (kt - k0) + P * tt
                        mm = nc.tensor.transpose(o[:, c:c + P], latn[:, tt, P * kt:P * (kt + 1)], ident)
                done(mm, f"latT{i}")
            unit_cols(G_U[1], hh, hl)
            pe.wait_ge(lat_lo, 3)
            for g in G_QN:
                unit_cols(g, lat_h[:, 0:3, :], lat_l[:, 0:3, :])
            unit_rows(G_QR, lat_h[:, 0:3, :], lat_l[:, 0:3, :])
            for g in G_KN:
                unit_cols(g, lat_h[:, 3:5, :], lat_l[:, 3:5, :])
            for g in G_VV:
                unit_rows(g, lat_h[:, 3:5, :], lat_l[:, 3:5, :])
            pe.wait_ge(rot_ready, 1)
            o = begin("krT")
            for tt in range(TT):
                mm = nc.tensor.transpose(o[:, P * tt:P * (tt + 1)], krot[:, tt, :], ident)
            done(mm, "krT")

            def pool_mix(g, part):
                i = part
                unit_evacuated(pe, G_VV[i])
                pe.wait_ge(pool_ready, 1)
                pe.wait_ge(pw_in, 16)
                for j in range(2):
                    mm = nc.tensor.matmul(bank[4 + G_VV[i] % 2][:, S * j:S * (j + 1)], pool_w[:, 2 * i + j, :],
                                          pooled[:, 2 * i + j, :], start=True, stop=True)
                mm.then_inc(pool_mixed, 1)

            pe.wait_ge(rot_ready, 2)
            o = begin("qrT")
            for blk in range(2):
                for tt in range(TT):
                    c = S * blk + P * tt
                    mm = nc.tensor.transpose(o[:, c:c + P], qrot[:, tt, P * blk:P * (blk + 1)], ident)
            done(mm, "qrT")
            evacuated(pe, "krT")
            keep_warm(1)
            evacuated(pe, "qrT")
            for g in G_QN[-1:] + G_KN:
                unit_evacuated(pe, g)
            attention(MLA, pool_mix, G_VV)

            def odd_ready(kt):
                if kt < 4:
                    return pool_lo, kt // 2 + 1
                b, k, _ = turns["pv", MLA, kt - 4]
                return bank_free[b], k + 1

            for g in G_OO:
                unit_rows(g, yh, yl, ready=odd_ready)
            mod_columns(1, (1,))
            keep_warm(3)
            transpose_rows(3, x, 5)
            ffn(1)
            keep_warm(16)
            transpose_rows(4, xn, 9)
            unit_cols(G_F, hh, hl, blocks=(0,), ready=h_ready(4), high=h_high_ready(4))
            for j, g in enumerate(G_QKV[FOX]):
                if j < 4:
                    unit_cols(g, hh, hl)
                else:
                    unit_rows(g, hh, hl)
            pe.wait_ge(c_ready, 1)
            o = begin("ccol")
            for tt in range(TT):
                mm = nc.tensor.transpose(o[:, 8 * tt:8 * tt + 8], f_t[1][:, P * tt:P * (tt + 1)], ident[0:8, 0:8])
            done(mm, "ccol")

            def projection(units_):
                return lambda g, part: (unit_cols if g < units_[4] else unit_rows)(g, hh, hl, part=part)

            for g in G_QKV[FOX][2:4]:
                unit_evacuated(pe, g)
            attention(FOX, projection(G_QKV[MOBA]), G_QKV[FOX][4:6])
            for g in G_QKV[MOBA][2:4]:
                unit_evacuated(pe, g)
            attention(MOBA, projection(G_QKVS), G_QKV[MOBA][4:6])
            for g in G_QKVS[2:4]:
                unit_evacuated(pe, g)
            def logits(h):
                o = begin(("z", h))
                p0, blk = DH * (h % 2), h // 2
                q, k = qT(0)[p0:p0 + DH, blk, :], kT(0)[p0:p0 + DH, blk, :]
                nc.tensor.matmul(o[:, 0:S], k[:, 0:P], q[:, 0:S], start=True, stop=True)
                mm = nc.tensor.matmul(o[:, S:S + P], k[:, P:S], q[:, P:S], start=True, stop=True)
                done(mm, ("z", h))

            logits(0)
            for st in range(HEADS + 2):
                if st + 1 < HEADS:
                    logits(st + 1)
                if 1 <= st <= HEADS:
                    h = st - 1
                    o, t = begin(("sfx", h)), sp[h % 2]
                    evacuated(pe, ("z", h))
                    nc.tensor.matmul(o[:, 0:S], C("suffix"), t[:, 0:S], start=True, stop=False)
                    nc.tensor.matmul(o[:, P:S], ones, t[:, S:S + P], start=False, stop=True)
                    mm = nc.tensor.matmul(o[:, S:S + P], C("suffix"), t[:, S:S + P], start=True, stop=True)
                    done(mm, ("sfx", h))
                if st >= 2:
                    h = st - 2
                    if h == 0:
                        for g in G_QKVS[4:6]:
                            unit_evacuated(pe, g)
                    pe.wait_ge(w_ready, h + 1)
                    weighted("stick", h, wT[h % 2], 0)
                for g, part in FILL["stick"][st]:
                    unit_cols(g, hh, hl, part=part)
            for g in G_GATE[10:]:
                unit_cols(g, hh, hl)
            out_split(MOBA)
            for c in range(4):
                for n in BRANCHES:
                    if (c, n) == (0, 0):
                        out_split("stick")
                    unit_cols(G_LIFT[c, n], o_h[n], o_l[n])

            def mixed_ready(kt):
                g = G_LIFT[kt // 2, BRANCHES[-1]]
                return bank_free[4 + g % 2], g // 2 + 1

            keep_warm(3)
            for g in G_WO:
                unit_rows(g, hh, hl, ready=mixed_ready)
            keep_warm(4)
            transpose_rows(5, xn, 11)
            ffn(2)

        @block.vector
        def _(dve):
            link = Chain(dve, dve_chain)
            V = nc.vector

            def modulation_add(s, kt, q, acc, out_):
                w, dst = ada[s][:, AC * q:AC * (q + 1)], out_ if kt == KD - 1 else acc
                if kt == 0:
                    return V.tensor_scalar(dst, w, cond[:, 0:1], None, ALU.mult)
                return V.scalar_tensor_tensor(dst, w, cond[:, kt:kt + 1], acc, ALU.mult, ALU.add)

            def modulation_half(a, acc):
                s, cols_ = a % 2, block_at(*half_at(a)[:2])
                dve.wait_ge(ada_in[s], 16 * (a // 2 + 1))
                if a:
                    dve.wait_ge(ada_acc, a)
                for q in range(KD // 2):
                    ins = modulation_add(s, KD // 2 * s + q, q, acc, accg[:, cols_])
                    if q < KD // 2 - 1:
                        link(ins)
                ins.then_inc(ada_acc, 1)

            def mod_columns(layer, parts):
                name = ("modc", layer, parts[0])
                o = full(dve, name)
                for i, part in enumerate(parts):
                    sh, sc = (modT[:, layer, 16 * part + 8 * k:16 * part + 8 * k + 8] for k in range(2))
                    link(V.scalar_tensor_tensor(sc, o[:, 16 * i + 8:16 * i + 16], 1.0, sc, ALU.add, ALU.add))
                    ins = V.tensor_tensor(sh, o[:, 16 * i:16 * i + 8], sh, ALU.add)
                    if part != parts[-1]:
                        link(ins)
                ins.then_inc(free(name), 1)
                evacuated(dve, name)

            def mod_rows(layer, w):
                dve.wait_ge(grow_in[layer], 32 if layer == 0 else 16 * (1 + w))
                for half in range(2):
                    name = ("modr", layer, w, half)
                    o, c = full(dve, name), slice(512 * half, 512 * (half + 1))
                    V.scalar_tensor_tensor(grow[:, w, c], o[:, :], 1.0, grow[:, w, c], ALU.add, ALU.add
                                           ).then_inc(free(name), 1)
                for half in range(2):
                    evacuated(dve, ("modr", layer, w, half))

            def h_columns(n, scale, shift):
                def whole(q):
                    o = full(dve, ("ht", n, q))
                    for i in range(2):
                        kt = 2 * q + i
                        dst, src = hf[:, kt, :], o[:, S * i:S * (i + 1)]
                        if shift is None:
                            ins = V.tensor_scalar(dst, src, scale[:, kt:kt + 1], None, ALU.mult)
                        else:
                            ins = V.tensor_scalar(dst, src, scale[:, kt:kt + 1], shift[:, kt:kt + 1], ALU.mult, ALU.add)
                        if i == 0:
                            link.mark(ins)
                    ins.then_inc(free(("ht", n, q)), 1)

                def low(q):
                    dve.wait_ge(h_hi, 4 * n + q + 1)
                    k = slice(2 * q, 2 * q + 2)
                    V.tensor_tensor(hl[:, k, :], hf[:, k, :], hh[:, k, :].bitcast(F32), ALU.subtract
                                    ).then_inc(h_lo[q % 2], 1)

                for q in (0, 2):
                    whole(q)
                for q in (0, 1, 2, 3) if n == 0 else (1, 3):
                    low(q)

            def chunk_statistics(tt, i, n):
                return V.bn_stats(bnst[:, tt, 6 * i:6 * i + 6], x[:, tt, n * i:n * (i + 1)])

            def aggregate(tt, chunks):
                link(V.bn_aggr(mv[:, tt, :], bnst[:, tt, 0:6 * chunks]))

            def layer_norm(n, rows):
                dve.wait_ge(ln_in, 32 * (rows + 1))
                dve.wait_ge(var_ready, n + 1)
                for tt in range(TT):
                    ins = V.scalar_tensor_tensor(x[:, tt, :], x[:, tt, :], mv[:, tt, 0:1], lnrow[:, 0, :],
                                                 ALU.subtract, ALU.mult)
                    if tt < TT - 1:
                        link.mark(ins)
                    else:
                        link(ins)
                dve.wait_ge(rstd_ready, n + 1)
                for tt in range(TT):
                    V.scalar_tensor_tensor(x[:, tt, :], x[:, tt, :], rstd[:, tt:tt + 1], lnrow[:, 1, :],
                                           ALU.mult, ALU.add).then_inc(row_ready, 1)
                dve.wait_ge(row_ready, 2 * (rows + 1))

            def rms_variance():
                for tt in range(TT):
                    ins = V.scalar_tensor_tensor(var[:, tt:tt + 1], mv[:, tt, 0:1], mv[:, tt, 0:1], mv[:, tt, 1:2],
                                                 ALU.mult, ALU.add)
                ins.then_inc(var_ready, 1)

            def rms_rows(n, scale):
                dve.wait_ge(rstd_ready, n + 1)
                for tt in range(TT):
                    V.tensor_scalar(xn[:, tt, :], x[:, tt, :], rstd[:, tt:tt + 1], scale, ALU.mult, ALU.mult
                                    ).then_inc(row_ready, 1)

            def soft(a, h):
                o = full(dve, ("score", a, h))
                marks = []
                for tt, (c0, n) in enumerate(((0, P), (P, S))):
                    def table(name):
                        return C(name)[:, P:S] if tt == 0 else C(name)
                    ps = o[:, c0:c0 + n]
                    if a == DSA:
                        ins = V.scalar_tensor_tensor(ps, distm[:, c0:c0 + n], -SLOPES[h], ps, ALU.mult, ALU.add)
                    elif a == MOBA:
                        ins = V.scalar_tensor_tensor(ps, table("dist_causal"), -SLOPES[h], ps, ALU.mult, ALU.add)
                    elif a == FOX:
                        ins = V.scalar_tensor_tensor(ps, ps, ccol[:, tt, h:h + 1], table("causal"), ALU.add, ALU.add)
                    else:
                        ins = V.tensor_tensor(ps, ps, table("chunk"), ALU.add)
                    marks.append(link.mark(ins))
                for tt, (c0, n) in enumerate(((0, P), (P, S))):
                    link.need(marks[tt])
                    ins = V.tensor_reduce(sbias[:, h, tt:tt + 1], o[:, c0:c0 + n], AX.X, ALU.max, negate=True)
                ins.then_inc(max_ready, 1)

            def normalize(a, h):
                o, t = bank[turns["score", a, h][0]], L[h % 2]
                dve.wait_ge(exp_done, att_count(a, h))
                if h >= 2:
                    full(dve, ("tr", a, h - 2))
                link(V.reciprocal(srec[:, h, :], ssum[:, h, :]))
                V.tensor_scalar(t[:, 0:P], o[:, 0:P], srec[:, h, 0:1], None, ALU.mult)
                V.tensor_scalar(t[:, P:P + S], o[:, P:P + S], srec[:, h, 1:2], None, ALU.mult
                                ).then_inc(free(("score", a, h)), 1)

            def out_low(a, p):
                dve.wait_ge(o_hi, 4 * ATT_N[a] + p + 1)
                hi, lo = ATT_OUT[a]
                V.tensor_tensor(lo[:, p, :], bank[turns["pv", a, p][0]][:, 0:S], hi[:, p, :].bitcast(F32), ALU.subtract
                                ).then_inc(free(("pv", a, p)), 1)

            def attention(a, between=None):
                for st in range(HEADS + 2):
                    if st < HEADS:
                        soft(a, st)
                    if 1 <= st <= HEADS:
                        normalize(a, st - 1)
                    if st >= 4 and st % 2 == 0:
                        out_low(a, (st - 4) // 2)
                    if between:
                        between(st)
                out_low(a, HEADS // 2 - 1)

            def mixer_residual(gs, w, before=None):
                for j, g in enumerate(gs):
                    if before:
                        before(j)
                    o = unit_full(dve, g)[:, :].rearrange("p (t n) -> p t n", t=TT)
                    c = slice(UC * j, UC * (j + 1))
                    if w is not None:
                        link(V.tensor_tensor(o, o, grow[:, w, c].unsqueeze(1).to_broadcast([P, TT, UC]), ALU.mult))
                        V.scalar_tensor_tensor(x[:, :, c], x[:, :, c], ALPHA, o, ALU.mult, ALU.add).then_inc(unit_free(g), 1)
                    else:
                        V.tensor_tensor(x[:, :, c], x[:, :, c], o, ALU.add).then_inc(unit_free(g), 1)
                    unit_evacuated(dve, g)
                    for tt in range(TT):
                        ins = chunk_statistics(tt, j, UC)
                link(ins)
                for tt in range(TT):
                    ins = V.bn_aggr(mv[:, tt, :], bnst[:, tt, :])
                if w is None:
                    link(ins)
                    rms_variance()
                else:
                    ins.then_inc(var_ready, 1)

            def ffn(f):
                g0, d0, nb = FFN_G0[f], FFN_D0[f], FFN_NB[f]
                half = units[g0]["kind"] == "pair"
                act0 = sum(FFN_NB[:f])

                mod0 = (MOD_FFN, MOD_FFN1, 0)[f]

                def body(i, k, mod):
                    b, s = 2 * i + k, (g0 + k) % 2
                    prod = bank[6][:, S * k:S * (k + 1)]

                    def tap(j, back):
                        t = (fv[k], fg[k])[j]
                        w = conv_w[f][:, bass.ds(b + ((2 - back) * 44 + 22 * j), 1)]
                        return V.scalar_tensor_tensor(t[:, back:S], bank[4 + s][:, S * j:S * (j + 1) - back], w,
                                                      t[:, back:S], ALU.mult, ALU.add)

                    def modulation(q):
                        ins = modulation_add(k, KD // 2 * k + q, q, bank[7][:, :], accg[:, bass.ds(i * AC, AC)])
                        if q < KD // 2 - 1:
                            return link.mark(ins)
                        ins.then_inc(ada_acc, 1)

                    dve.wait_ge(tap_done, b + (act0 + 1))
                    if half:
                        gate = link.mark(tap(1, 1))
                        value = link.mark(tap(0, 1))
                        link.need(gate)
                        tap(1, 2).then_inc(gate_done, 1)
                        link.need(value)
                        tap(0, 2).then_inc(bank_free[4 + s], 1)
                        if mod:
                            dve.wait_ge(ada_in[k], i * 16 + 16 * (mod0 // 2 + 1))
                            dve.wait_ge(ada_acc, b + mod0)
                            step = modulation(0)
                        dve.wait_ge(silu_done, b + (act0 + 1))
                        dve.wait_ge(bank_free[4 + s], i + ((g0 + k) // 2 + 1))
                        V.tensor_tensor(prod, fv[k], prod, ALU.mult).then_inc(prod_done, 1)
                        if mod:
                            link.need(step)
                            step = modulation(1)
                    else:
                        V.tensor_tensor(prod, bank[4 + s][:, 0:S], fv[k], ALU.mult).then_inc(bank_free[4 + s], 1)
                    dve.wait_ge(act_hi, b + (act0 + 1))
                    V.tensor_tensor(actl[k], prod, acth[k].bitcast(F32), ALU.subtract).then_inc(act_lo, 1)
                    if mod:
                        for q in (2, 3):
                            link.need(step)
                            step = modulation(q)

                per = 2 * (5, 2, 0)[f]
                peeled = 2 if f == 1 else 1
                for b in range(2 * peeled):
                    body(b // 2, b % 2, f < 2)
                with dve.Fori(peeled, nb // 2) as i:
                    link.enter(i, peeled, per)
                    for k in range(2):
                        body(i, k, f == 0)
                link.leave(nb // 2 - peeled, per)
                chunks = [(tt, i) for tt in range(TT) for i in range(2)]

                def gated(j):
                    o = bank[j]
                    if j < 3:
                        full(dve, ("acc", f, j))
                    else:
                        dve.wait_ge(down_done, d0 + nb)
                    return link.mark(V.tensor_tensor(o[:, :], o[:, :], grow[:, 1, 512 * (j % 2):512 * (j % 2 + 1)], ALU.mult))

                if f < 2:
                    dve.wait_ge(grow_in[f], 32)
                    for i in range(2):
                        dve.wait_ge(gate_rows, 2 * f + i + 1)
                        o, c = bank[4 + (g0 + nb - 2 + i) % 2], slice(512 * i, 512 * (i + 1))
                        ins = V.scalar_tensor_tensor(grow[:, 1, c], o[:, :], 1.0, grow[:, 1, c], ALU.add, ALU.add)
                    link(ins)
                mark = gated(0) if f < 2 else None
                for j, (tt, i) in enumerate(chunks):
                    c, o = slice(512 * i, 512 * (i + 1)), bank[j]
                    if f < 2:
                        after = gated(j + 1) if j < 3 else None
                        link.need(mark)
                        V.scalar_tensor_tensor(x[:, tt, c], x[:, tt, c], ALPHA, o[:, :], ALU.mult, ALU.add
                                               ).then_inc(free(("acc", f, j)), 1)
                        mark = after
                    else:
                        if j < 3:
                            full(dve, ("acc", f, j))
                        else:
                            dve.wait_ge(down_done, d0 + nb)
                        V.tensor_tensor(x[:, tt, c], x[:, tt, c], o[:, :], ALU.add).then_inc(free(("acc", f, j)), 1)
                    evacuated(dve, ("acc", f, j))
                    link(chunk_statistics(tt, i, 512))
                for tt in range(TT):
                    ins = V.bn_aggr(mv[:, tt, :], bnst[:, tt, 0:12])
                if f < 2:
                    ins.then_inc(var_ready, 1)
                else:
                    link(ins)
                    rms_variance()

            dve.wait_ge(cond_exp, 1)
            link(V.tensor_scalar(cond, cond, 1.0, None, ALU.add))
            link(V.reciprocal(cond, cond))
            V.tensor_tensor(cond, bank[turns["cond"][0]][:, 0:KD], cond, ALU.mult).then_inc(free("cond"), 1)
            evacuated(dve, "cond")
            for a in range(MOD_START - 1):
                modulation_half(a, bank[7][:, :])
            o = full(dve, "stage")
            link(V.tensor_copy(cols[:, 0:PCOLS], o[:, 0:PCOLS]))
            link(V.tensor_copy(conv_w[0][:, 0:P], o[:, P:2 * P]))
            link(V.tensor_copy(conv_w[1][:, 0:P], o[:, 2 * P:3 * P]))
            link(V.tensor_copy(conv_w[0][:, P:132], o[:, 3 * P:3 * P + 4]))
            V.tensor_copy(conv_w[1][:, P:132], o[:, 3 * P + 4:3 * P + 8]).then_inc(free("stage"), 1)
            evacuated(dve, "stage")
            modulation_half(MOD_START - 1, bank[7][:, :])
            mod_columns(0, (0,))
            h_columns(0, modT[:, 0, 8:16], modT[:, 0, 0:8])
            for a in SUM_FIRST:
                modulation_half(a, bank[7][:, :])
            evacuated(dve, "wi")
            for h in range(HEADS):
                dve.wait_ge(idx_relu, h + 1)
                r = bank[turns["idx", h][0]]
                if h:
                    evacuated(dve, ("idx", h - 1))
                for tt, (c0, n) in enumerate(((0, P), (P, S))):
                    w, d, t = wi[:, 8 * tt + h:8 * tt + h + 1], idx[:, c0:c0 + n], r[:, c0:c0 + n]
                    if h == 0:
                        ins = V.tensor_scalar(d, t, w, None, ALU.mult)
                    else:
                        ins = V.scalar_tensor_tensor(d, t, w, d, ALU.mult, ALU.add)
                ins.then_inc(free(("idx", h)), 1)
                for a in SUM_IDX.get(h, []):
                    modulation_half(a, bank[7][:, :])
            evacuated(dve, ("idx", HEADS - 1))
            dve.wait_ge(const_in, 16)
            for tt, (c0, n) in enumerate(((0, P), (P, S))):
                d = idx[:, c0:c0 + n]
                link(V.tensor_tensor(d, d, C("chunk")[:, P:S] if tt == 0 else C("chunk"), ALU.add))
                for _ in range(TOPK // 8):
                    link(V.max(top8, d))
                    link(V.match_replace(d, top8, d, REMOVED))
                m = distm[:, c0:c0 + n]
                link(V.tensor_scalar(m, d, REMOVED / 1.5, BIG, ALU.is_gt, ALU.mult))
                link(V.tensor_tensor(m, m, C("dist_chunk")[:, P:S] if tt == 0 else C("dist_chunk"), ALU.add))
            for b, g in enumerate(G_CX):
                o = unit_full(dve, g)
                dve.wait_ge(cg_ready, b + 1)
                p_ = o[:, S:2 * S]
                link(V.tensor_tensor(p_, p_, cgb[b % 2], ALU.mult))
                link(V.tensor_scalar(ybc[:, b, :], p_, ev_conv[:, 8 + b:9 + b], None, ALU.mult))
                for back in (1, 2):
                    w = ev_conv[:, 4 * (2 - back) + b:4 * (2 - back) + b + 1]
                    ins = V.scalar_tensor_tensor(ybc[:, b, back:S], p_[:, 0:S - back], w, ybc[:, b, back:S],
                                                 ALU.mult, ALU.add)
                    if back == 1:
                        link(ins)
                ins.then_inc(unit_free(g), 1)
                if b < 2:
                    modulation_half(SUM_CONV[b], bank[7][:, :])
            unit_evacuated(dve, G_CX[-1])

            def dsa_between(st):
                for g in DONE[DSA].get(st, []):
                    i = g - G_BG[0]
                    o = unit_full(dve, g)[:, :].rearrange("p (k t) -> p k t", k=2)
                    V.tensor_tensor(o, o, ybc[:, 2 * i:2 * i + 2, :], ALU.mult).then_inc(bg_ready, 1)
                    dve.wait_ge(yb_hi, i + 1)
                    V.tensor_tensor(yl[:, 4 + 2 * i:6 + 2 * i, :], o, yh[:, 4 + 2 * i:6 + 2 * i, :].bitcast(F32),
                                    ALU.subtract).then_inc(unit_free(g), 1)

            attention(DSA, dsa_between)
            mod_rows(0, 0)
            dve.wait_ge(x_in, 16)

            mixer_residual(G_EO, 0, lambda j: modulation_half(SUM_EVEN[j], bank[7][:, :]))
            layer_norm(0, 0)
            mod_columns(0, (1,))
            h_columns(1, modT[:, 0, 24:32], modT[:, 0, 16:24])
            ffn(0)
            layer_norm(1, 1)
            mod_columns(1, (0,))
            h_columns(2, modT[:, 1, 8:16], modT[:, 1, 0:8])
            for a in SUM_AFTER:
                modulation_half(a, bank[7][:, :])
            mod_rows(1, 0)
            dve.wait_ge(lat_sq, 4)
            link(V.tensor_scalar(var[:, 0:2], sqs[:, 0:2], 1.0 / Q_LORA, RMS_EPS, ALU.mult, ALU.add))
            V.tensor_scalar(var[:, 2:4], sqs[:, 2:4], 1.0 / KV_LORA, RMS_EPS, ALU.mult, ALU.add).then_inc(var_ready, 1)
            dve.wait_ge(rstd_ready, 3)
            for tt in range(TT):
                V.tensor_scalar(latn[:, tt, 0:Q_LORA], zrow[:, tt, 0:Q_LORA], rstd[:, tt:tt + 1], None, ALU.mult)
                ins = V.tensor_scalar(latn[:, tt, Q_LORA:640], zrow[:, tt, Q_LORA:640], rstd[:, 2 + tt:3 + tt], None, ALU.mult)
            ins.then_inc(lat_norm, 1)

            def lat_columns(i, k0, k1):
                o = full(dve, f"latT{i}")
                for kt in range(k0, k1):
                    gain = q_gain[:, kt:kt + 1] if kt < 3 else kv_gain[:, kt - 3:kt - 2]
                    c = S * (kt - k0)
                    ins = V.tensor_scalar(lat_f[:, 512 * (i % 2) + c:512 * (i % 2) + c + S], o[:, c:c + S], gain, None, ALU.mult)
                    if kt < k1 - 1:
                        link(ins)
                ins.then_inc(free(f"latT{i}"), 1)

            def lat_low(i, k0, k1):
                dve.wait_ge(lat_hi, i + 1)
                n = k1 - k0
                V.tensor_tensor(lat_l[:, k0:k1, :], lat_f[:, 512 * (i % 2):512 * (i % 2) + S * n]
                                .rearrange("p (k t) -> p k t", k=n), lat_h[:, k0:k1, :].bitcast(F32), ALU.subtract
                                ).then_inc(lat_lo, 1)

            lat_columns(0, 0, 2)
            lat_columns(1, 2, 4)
            lat_low(0, 0, 2)
            dve.wait_ge(lat_lo, 1)
            lat_columns(2, 4, 5)
            lat_low(1, 2, 4)
            lat_low(2, 4, 5)

            def rotate(src, dst, heads, tt):
                cos, sin = (C("rope")[:, 32 * tt + 16 * i:32 * tt + 16 * i + 16].unsqueeze(1).to_broadcast([P, heads, 16])
                            for i in range(2))
                x1, x2 = src[:, :, 0:16], src[:, :, 16:32]
                a, b = (r[:, 0:heads * 16].rearrange("p (h c) -> p h c", h=heads) for r in rt)
                link(V.tensor_tensor(a, x1, cos, ALU.mult))
                link(V.tensor_tensor(b, x2, sin, ALU.mult))
                link(V.tensor_tensor(dst[:, :, 0:16], a, b, ALU.subtract))
                link(V.tensor_tensor(a, x2, cos, ALU.mult))
                link(V.tensor_tensor(b, x1, sin, ALU.mult))
                return V.tensor_tensor(dst[:, :, 16:32], a, b, ALU.add)

            for tt in range(TT):
                ins = rotate(zrow[:, tt, 640:672].unsqueeze(1).to_broadcast([P, 4, D_ROPE]),
                             krot[:, tt, :].rearrange("p (h c) -> p h c", h=4), 4, tt)
                if tt == 0:
                    link(ins)
            ins.then_inc(rot_ready, 1)
            dve.wait_ge(rot_ready, 1)
            for g in G_U:
                unit_evacuated(dve, g)
            for gi, win in enumerate(WINDOWS):
                src, w, n = upad[:, gi, :], 1, 0
                while w < win:
                    dst = pp[n % 2]
                    link(V.tensor_tensor(dst[:, PAD:PAD + S], src[:, PAD:PAD + S], src[:, PAD - w:PAD + S - w], ALU.add))
                    src, w, n = dst, 2 * w, n + 1
                u = upad[:, gi, :]
                link(V.scalar_tensor_tensor(pooled[:, gi, PAD:S], src[:, 2 * PAD:PAD + S], 1.0 / win, u[:, 2 * PAD:PAD + S],
                                            ALU.mult, ALU.subtract))
                link(V.tensor_tensor(pooled[:, gi, 0:PAD], src[:, PAD:2 * PAD], C("rcount")[:, PAD * gi:PAD * (gi + 1)], ALU.mult))
                ins = V.tensor_tensor(pooled[:, gi, 0:PAD], pooled[:, gi, 0:PAD], u[:, PAD:2 * PAD], ALU.subtract)
                if gi < 3:
                    link(ins)
            ins.then_inc(pool_ready, 1)
            unit_evacuated(dve, G_QR)
            for tt in range(TT):
                ins = rotate(qrow[:, tt, :].rearrange("p (h c) -> p h c", h=HEADS),
                             qrot[:, tt, :].rearrange("p (h c) -> p h c", h=HEADS), HEADS, tt)
                if tt == 0:
                    link(ins)
            ins.then_inc(rot_ready, 1)
            dve.wait_ge(lat_lo, 3)

            def mla_between(st):
                i = st % 2
                if st in (2, 3):
                    dve.wait_ge(pool_mixed, i + 1)
                    o = bank[4 + G_VV[i] % 2]
                    for j in range(2):
                        ins = V.tensor_scalar(lat_f[:, 512 * i + S * j:512 * i + S * (j + 1)], o[:, S * j:S * (j + 1)],
                                              pool_scale[:, 2 * i + j:2 * i + j + 1], None, ALU.mult)
                        if j == 0:
                            link.mark(ins)
                    ins.then_inc(pool_scaled, 1)
                if st in (4, 5):
                    dve.wait_ge(pool_hi, i + 1)
                    V.tensor_tensor(yl[:, 2 * i:2 * i + 2, :], lat_f[:, 512 * i:512 * i + 512]
                                    .rearrange("p (k t) -> p k t", k=2), yh[:, 2 * i:2 * i + 2, :].bitcast(F32),
                                    ALU.subtract).then_inc(pool_lo, 1)

            attention(MLA, mla_between)
            mixer_residual(G_OO, 0)
            layer_norm(3, 2)
            mod_columns(1, (1,))
            h_columns(3, modT[:, 1, 24:32], modT[:, 1, 16:24])
            ffn(1)
            layer_norm(4, 3)
            rms_rows(5, D ** 0.5)
            h_columns(4, mix_gain, None)
            o = unit_full(dve, G_F)
            dve.wait_ge(stage_in, 16 * len(STAGED))
            V.tensor_scalar(f_t[0], o[0:8, 0:S], bfor, None, ALU.add).then_inc(unit_free(G_F), 1)
            dve.wait_ge(f_log, 1)
            link(V.scalar_tensor_tensor(f_t[2], f_t[0], 0.0, f_t[1], ALU.min, ALU.subtract))
            link(V.tensor_tensor_scan(f_t[3], ones[0:8, 0:1].to_broadcast([8, S]), f_t[2], 0.0, ALU.mult, ALU.add))
            V.tensor_scalar(f_t[1], f_t[3], -1.0, None, ALU.mult).then_inc(c_ready, 1)
            o = full(dve, "ccol")
            V.tensor_scalar(ccol, o[:, 0:16].rearrange("p (t h) -> p t h", t=TT), -1.0, None, ALU.mult).then_inc(free("ccol"), 1)
            evacuated(dve, "ccol")
            attention(FOX)
            attention(MOBA)
            for st in range(HEADS + 2):
                if st < HEADS:
                    h = st
                    o = full(dve, ("z", h))
                    if h >= 2:
                        evacuated(dve, ("sfx", h - 2))
                    V.tensor_tensor(zm[h % 2], o[:, 0:384], C("past_T"), ALU.add).then_inc(z_ready, 1)
                    dve.wait_ge(soft_log, h + 1)
                    if h >= 2:
                        full(dve, ("sfx", h - 2))
                    V.scalar_tensor_tensor(sp[h % 2], zm[h % 2], 0.0, o[:, 0:384], ALU.max, ALU.add
                                           ).then_inc(free(("z", h)), 1)
                if 1 <= st <= HEADS:
                    h = st - 1
                    o = full(dve, ("sfx", h))
                    if h >= 2:
                        dve.wait_ge(pv_done, att_count("stick", h) - 2)
                    V.tensor_tensor(wT[h % 2], zm[h % 2], o[:, 0:384], ALU.subtract).then_inc(free(("sfx", h)), 1)
                if st >= 2 and st % 2 == 1:
                    out_low("stick", (st - 2) // 2)
            for c in range(4):
                for i, n in enumerate(BRANCHES):
                    g = G_LIFT[c, n]
                    o = unit_full(dve, g)[:, :].rearrange("p (k t) -> p k t", k=2)
                    dve.wait_ge(gate_ready, 3 * c + i + 1)
                    gate = gates[:, 8 * n + 2 * c:8 * n + 2 * c + 2, :]
                    if i == 0:
                        V.tensor_tensor(mixed, o, gate, ALU.mult).then_inc(unit_free(g), 1)
                        continue
                    link(V.tensor_tensor(o, o, gate, ALU.mult))
                    if i == 1:
                        unit_evacuated(dve, G_LIFT[c, BRANCHES[0]])
                        V.tensor_tensor(mixed, mixed, o, ALU.add).then_inc(unit_free(g), 1)
                        unit_evacuated(dve, g)
                    else:
                        V.tensor_tensor(o, mixed, o, ALU.add).then_inc(mix_ready, 1)
                        dve.wait_ge(mix_hi, c + 1)
                        V.tensor_tensor(hl[:, 2 * c:2 * c + 2, :], o, hh[:, 2 * c:2 * c + 2, :].bitcast(F32), ALU.subtract
                                        ).then_inc(unit_free(g), 1)
            mixer_residual(G_WO, None)
            rms_rows(6, 1.0)
            h_columns(5, mlp_gain, None)
            ffn(2)
            dve.wait_ge(rstd_ready, 8)
            dve.wait_ge(ln_in, 32 * 4 + 16)
            for tt in range(TT):
                V.scalar_tensor_tensor(xn[:, tt, :], x[:, tt, :], rstd[:, tt:tt + 1], lnrow[:, 0, :], ALU.mult, ALU.mult
                                       ).then_inc(row_ready, 1)


_INS = ["x", "c", "ada_w", "ada_b", "ln_mix_g", "ln_mix_b", "ln_ffn_g", "ln_ffn_b", "ev_w_in", "ev_conv_w", "ev_w_out",
        "od_w_in", "pool_w", "pool_scale", "q_norm_g", "w_uq", "kv_norm_g", "w_ukv", "od_w_out", "ffn_w_up", "ffn_conv_w",
        "ffn_w_down", "norm_mix_2", "w_in_2", "b_forget_2", "w_branch_2", "w_out_2", "norm_mlp_2", "w_up_2", "w_down_2",
        "norm_final_2"]


def kernel(**inputs):
    import concourse.bacc as bacc
    from concourse.bass_utils import run_bass_kernel_spmd

    nc = bacc.Bacc("TRN2", target_bir_lowering=False, num_devices=1)
    arrays, aps = {}, {}
    for name in _INS:
        a = np.ascontiguousarray(inputs[name])
        arrays[f"in_{name}"] = a
        aps[name] = nc.dram_tensor(f"in_{name}", a.shape, mybir.dt.from_np(a.dtype), kind="ExternalInput").ap()
    arrays["shape_constants"] = shape_constants()
    consts = nc.dram_tensor("shape_constants", (P, N_CONST), F32, kind="ExternalInput").ap()
    out = nc.dram_tensor("out_0", (1, S, D), F32, kind="ExternalOutput").ap()
    build(nc, aps, consts, out)
    r = run_bass_kernel_spmd(nc, [arrays], core_ids=[0])
    return r.results[0]["out_0"]
```
